# Optimizing a Trainium2 kernel written in Bass

```python
import math
import jax, jax.numpy as jnp
from jax import lax
import numpy as np

D_MODEL = 1024
BATCH = 1
SEQ = 2048
DEPTH = 1

CHUNK = 64
ATTN_HEADS = 16
ATTN_KV_HEADS = 2
HEAD_DIM = 64
WINDOW = 128
WINDOW_CHUNKS = WINDOW // CHUNK
ROPE_THETA = 500000.0
ROT_DIM = HEAD_DIM // 4
SSD_EXPAND = 2
SSD_INNER = SSD_EXPAND * D_MODEL
SSD_HEAD_DIM = 64
SSD_HEADS = SSD_INNER // SSD_HEAD_DIM
SSD_GROUPS = 4
SSD_STATE = 128
CONV_WIDTH = 4
N_BRANCHES = 2

ATTN_Q = ATTN_HEADS * HEAD_DIM
ATTN_KV = ATTN_KV_HEADS * HEAD_DIM
SSD_BC = SSD_GROUPS * SSD_STATE
CONV_DIM = SSD_INNER + 2 * SSD_BC
IN_WIDTHS = (ATTN_Q, ATTN_KV, ATTN_KV, ATTN_Q, SSD_INNER, CONV_DIM, SSD_HEADS, N_BRANCHES * D_MODEL)
IN_DIM = sum(IN_WIDTHS)

DEEPNORM_ALPHA = (2.0 * DEPTH) ** 0.25
DEEPNORM_BETA = (8.0 * DEPTH) ** -0.25
LN_EPS = 1e-5
RMS_EPS = 1e-5
DT_MIN = 1e-3
DT_MAX = 1e-1

kernel_name = 'hybrid_swa_sink_ssd_gated_merge_layer'

def split_columns(t, widths):
    outs, start = [], 0
    for wdt in widths:
        outs.append(t[..., start:start + wdt])
        start += wdt
    return outs

def standardize(x):
    xf = x.astype(jnp.float32)
    mu = jnp.mean(xf, axis=-1, keepdims=True)
    var = jnp.mean(jnp.square(xf - mu), axis=-1, keepdims=True)
    return ((xf - mu) * lax.rsqrt(var + LN_EPS)).astype(x.dtype)

def partial_rotary(t, pos):
    half = ROT_DIM // 2
    inv_freq = jnp.power(ROPE_THETA, -jnp.arange(half, dtype=jnp.float32) / half)
    ang = pos.astype(jnp.float32)[:, None] * inv_freq[None, :]
    cos = jnp.cos(ang)[None, :, None, :]
    sin = jnp.sin(ang)[None, :, None, :]
    t_rot = t[..., :ROT_DIM].astype(jnp.float32)
    t1, t2 = t_rot[..., :half], t_rot[..., half:]
    rot = jnp.concatenate([t1 * cos - t2 * sin, t2 * cos + t1 * sin], axis=-1).astype(t.dtype)
    return jnp.concatenate([rot, t[..., ROT_DIM:]], axis=-1)

def sliding_window_sink_attention(q, k, v, sinks):
    bsz, seq = q.shape[0], q.shape[1]
    nc = seq // CHUNK
    grp = ATTN_HEADS // ATTN_KV_HEADS
    qc = q.reshape(bsz, nc, CHUNK, ATTN_KV_HEADS, grp, HEAD_DIM)
    kc = k.reshape(bsz, nc, CHUNK, ATTN_KV_HEADS, HEAD_DIM)
    vc = v.reshape(bsz, nc, CHUNK, ATTN_KV_HEADS, HEAD_DIM)

    def band(t):
        parts = []
        for w in range(WINDOW_CHUNKS - 1, -1, -1):
            parts.append(jnp.pad(t, ((0, 0), (w, 0), (0, 0), (0, 0), (0, 0)))[:, :nc])
        return jnp.concatenate(parts, axis=2)

    kb, vb = band(kc), band(vc)
    key_chunk_back = jnp.repeat(jnp.arange(WINDOW_CHUNKS - 1, -1, -1), CHUNK)
    valid = jnp.arange(nc)[:, None] >= key_chunk_back[None, :]
    scores = jnp.einsum('bcqkgd,bcskd->bckgqs', qc, kb).astype(jnp.float32) * (HEAD_DIM ** -0.5)
    scores = jnp.where(valid[None, :, None, None, None, :], scores, -jnp.inf)
    sink = jnp.broadcast_to(sinks.astype(jnp.float32).reshape(ATTN_KV_HEADS, grp)[None, None, :, :, None, None],
                            scores.shape[:-1] + (1,))
    probs = jax.nn.softmax(jnp.concatenate([scores, sink], axis=-1), axis=-1)[..., :-1]
    out = jnp.einsum('bckgqs,bcskd->bcqkgd', probs.astype(v.dtype), vb)
    return out.reshape(bsz, seq, ATTN_Q)

def causal_depthwise_conv(u, w, bias):
    out = lax.conv_general_dilated(u, w[:, None, :].astype(u.dtype), window_strides=(1,),
                                   padding=[(CONV_WIDTH - 1, 0)],
                                   dimension_numbers=('NWC', 'WIO', 'NWC'),
                                   feature_group_count=u.shape[-1])
    return out + bias

def segsum(a):
    cs = jnp.cumsum(a, axis=-1)
    diff = cs[..., :, None] - cs[..., None, :]
    t = a.shape[-1]
    return jnp.where(jnp.tril(jnp.ones((t, t), dtype=bool)), diff, -jnp.inf)

def ssd_chunked_scan(x, dt, a, bm, cm):
    bsz, seq, nh, hp = x.shape
    nc = seq // CHUNK
    hg = nh // SSD_GROUPS
    xdt = (x.astype(jnp.float32) * dt[..., None]).reshape(bsz, nc, CHUNK, SSD_GROUPS, hg, hp)
    adt = jnp.moveaxis((dt * a).reshape(bsz, nc, CHUNK, SSD_GROUPS, hg), 2, -1)
    a_cs = jnp.cumsum(adt, axis=-1)
    bc = bm.astype(jnp.float32).reshape(bsz, nc, CHUNK, SSD_GROUPS, SSD_STATE)
    cc = cm.astype(jnp.float32).reshape(bsz, nc, CHUNK, SSD_GROUPS, SSD_STATE)
    decay = jnp.exp(segsum(adt))
    cb = jnp.einsum('bclgn,bcsgn->bcgls', cc, bc)
    y_diag = jnp.einsum('bcgls,bcghls,bcsghp->bclghp', cb, decay, xdt)
    decay_to_end = jnp.exp(a_cs[..., -1:] - a_cs)
    chunk_states = jnp.einsum('bclgn,bcghl,bclghp->bcghpn', bc, decay_to_end, xdt)
    chunk_decay = jnp.exp(a_cs[..., -1])

    def step(state, inp):
        s_new, dec = inp
        return state * dec[..., None, None] + s_new, state

    init = jnp.zeros((bsz, SSD_GROUPS, hg, hp, SSD_STATE), jnp.float32)
    _, states_in = lax.scan(step, init, (jnp.moveaxis(chunk_states, 1, 0), jnp.moveaxis(chunk_decay, 1, 0)))
    states_in = jnp.moveaxis(states_in, 0, 1)
    y_off = jnp.einsum('bclgn,bcghpn,bcghl->bclghp', cc, states_in, jnp.exp(a_cs))
    return (y_diag + y_off).reshape(bsz, seq, nh, hp)

def mamba2_ssd_branch(z, xbc, dt_raw, conv_w, conv_b, dt_bias, a_log, d_skip, norm_w):
    bsz, seq = z.shape[0], z.shape[1]
    xbc = jax.nn.silu(causal_depthwise_conv(xbc, conv_w, conv_b))
    xs, bm, cm = split_columns(xbc, (SSD_INNER, SSD_BC, SSD_BC))
    xs = xs.reshape(bsz, seq, SSD_HEADS, SSD_HEAD_DIM)
    bm = bm.reshape(bsz, seq, SSD_GROUPS, SSD_STATE)
    cm = cm.reshape(bsz, seq, SSD_GROUPS, SSD_STATE)
    dt = jax.nn.softplus(dt_raw.astype(jnp.float32) + dt_bias.astype(jnp.float32))
    a = -jnp.exp(a_log.astype(jnp.float32))
    y = ssd_chunked_scan(xs, dt, a, bm, cm) + xs.astype(jnp.float32) * d_skip.astype(jnp.float32)[:, None]
    g = (y.reshape(bsz, seq, SSD_INNER) * jax.nn.silu(z.astype(jnp.float32)))
    g = g.reshape(bsz, seq, SSD_GROUPS, SSD_INNER // SSD_GROUPS)
    g = g * lax.rsqrt(jnp.mean(jnp.square(g), axis=-1, keepdims=True) + RMS_EPS)
    return (g.reshape(bsz, seq, SSD_INNER) * norm_w.astype(jnp.float32)).astype(z.dtype)

def hybrid_layer(x, c, w_ada, b_ada, w_in, b_qkv, b_merge, sinks, conv_w, conv_b, dt_bias, a_log,
                 d_skip, norm_w, w_br_attn, w_br_ssd, w_out, ln_g, ln_b):
    bsz, seq = x.shape[0], x.shape[1]
    shift, scale, gate = jnp.split(jax.nn.silu(c) @ w_ada + b_ada, 3, axis=-1)
    h = standardize(x) * (1.0 + scale[:, None, :]) + shift[:, None, :]
    q, k, v, g_attn, z, xbc, dt_raw, g_merge = split_columns(h @ w_in, IN_WIDTHS)
    bq, bk, bv = split_columns(b_qkv, (ATTN_Q, ATTN_KV, ATTN_KV))
    pos = jnp.arange(seq)
    q = partial_rotary((q + bq).reshape(bsz, seq, ATTN_HEADS, HEAD_DIM), pos)
    k = partial_rotary((k + bk).reshape(bsz, seq, ATTN_KV_HEADS, HEAD_DIM), pos)
    v = (v + bv).reshape(bsz, seq, ATTN_KV_HEADS, HEAD_DIM)
    y_attn = sliding_window_sink_attention(q, k, v, sinks) * jax.nn.silu(g_attn)
    y_ssd = mamba2_ssd_branch(z, xbc, dt_raw, conv_w, conv_b, dt_bias, a_log, d_skip, norm_w)
    g_a, g_s = jnp.split(jax.nn.sigmoid(g_merge + b_merge), N_BRANCHES, axis=-1)
    mixed = g_a * (y_attn @ w_br_attn) + g_s * (y_ssd @ w_br_ssd)
    out = mixed @ w_out
    res = DEEPNORM_ALPHA * x + gate[:, None, :] * out
    return standardize(res) * ln_g + ln_b

def setup_inputs(seed: int = 0) -> dict:
    key = jax.random.key(seed)
    ks = jax.random.split(key, 20)
    f32 = jnp.float32
    nrm = lambda k, shape, s: jax.random.normal(k, shape, f32) * s
    u = jax.random.uniform(ks[10], (DEPTH, SSD_HEADS), f32)
    dt0 = jnp.exp(u * (math.log(DT_MAX) - math.log(DT_MIN)) + math.log(DT_MIN))
    dt_bias = dt0 + jnp.log(-jnp.expm1(-dt0))
    a_log = jnp.log(jax.random.uniform(ks[11], (DEPTH, SSD_HEADS), f32, 1.0, 16.0))
    return {
        'x': nrm(ks[0], (BATCH, SEQ, D_MODEL), 1.0),
        'c': nrm(ks[1], (BATCH, D_MODEL), 1.0),
        'w_ada': nrm(ks[2], (DEPTH, D_MODEL, 3 * D_MODEL), D_MODEL ** -0.5),
        'b_ada': nrm(ks[3], (DEPTH, 3 * D_MODEL), 0.02),
        'w_in': nrm(ks[4], (DEPTH, D_MODEL, IN_DIM), D_MODEL ** -0.5),
        'b_qkv': nrm(ks[5], (DEPTH, ATTN_Q + 2 * ATTN_KV), 0.02),
        'b_merge': nrm(ks[6], (DEPTH, N_BRANCHES * D_MODEL), 0.02),
        'attn_sinks': nrm(ks[7], (DEPTH, ATTN_HEADS), 1.0),
        'conv_w': nrm(ks[8], (DEPTH, CONV_WIDTH, CONV_DIM), CONV_WIDTH ** -0.5),
        'conv_b': nrm(ks[9], (DEPTH, CONV_DIM), 0.02),
        'dt_bias': dt_bias,
        'a_log': a_log,
        'd_skip': 1.0 + nrm(ks[12], (DEPTH, SSD_HEADS), 0.1),
        'ssd_norm_w': 1.0 + nrm(ks[13], (DEPTH, SSD_INNER), 0.1),
        'w_branch_attn': nrm(ks[14], (DEPTH, ATTN_Q, D_MODEL), ATTN_Q ** -0.5 * DEEPNORM_BETA),
        'w_branch_ssd': nrm(ks[15], (DEPTH, SSD_INNER, D_MODEL), SSD_INNER ** -0.5 * DEEPNORM_BETA),
        'w_out': nrm(ks[16], (DEPTH, D_MODEL, D_MODEL), D_MODEL ** -0.5 * DEEPNORM_BETA),
        'ln_g': 1.0 + nrm(ks[17], (DEPTH, D_MODEL), 0.1),
        'ln_b': nrm(ks[18], (DEPTH, D_MODEL), 0.02),
    }

def reference(x, c, w_ada, b_ada, w_in, b_qkv, b_merge, attn_sinks, conv_w, conv_b, dt_bias, a_log,
              d_skip, ssd_norm_w, w_branch_attn, w_branch_ssd, w_out, ln_g, ln_b):
    for i in range(DEPTH):
        x = hybrid_layer(x, c, w_ada[i], b_ada[i], w_in[i], b_qkv[i], b_merge[i], attn_sinks[i], conv_w[i],
                         conv_b[i], dt_bias[i], a_log[i], d_skip[i], ssd_norm_w[i], w_branch_attn[i],
                         w_branch_ssd[i], w_out[i], ln_g[i], ln_b[i])
    return x


_drawn_inputs = setup_inputs


def setup_inputs(seed=0):
    import zlib

    import numpy as np

    out = dict(_drawn_inputs(seed))
    spreads = {}
    factors = {'b_ada': 8.0,
     'b_qkv': 37.167,
     'b_merge': 8.0,
     'attn_sinks': 34.538,
     'conv_b': 8.0,
     'd_skip': 8.0,
     'ssd_norm_w': 5.277,
     'ln_b': 2.925}
    for name, (base, spread) in spreads.items():
        noise = np.random.default_rng([zlib.crc32(name.encode()), seed]).standard_normal(out[name].shape)
        drawn = base * np.exp(spread * noise) if base else spread * noise
        out[name] = __import__('jax').numpy.asarray(drawn.astype(out[name].dtype))
    for name, factor in factors.items():
        out[name] = (out[name] * factor).astype(out[name].dtype)
    return out
```

```python
from contextlib import ExitStack

import concourse.bass as bass
from concourse import mybir

ALU = mybir.AluOpType
ACT = mybir.ActivationFunctionType
AX = mybir.AxisListType
F32 = mybir.dt.float32
F32R = mybir.dt.float32r

P = 128
D = 1024
SEQ = 2048
T = 512
NB = SEQ // T
NT = T // P
KT = D // P
CH = 64
NCH = T // CH
HD = 64
KV = 2
GROUPS = 4
HG = 8
CONVT = 24
COL_Q, COL_K, COL_V, COL_GATE = 0, 1024, 1152, 1280
COL_Z, COL_XBC, COL_DT, COL_MERGE = 2304, 4352, 7424, 7456
ALPHA = 2.0 ** 0.25
EPS = 1e-5
SCALE = HD ** -0.5

PARAMS = {}
_at = 0
for _name, _n in (("c", KT), ("b_ada", 24), ("b_q", 8), ("b_k", 1), ("b_v", 1), ("b_merge", 16),
                  ("conv_w", 4 * CONVT), ("conv_b", CONVT), ("norm_w", 16), ("dt_bias", 1), ("a_log", 1),
                  ("sink", 8), ("d_skip", 32)):
    PARAMS[_name] = (_at, _n)
    _at += _n
NPARAM = _at


def plan_units():
    units, loads = [], []

    def unit(*key):
        units.append(key)

    def branch(br):
        for m in range(KT):
            unit("br", br, m)
        loads.extend(("br", br, i) for i in range(4))

    unit("dt")
    loads.extend([("dt", 0), ("dt", 1)])
    for g in range(GROUPS):
        for t in range(6):
            unit("x", g, t)
            loads.append(("x", g, t))
        if g == 0:
            unit("dtT")
        for tt in range(NT):
            unit("z", g, tt)
        loads.extend(("z", g, i) for i in range(4))
        if g:
            branch(g - 1)
    for key in (("k",), ("v",)):
        unit(*key)
        loads.append(key)
    for kv in range(KV):
        for kind in ("q", "gate"):
            for j in range(4):
                unit(kind, kv, j)
                loads.append((kind, kv, j))
        branch(3 + kv)
    for m in range(KT):
        unit("ms", m)
        loads.append(("ms", m))
    branch(5)
    for kind in ("ma", "out"):
        for m in range(KT):
            unit(kind, m)
            loads.append((kind, m))
    return units, loads


UNITS, LOADS = plan_units()
UNIT = {key: n for n, key in enumerate(UNITS)}
LOAD = {key: n for n, key in enumerate(LOADS)}
NU, NL = len(UNITS), len(LOADS)
RAW, SPLIT, UBANKS = 3, 2, 4
assert NU % UBANKS == 0 and NL % (RAW * SPLIT) == 0
GATED = {key: n for n, key in enumerate(k for k in UNITS if k[0] in ("x", "z", "gate", "ms", "ma"))}
BRANCH = {key: n for n, key in enumerate(k for k in UNITS if k[0] == "br")}
PARTS = {key: n for n, key in enumerate(
    [("dt", 0)] + [("z", g, i) for g in range(GROUPS) for i in range(3)])}


def program(nc, x, params, w_ada, w_in, w_br_attn, w_br_ssd, w_out, ln_g, ln_b, consts, trig, kmask, out):
    ctx = ExitStack()
    with ctx:
        base = [(nc.sbuf_base + 63) // 64 * 64]

        def place(name, shape, dt=F32, at=None):
            size = 4
            for n in shape[1:]:
                size *= n
            if at is None:
                at = base[0]
                base[0] += (size + 31) // 32 * 32
            return nc.alloc_sbuf_tensor_at(name, list(shape), dt, offset=at)

        class Signal:

            def __init__(self, name, per_block, credit=1):
                self.sem = ctx.enter_context(nc.semaphore(name))
                self.per_block, self.credit, self.seen = per_block, credit, 0

            def at(self, b, n):
                assert n + self.credit >= 1, (self.sem, n)
                return self.sem, b * self.per_block + (n + self.credit)

            def done(self):
                self.seen += 1
                return self.sem, 1

        class Landed:

            def __init__(self, name, per_block, before=0):
                self.sem = ctx.enter_context(nc.semaphore(name))
                self.per_block, self.before = per_block, before

            def at(self, b, n):
                return self.sem, b * (16 * self.per_block) + 16 * (n + self.before)

            def done(self):
                return self.sem, 16

        o_h = base[0]
        h_hi = place("h_hi", [P, KT, T], F32R)
        h_lo = place("h_lo", [P, KT, T], F32R)
        acc_s = place("acc_s", [P, KT, T])
        acc_a = place("acc_a", [P, KT, T])
        w_raw = place("w_raw", [P, RAW, KT * P])
        w_hi = place("w_hi", [P, SPLIT, KT * P], F32R)
        w_lo = place("w_lo", [P, SPLIT, KT * P], F32R)
        o_xz = base[0]
        conv = place("conv", [P, 6, T])
        zbuf = place("zbuf", [P, NT, T])
        xres = place("xres", [P, NT, D], at=o_xz)
        ys_hi = place("ys_hi", [P, 4, T], F32R)
        ys_lo = place("ys_lo", [P, 4, T], F32R)
        kz = place("kz", [P, 4, CH + T])
        state = place("state", [P, GROUPS, HG * HD])
        vT = place("vT", [P, CH + T])
        th = place("th", [P, 2, T])
        ident = place("ident", [P, P])
        causal = place("causal", [P, P])
        partner = place("partner", [P, P])
        lng = place("lng", [P, D])
        lnb = place("lnb", [P, D])
        maskb = place("maskb", [P, NB, CH])
        prm = place("prm", [P, NPARAM])
        ada = place("ada", [P, 24])
        aneg = place("aneg", [P, 1])
        eps = place("eps", [P, 1])
        one = place("one", [P, 1])
        negsink = place("negsink", [P, KV, 4])
        hist = place("hist", [P, CONVT, 3])
        tok = place("tok", [P, 2, NT, 32])
        ecs = place("ecs", [P, NT, 32])
        stats = place("stats", [P, NT, 2, 6])
        mv = place("mv", [P, NT, 2])
        std = place("std", [P, NT])
        rstd = place("rstd", [P, NT])
        ss = place("ss", [P, NT])
        gstd = place("gstd", [P, NT])
        grs = place("grs", [P, NT])
        ends = place("ends", [P, 2, 2 * HG])
        top = place("top", [P, 2, 4])
        nbias = place("nbias", [P, 2, 4])
        nsink = place("nsink", [P, 2, 4])
        rsum = place("rsum", [P, 2, 4])
        esink = place("esink", [P, 2, 4])
        rden = place("rden", [P, 2, 4])
        o_r = base[0]
        K = 1024
        gmat = place("gmat", [P, HG, P], at=o_r)
        dif = place("dif", [P, HG, P], at=o_r + 4 * K)
        xdt = place("xdt", [P, 2, HG * HD], at=o_r + 8 * K)
        xd = place("xd", [P, 2, HG * HD], at=o_r + 12 * K)
        xw = place("xw", [P, HG * HD], at=o_r + 16 * K)
        bts = place("bts", [P, 2, P], at=o_r + 18 * K)
        cbm = place("cbm", [P, P], at=o_r + 19 * K)
        csb = place("csb", [P, 2, HG, P], at=o_r + 20 * K)
        u = place("u", [P, 2, T + 4], at=o_r + 28 * K)
        junk = place("junk", [P, T], at=o_r + 28 * K + 8 * (T + 4))
        o_y = o_r + 28 * K + 8 * (T + 4) + 4 * T
        ybuf = place("ybuf", [P, NT, HG * HD], at=o_y)
        silu_c = place("silu_c", [P, KT], at=o_y)
        dtmp = place("dtmp", [P, 3, T], at=o_y)
        rf = place("rf", [P, 2, T], at=o_r)
        ra = place("ra", [P, 2, T], at=o_r + 4 * K)
        rb = place("rb", [P, T], at=o_r + 8 * K)
        pbuf = place("pbuf", [P, 2, 4, P], at=o_r + 10 * K)
        ptb = place("ptb", [P, 2, 4, P], at=o_r + 14 * K)
        trg = place("trg", [P, 2, T], at=o_r + 20 * K)
        vw = place("vw", [P, NCH, 5 * HD], at=o_r + 24 * K)
        qbuf = place("qbuf", [P, NCH, 4, CH], at=o_y)
        mix_hi = place("mix_hi", [P, KT, T], F32R, at=o_r)
        mix_lo = place("mix_lo", [P, KT, T], F32R, at=o_r + 16 * K)
        og = place("og", [P, 2, T], at=o_r + 32 * K)
        hf = place("hf", [P, 2, T], at=o_r)
        ada_w = [place(f"ada_w{n}", [P, KT, T], at=a) for n, a in enumerate(
            [o_h + 16 * K * n for n in range(4)] + [o_r, o_r + 16 * K])]
        end = o_y + 8 * K
        assert end <= nc.sbuf_usable_end, (end, nc.sbuf_usable_end)

        ubank = [ctx.enter_context(nc.psum_tensor(f"ubank{n}", [P, T], F32)) for n in range(UBANKS)]
        bank_x, bank_s, bank_y, bank_o = sbank = [
            ctx.enter_context(nc.psum_tensor(f"bank_{n}", [P, T], F32)) for n in "xsyo"]
        cs_dram = nc.dram_tensor("cs_dram", [NB, 32, T], F32, kind="Internal").ap()

        def par(name, n=None, m=None):
            at, size = PARAMS[name]
            if n is None:
                return prm[:, at:at + size]
            return prm[:, at + n:at + n + (m or 1)]

        sem = lambda name: ctx.enter_context(nc.semaphore(name))
        prm_landed, const_landed = sem("prm_landed"), sem("const_landed")
        setup_dve2, waited = sem("setup_dve2"), sem("waited")
        ada_landed = [sem(f"ada_landed{n}") for n in range(6)]
        setup_dve, setup_act, setup_pool, ada_filled = (sem(n) for n in ("setup_dve", "setup_act", "setup_pool", "ada_filled"))
        unit_filled = Signal("unit_filled", NU, 2)
        part_used = Signal("part_used", len(PARTS), 2)
        ht_filled = Signal("ht_filled", KT)
        xT_filled, bc_filled, yoff_filled, ydiag_filled, new_filled, fin_filled = (
            Signal(n, 16, 2) for n in ("xT_filled", "bc_filled", "yoff_filled", "ydiag_filled", "new_filled", "fin_filled"))
        perm_filled = Signal("perm_filled", 9, 2)
        vT_filled = Signal("vT_filled", 2)
        score_filled, pT_filled, pv_filled = (Signal(n, 16, 2) for n in ("score_filled", "pT_filled", "pv_filled"))
        outT_filled = Signal("outT_filled", KT, 2)
        pe_signals = [unit_filled, part_used, ht_filled, xT_filled, bc_filled, yoff_filled, ydiag_filled,
                      new_filled, fin_filled, perm_filled, vT_filled, score_filled, pT_filled, pv_filled, outT_filled]
        hi_ready = Signal("hi_ready", NL)
        hf_ready = Signal("hf_ready", KT)
        std_ready = Signal("std_ready", 2)
        dt_parts = Signal("dt_parts", 1)
        ecs_ready = Signal("ecs_ready", 1)
        u_ready, tap_ready = Signal("u_ready", CONVT), Signal("tap_ready", CONVT)
        th_ready = Signal("th_ready", len(GATED), 2)
        decays_ready, e_ready, sq_ready = (Signal(n, 16, 2) for n in ("decays_ready", "e_ready", "sq_ready"))
        gstd_ready = Signal("gstd_ready", GROUPS)
        yhi_ready = Signal("yhi_ready", 24)
        rf_ready = Signal("rf_ready", 9)
        v_ready = Signal("v_ready", 1)
        p_ready, pt_ready = Signal("p_ready", 16, 2), Signal("pt_ready", 16, 2)
        mixhi_ready = Signal("mixhi_ready", KT)
        og_ready = Signal("og_ready", KT, 4)
        act_chain = Signal("act_chain", 4)
        act_signals = [hi_ready, hf_ready, std_ready, dt_parts, ecs_ready, u_ready, tap_ready, th_ready, decays_ready, e_ready,
                       sq_ready, gstd_ready, yhi_ready, rf_ready, v_ready, p_ready, pt_ready, mixhi_ready, og_ready,
                       act_chain]
        var_ready = Signal("var_ready", 2)
        xn_ready = Signal("xn_ready", NT)
        hhi_ready = Signal("hhi_ready", KT, 2)
        dt_ready, cs_ready, tok_ready = Signal("dt_ready", 1), Signal("cs_ready", 1), Signal("tok_ready", 1)
        conv_done = Signal("conv_done", CONVT, 2)
        hist_in, hist_out = Signal("hist_in", CONVT, 2), Signal("hist_out", CONVT, 2)
        gated = Signal("gated", len(GATED), 2)
        dif_ready, ends_ready = Signal("dif_ready", 16, 2), Signal("ends_ready", 16, 2)
        xdt_ready, xd_ready, bts_ready, cbm_ready = (
            Signal(n, 16, 2) for n in ("xdt_ready", "xd_ready", "bts_ready", "cbm_ready"))
        g_ready, y1_ready, y_ready, state_ready = (
            Signal(n, 16, 2) for n in ("g_ready", "y1_ready", "y_ready", "state_ready"))
        yn_ready = Signal("yn_ready", 16)
        ylo_ready = Signal("ylo_ready", 24)
        acc_ready = Signal("acc_ready", len(BRANCH), 1)
        rot_ready = Signal("rot_ready", 9, 2)
        vw_ready = Signal("vw_ready", 2)
        nb_ready, rec_ready, yatt_ready = (Signal(n, 16, 2) for n in ("nb_ready", "rec_ready", "yatt_ready"))
        mixlo_ready = Signal("mixlo_ready", KT)
        res_ready = Signal("res_ready", KT, 2)
        ln_ready = Signal("ln_ready", NT)
        dve_chain = Signal("dve_chain", 131)
        dve_signals = [var_ready, xn_ready, hhi_ready, dt_ready, cs_ready, tok_ready, conv_done, hist_in, hist_out, gated, dif_ready,
                       ends_ready, xdt_ready, xd_ready, bts_ready, cbm_ready, g_ready, y1_ready, y_ready,
                       state_ready, yn_ready, ylo_ready, acc_ready, rot_ready, vw_ready, nb_ready, rec_ready,
                       yatt_ready, mixlo_ready, res_ready, ln_ready, dve_chain]
        lo_ready = Signal("lo_ready", NL, 3)
        hlo_ready = Signal("hlo_ready", KT, 2)
        xw_ready, sdec_ready, y2_ready, gate_done = (
            Signal(n, 16, 2) for n in ("xw_ready", "sdec_ready", "y2_ready", "gate_done"))
        ra_ready = Signal("ra_ready", 9, 2)
        vz_ready = Signal("vz_ready", 1)
        pn_ready = Signal("pn_ready", 16, 2)
        mixf_ready = Signal("mixf_ready", KT)
        lnw_ready, out_ready = Signal("lnw_ready", NT), Signal("out_ready", NT)
        pool_signals = [lo_ready, hlo_ready, xw_ready, sdec_ready, y2_ready, gate_done, ra_ready,
                        vz_ready, pn_ready, mixf_ready, lnw_ready, out_ready]
        w_landed = [Landed(f"w_landed{n}", NL // RAW) for n in range(RAW)]
        x_landed = Landed("x_landed", 2)
        cs_stored = Landed("cs_stored", 1)
        csb_landed = [Landed(f"csb_landed{n}", 8) for n in range(2)]
        trig_landed = Landed("trig_landed", 2)
        out_stored = Landed("out_stored", NT, 1)

        def release(l):
            if l < 0:
                n = UNIT[LOADS[NL + l]] + 1 - NU
                return unit_filled, n
            key = LOADS[l]
            if key in PARTS:
                return part_used, PARTS[key] + 1
            if key[0] == "dt":
                return unit_filled, UNIT[("dt",)] + 1
            if key[0] == "z":
                return unit_filled, UNIT[("z", key[1], 3)] + 1
            if key[0] == "br":
                return unit_filled, UNIT[("br", key[1], 2 * key[2] + 1)] + 1
            return unit_filled, UNIT[key] + 1

        def drained(n):
            if n < 0:
                return og_ready, UNITS[NU + n][1] + 1 - KT
            key = UNITS[n]
            kind = key[0]
            if kind == "dt":
                return dt_parts, 1
            if kind == "dtT":
                return tok_ready, 1
            if kind == "x":
                return u_ready, key[1] * 6 + key[2] + 1
            if kind in ("z", "gate"):
                return gated, GATED[key] + 1
            if kind in ("ms", "ma"):
                return th_ready, GATED[key] + 1
            if kind == "k":
                return rf_ready, 1
            if kind == "q":
                return rf_ready, 2 + 4 * key[1] + key[2]
            if kind == "v":
                return v_ready, 1
            if kind == "br":
                return acc_ready, BRANCH[key] + 1
            return og_ready, key[1] + 1

        block = ctx.enter_context(nc.Block())
        w_in_t = w_in[0].rearrange("(k p) n -> p k n", p=P)
        w_ada_t = w_ada[0].rearrange("(k p) n -> p k n", p=P)
        w_out_t = w_out[0].rearrange("(k p) n -> p k n", p=P)
        w_bra_t = w_br_attn[0].rearrange("(k p) n -> p k n", p=P)
        w_brs_t = w_br_ssd[0].rearrange("(k p) n -> p k n", p=P)

        def raw_view(l):
            key = LOADS[l]
            kind = key[0]
            slot = w_raw[:, l % RAW, :]
            if kind == "dt":
                return slot[:, 0:512].rearrange("p (k n) -> p k n", n=P), w_in_t[:, 4 * key[1]:4 * key[1] + 4, COL_DT:COL_DT + P]
            if kind == "z":
                c = COL_Z + 512 * key[1]
                return slot.rearrange("p (k n) -> p k n", n=512), w_in_t[:, 2 * key[2]:2 * key[2] + 2, c:c + 512]
            if kind == "br":
                br, i = key[1], key[2]
                src = w_brs_t[:, 4 * br:4 * br + 4] if br < GROUPS else w_bra_t[:, 4 * (br - GROUPS):4 * (br - GROUPS) + 4]
                return slot.rearrange("p (k n) -> p k n", n=256), src[:, :, 256 * i:256 * i + 256]
            slot = slot.rearrange("p (k n) -> p k n", n=P)
            if kind == "out":
                return slot, w_out_t[:, :, P * key[1]:P * key[1] + P]
            c = {"x": lambda: COL_XBC + P * (4 * key[1] + key[2] if key[2] < 4 else 16 + 4 * (key[2] - 4) + key[1]),
                 "k": lambda: COL_K, "v": lambda: COL_V,
                 "q": lambda: COL_Q + P * (4 * key[1] + key[2]), "gate": lambda: COL_GATE + P * (4 * key[1] + key[2]),
                 "ma": lambda: COL_MERGE + P * key[1], "ms": lambda: COL_MERGE + D + P * key[1]}[kind]()
            return slot, w_in_t[:, :, c:c + P]

        def width(l):
            return 512 if LOADS[l][0] == "dt" else KT * P

        @block.sync
        def _(sp):
            sp.dma_start(prm[:, :], params).then_inc(prm_landed, 16)
            for n in range(6):
                sp.dma_start(ada_w[n][:, :, :], w_ada_t[:, :, T * n:T * n + T]).then_inc(ada_landed[n], 16)
            for n, t in enumerate((ident, causal, partner)):
                sp.dma_start(t[:, :], consts[n]).then_inc(const_landed, 16)
            sp.dma_start(maskb[:, :, :], kmask).then_inc(const_landed, 16)
            sp.dma_start(lng[:, :], ln_g.partition_broadcast(P)).then_inc(const_landed, 16)
            sp.dma_start(lnb[:, :], ln_b.partition_broadcast(P)).then_inc(const_landed, 16)
            with sp.Fori(0, NB) as b:
                rows = sp.snap(b * T)
                sp.wait_ge(*out_stored.at(b, 0))
                sp.dma_start(xres[:, :, :], x[0, bass.ds(rows, T), :].rearrange("(t p) d -> p t d", p=P)
                             ).then_inc(*x_landed.done())
                for l in range(NL):
                    if LOADS[l] == ("out", 4):
                        sp.wait_ge(*ylo_ready.at(b, 24))
                        sp.dma_start(xres[:, :, :], x[0, bass.ds(rows, T), :].rearrange("(t p) d -> p t d", p=P)
                                     ).then_inc(*x_landed.done())
                    slot, src = raw_view(l)
                    sp.wait_ge(*lo_ready.at(b, l - RAW + 1))
                    sp.dma_start(slot, src).then_inc(*w_landed[l % RAW].done())
                for tt in range(NT):
                    row = sp.snap(b * T + tt * P)
                    sp.wait_ge(*out_ready.at(b, tt + 1))
                    sp.dma_start(out[0, bass.ds(row, P), :], xres[:, tt, :]).then_inc(*out_stored.done())
            sp.wait_ge(out_stored.sem, 16 * (NT * NB + 1))

        @block.tensor
        def _(pe):
            for s in pe_signals:
                pe.sem_inc(s.sem, s.credit)
            pe.wait_ge(setup_dve, 1)
            for t in range(24):
                if t % 4 == 0:
                    pe.wait_ge(ada_landed[t // 4], 16)
                for k in range(KT):
                    mm = pe.matmul(ubank[0][:, t:t + 1], ada_w[t // 4][:, k, P * (t % 4):P * (t % 4) + P],
                                   silu_c[:, k:k + 1], start=(k == 0), stop=(k == KT - 1))
            mm.then_inc(ada_filled, 1)
            pe.wait_ge(const_landed, 96)
            pe.wait_ge(setup_pool, 3)

            with pe.Fori(0, NB) as b:
                def three(out_ap, a_hi, a_lo, m_hi, m_lo, first, last):
                    pe.matmul(out_ap, a_hi, m_hi, start=first, stop=False)
                    pe.matmul(out_ap, a_hi, m_lo, start=False, stop=False)
                    return pe.matmul(out_ap, a_lo, m_hi, start=False, stop=last)

                def bank_for(key):
                    n = UNIT[key]
                    s, at = drained(n - UBANKS)
                    pe.wait_ge(*s.at(b, at))
                    return ubank[n % UBANKS][:, :]

                def split_slot(l, n):
                    pe.wait_ge(*lo_ready.at(b, l + 1))
                    view = lambda w: w[:, l % SPLIT, :].rearrange("p (k n) -> p k n", n=n)
                    return view(w_hi), view(w_lo)

                def project(key, m_hi=h_hi, m_lo=h_lo):
                    bank = bank_for(key)
                    hi, lo = split_slot(LOAD[key], P)
                    for k in range(KT):
                        mm = three(bank, hi[:, k, :], lo[:, k, :], m_hi[:, k, :], m_lo[:, k, :], k == 0, k == KT - 1)
                    mm.then_inc(*unit_filled.done())

                def z_part(g, i):
                    banks = [bank_for(("z", g, tt)) for tt in range(NT)] if i == 0 else [
                        ubank[UNIT[("z", g, tt)] % UBANKS][:, :] for tt in range(NT)]
                    hi, lo = split_slot(LOAD[("z", g, i)], 512)
                    for j in range(2):
                        k = 2 * i + j
                        for tt in range(NT):
                            tk = slice(P * tt, P * tt + P)
                            pe.matmul(banks[tt], h_hi[:, k, tk], hi[:, j, :], start=(k == 0), stop=False)
                            pe.matmul(banks[tt], h_hi[:, k, tk], lo[:, j, :], start=False, stop=False)
                            mm = pe.matmul(banks[tt], h_lo[:, k, tk], hi[:, j, :], start=False, stop=(k == KT - 1))
                            if k == KT - 1:
                                mm.then_inc(*unit_filled.done())
                    if i < 3:
                        mm.then_inc(*part_used.done())

                def branch(br, m):
                    bank = bank_for(("br", br, m))
                    hi, lo = split_slot(LOAD[("br", br, m // 2)], 256)
                    if m == 0:
                        pe.wait_ge(*ylo_ready.at(b, 4 * br + 4))
                    cols = slice(P * (m % 2), P * (m % 2) + P)
                    for k in range(4):
                        mm = three(bank, hi[:, k, cols], lo[:, k, cols], ys_hi[:, k, :], ys_lo[:, k, :], k == 0, k == 3)
                    mm.then_inc(*unit_filled.done())

                pe.wait_ge(*xn_ready.at(b, NT))
                for k in range(KT):
                    if k >= 4:
                        pe.wait_ge(*hf_ready.at(b, k - 3))
                    for tt in range(NT):
                        mm = pe.transpose(sbank[k % 4][:, P * tt:P * tt + P], xres[:, tt, P * k:P * k + P], ident[:, :])
                    mm.then_inc(*ht_filled.done())
                pe.wait_ge(*hlo_ready.at(b, KT))
                bank = bank_for(("dt",))
                for i in range(2):
                    hi, lo = split_slot(LOAD[("dt", i)], P)
                    for k in range(4):
                        mm = three(bank, hi[:, k, :], lo[:, k, :], h_hi[:, 4 * i + k, :], h_lo[:, 4 * i + k, :],
                                   i == 0 and k == 0, i == 1 and k == 3)
                    mm.then_inc(*(unit_filled if i else part_used).done())

                def pre(s):
                    g, c = divmod(s, NT)
                    tk = slice(P * c, P * c + P)
                    if c == 0:
                        pe.wait_ge(*gated.at(b, GATED[("x", g, 5)] + 1))
                        pe.wait_ge(*ylo_ready.at(b, 4 * g))
                        pe.wait_ge(*hlo_ready.at(b, KT))
                    pe.wait_ge(*xd_ready.at(b, s))
                    for t in range(4):
                        mm = pe.transpose(bank_x[:, P * t:P * t + P], conv[:, t, tk], ident[:, :])
                    mm.then_inc(*xT_filled.done())
                    pe.wait_ge(*cbm_ready.at(b, s))
                    pe.transpose(bank_s[:, 0:P], conv[:, 4, tk], ident[:, :])
                    pe.matmul(bank_s[:, P:2 * P], conv[:, 4, tk], conv[:, 5, tk], start=True, stop=True
                              ).then_inc(*bc_filled.done())

                def finish(g):
                    pe.wait_ge(*yn_ready.at(b, 4 * g + 4))
                    for t in range(4):
                        for c in range(NT):
                            mm = pe.transpose(sbank[t][:, P * c:P * c + P], ybuf[:, c, P * t:P * t + P], ident[:, :])
                        mm.then_inc(*fin_filled.done())

                def filler(g, c, half):
                    if c < 2:
                        z_part(g, 2 * c + half)
                    elif g:
                        branch(g - 1, 4 * (c - 2) + 2 * half)
                        branch(g - 1, 4 * (c - 2) + 2 * half + 1)

                for g in range(GROUPS):
                    for t in range(6):
                        project(("x", g, t))
                        if t == 1 and g:
                            finish(g - 1)
                    if g == 0:
                        bank = bank_for(("dtT",))
                        pe.wait_ge(*cs_ready.at(b, 1))
                        for n, src in enumerate((1, 2)):
                            for c in range(NT):
                                mm = pe.matmul(bank[:, P * n + 32 * c:P * n + 32 * c + 32],
                                               dtmp[:, src, P * c:P * c + P], ident[:, 0:32], start=True, stop=True)
                        mm.then_inc(*unit_filled.done())
                    pre(4 * g)
                    for c in range(NT):
                        s = 4 * g + c
                        pe.wait_ge(*state_ready.at(b, s))
                        pe.matmul(bank_o[:, :], conv[:, 5, P * c:P * c + P], state[:, g, :], start=True, stop=True
                                  ).then_inc(*yoff_filled.done())
                        pe.wait_ge(*g_ready.at(b, s + 1))
                        pe.wait_ge(*y_ready.at(b, s))
                        for h in range(HG):
                            mm = pe.matmul(bank_y[:, HD * h:HD * h + HD], gmat[:, h, :],
                                           xdt[:, s % 2, HD * h:HD * h + HD], start=True, stop=True)
                        mm.then_inc(*ydiag_filled.done())
                        if c < NT - 1:
                            pre(s + 1)
                        filler(g, c, 0)
                        pe.wait_ge(*y1_ready.at(b, s + 1))
                        pe.wait_ge(*xw_ready.at(b, s + 1))
                        pe.matmul(bank_o[:, :], bts[:, s % 2, :], xw[:, :], start=True, stop=True
                                  ).then_inc(*new_filled.done())
                        filler(g, c, 1)

                project(("k",))
                project(("v",))
                finish(3)

                def partners(r):
                    pe.wait_ge(*rf_ready.at(b, r + 1))
                    pe.wait_ge(*rot_ready.at(b, r - 1))
                    if r == 0:
                        pe.wait_ge(*ylo_ready.at(b, 16))
                    pe.matmul((bank_y, bank_s)[r % 2][:, :], partner[:, :], rf[:, r % 2, :], start=True, stop=True
                              ).then_inc(*perm_filled.done())

                partners(0)
                pe.wait_ge(*v_ready.at(b, 1))
                for n, bk in enumerate((bank_x, bank_o)):
                    for c in range(4):
                        w0 = CH * (4 * n + c)
                        mm = pe.transpose(bk[:, P * c:P * c + P], vT[:, w0:w0 + P], ident[:, :])
                    mm.then_inc(*vT_filled.done())

                def scores(a):
                    kv, c = divmod(a, NCH)
                    pe.wait_ge(*rot_ready.at(b, 5 + 4 * kv))
                    pe.wait_ge(*p_ready.at(b, a))
                    pe.wait_ge(*vw_ready.at(b, 2))
                    for sl in range(4):
                        half, pair = divmod(sl, 2)
                        mm = pe.matmul(bank_x[:, P * sl:P * sl + P], qbuf[:, c, 2 * pair:2 * pair + 2, :],
                                       kz[:, 2 * kv + half, CH * c:CH * c + P], start=True, stop=True)
                    mm.then_inc(*score_filled.done())

                for kv in range(KV):
                    for j in range(4):
                        project(("q", kv, j))
                        if j:
                            partners(4 * kv + j)
                    for j in range(4):
                        project(("gate", kv, j))
                        if j == 0:
                            partners(4 * kv + 4)
                    scores(8 * kv)
                    for c in range(NCH):
                        a = 8 * kv + c
                        if c < NCH - 1:
                            scores(a + 1)
                        pe.wait_ge(*pn_ready.at(b, a + 1))
                        pe.wait_ge(*pt_ready.at(b, a))
                        for sl in range(4):
                            mm = pe.transpose(bank_y[:, P * sl:P * sl + P], pbuf[:, a % 2, sl, :], ident[:, :])
                        mm.then_inc(*pT_filled.done())
                        branch(3 + kv, c)
                        pe.wait_ge(*pt_ready.at(b, a + 1))
                        pe.wait_ge(*yatt_ready.at(b, a))
                        for half in range(2):
                            v0 = HD * (2 * kv + 1 - half)
                            mm = pe.matmul(bank_o[:, 0:256], vw[:, c, v0:v0 + P], ptb[:, a % 2, 2 * half:2 * half + 2, :],
                                           start=(half == 0), stop=(half == 1))
                        mm.then_inc(*pv_filled.done())

                for m in range(KT):
                    project(("ms", m))
                for m in range(KT):
                    branch(5, m)
                for m in range(KT):
                    project(("ma", m))

                def back(m):
                    pe.wait_ge(*og_ready.at(b, m + 1))
                    pe.wait_ge(*res_ready.at(b, m - 1))
                    for tt in range(NT):
                        mm = pe.transpose((bank_x, bank_y)[m % 2][:, P * tt:P * tt + P], og[:, m % 2, P * tt:P * tt + P],
                                          ident[:, :])
                    mm.then_inc(*outT_filled.done())

                pe.wait_ge(*mixlo_ready.at(b, KT))
                for m in range(KT):
                    project(("out", m), mix_hi, mix_lo)
                    if m:
                        back(m - 1)
                back(KT - 1)

        @block.scalar
        def _(act):
            for s in act_signals:
                act.sem_inc(s.sem, s.credit)
            act.wait_ge(prm_landed, 16)
            act.activation(silu_c[:, :], par("c"), ACT.Tanh, scale=0.5).then_inc(setup_act, 1)
            act.activation(aneg[:, :], par("a_log"), ACT.Exp).then_inc(setup_act, 1)
            act.wait_ge(setup_dve, 8)

            with act.Fori(0, NB) as b:
                chain = act_chain

                def split(l):
                    act.wait_ge(*w_landed[l % RAW].at(b, l // RAW + 1))
                    s, at = release(l - SPLIT)
                    act.wait_ge(*s.at(b, at))
                    n = width(l)
                    act.activation(w_hi[:, l % SPLIT, 0:n], w_raw[:, l % RAW, 0:n], ACT.Copy).then_inc(*hi_ready.done())

                def next_split(key):
                    if LOAD[key] + SPLIT < NL:
                        split(LOAD[key] + SPLIT)

                def filled(key):
                    act.wait_ge(*unit_filled.at(b, UNIT[key] + 1))
                    return ubank[UNIT[key] % UBANKS][:, :]

                def tanh(key, src, **kw):
                    n = GATED[key]
                    act.wait_ge(*gated.at(b, n - 1))
                    act.activation(th[:, n % 2, :], src, ACT.Tanh, **kw).then_inc(*th_ready.done())

                split(0)
                split(1)
                act.wait_ge(*var_ready.at(b, 1))
                act.activation(std[:, :], mv[:, :, 1], ACT.Sqrt, bias=eps[:, :]).then_inc(*std_ready.done())
                for k in range(KT):
                    act.wait_ge(*ht_filled.at(b, k + 1))
                    act.wait_ge(*hhi_ready.at(b, k - 1))
                    act.wait_ge(*hlo_ready.at(b, k - 1))
                    act.activation(hf[:, k % 2, :], sbank[k % 4][:, :], ACT.Identity, scale=ada[:, 8 + k:9 + k],
                                   bias=ada[:, k:k + 1]).then_inc(*hf_ready.done())
                next_split(("dt", 0))
                bank = filled(("dt",))
                next_split(("dt", 1))
                act.activation(dtmp[:, 0, :], bank, ACT.Abs, bias=par("dt_bias")).then_inc(*chain.done())
                act.activation(dtmp[:, 1, :], bank, ACT.Relu, bias=par("dt_bias")).then_inc(*chain.done())
                act.wait_ge(*chain.at(b, 1))
                act.activation(dtmp[:, 0, :], dtmp[:, 0, :], ACT.Exp, scale=-1.0).then_inc(*chain.done())
                act.wait_ge(*chain.at(b, 3))
                act.activation(dtmp[:, 0, :], dtmp[:, 0, :], ACT.Ln, bias=one[:, :]).then_inc(*dt_parts.done())

                def load_csb(s):
                    g, c = divmod(s, NT)
                    src = cs_dram[bass.ds(b, 1), HG * g:HG * g + HG, P * c:P * c + P].rearrange("a h t -> (a h) t")
                    act.dma_start(csb[:, s % 2, :, :], src.partition_broadcast(P)).then_inc(*csb_landed[s % 2].done())

                def decays(s):
                    act.wait_ge(*ends_ready.at(b, s + 1))
                    act.activation(ends[:, s % 2, :], ends[:, s % 2, :], ACT.Exp).then_inc(*decays_ready.done())
                    act.wait_ge(*dif_ready.at(b, s + 1))
                    act.activation(dif[:, :, :], dif[:, :, :], ACT.Exp).then_inc(*e_ready.done())
                    if s + 2 < 16:
                        load_csb(s + 2)

                def square(s):
                    g, c = divmod(s, NT)
                    act.wait_ge(*gate_done.at(b, s + 1))
                    act.wait_ge(*sq_ready.at(b, s))
                    act.activation(junk[:, :], ybuf[:, c, :], ACT.Square, accum_out=ss[:, c:c + 1]
                                   ).then_inc(*sq_ready.done())

                def finish(g):
                    act.wait_ge(*sq_ready.at(b, 4 * g + 4))
                    act.activation(gstd[:, :], ss[:, :], ACT.Sqrt, scale=0.25 / 512, bias=eps[:, :]
                                   ).then_inc(*gstd_ready.done())

                def finish_hi(g):
                    if g:
                        act.wait_ge(*unit_filled.at(b, UNIT[("br", g - 1, 7)] + 1))
                    for t in range(4):
                        act.wait_ge(*fin_filled.at(b, 4 * g + t + 1))
                        act.activation(ys_hi[:, t, :], sbank[t][:, :], ACT.Copy, scale=par("norm_w", 4 * g + t)
                                       ).then_inc(*yhi_ready.done())

                def conv_in(g, t):
                    n = 6 * g + t
                    ct = 4 * g + t if t < 4 else 16 + 4 * (t - 4) + g
                    bank = filled(("x", g, t))
                    next_split(("x", g, t))
                    act.wait_ge(*conv_done.at(b, n - 1))
                    act.wait_ge(*hist_out.at(b, n - 1))
                    act.activation(conv[:, t, :], bank, ACT.Identity, scale=par("conv_w", 4 * ct + 3),
                                   bias=par("conv_b", ct)).then_inc(*tap_ready.done())
                    act.activation(u[:, n % 2, 3:3 + T], bank, ACT.Copy).then_inc(*u_ready.done())

                def conv_tanh(g, t):
                    act.wait_ge(*conv_done.at(b, 6 * g + t + 1))
                    tanh(("x", g, t), conv[:, t, :])

                def filler(g, c, half):
                    if c < 2:
                        i = 2 * c + half
                        next_split(("z", g, i))
                        if i == 3:
                            for tt in range(NT):
                                tanh(("z", g, tt), filled(("z", g, tt)), scale=0.5)
                    elif g:
                        next_split(("br", g - 1, 2 * (c - 2) + half))

                for g in range(GROUPS):
                    for t in range(6):
                        if t == 0 and g:
                            act.wait_ge(*yoff_filled.at(b, 4 * g))
                        conv_in(g, t)
                        if t:
                            conv_tanh(g, t - 1)
                        if t == 1 and g:
                            finish_hi(g - 1)
                    conv_tanh(g, 5)
                    if g == 0:
                        act.wait_ge(*cs_ready.at(b, 1))
                        act.dma_start(cs_dram[bass.ds(b, 1), :, :].rearrange("a h t -> (a h) t"), dtmp[0:32, 2, :]
                                      ).then_inc(*cs_stored.done())
                        act.wait_ge(*tok_ready.at(b, 1))
                        act.activation(ecs[:, :, :], tok[:, 1, :, :], ACT.Exp).then_inc(*ecs_ready.done())
                        act.wait_ge(*cs_stored.at(b, 1))
                        load_csb(0)
                        load_csb(1)
                    decays(4 * g)
                    for c in range(NT):
                        s = 4 * g + c
                        if c < NT - 1:
                            decays(s + 1)
                        filler(g, c, 0)
                        filler(g, c, 1)
                        if c == 1:
                            square(4 * g)
                            square(4 * g + 1)
                        if c > 1:
                            square(s)
                    finish(g)

                def rope_in(r, key, name, n):
                    bank = filled(key)
                    next_split(key)
                    act.wait_ge(*ra_ready.at(b, r - 1))
                    act.wait_ge(*perm_filled.at(b, r - 1))
                    act.activation(rf[:, r % 2, :], bank, ACT.Identity, bias=par(name, n)).then_inc(*rf_ready.done())

                for n in range(2):
                    src = trig[n][:, bass.ds(b * T, T)]
                    act.dma_start(trg[:, n, :], src).then_inc(*trig_landed.done())
                rope_in(0, ("k",), "b_k", 0)
                act.activation(vT[:, 0:CH], vT[:, T:T + CH], ACT.Copy).then_inc(*chain.done())
                bank = filled(("v",))
                next_split(("v",))
                act.wait_ge(*chain.at(b, 4))
                act.activation(vT[:, CH:], bank, ACT.Identity, scale=0.5, bias=par("b_v")).then_inc(*v_ready.done())
                finish_hi(3)

                def attn_hi(kv, j):
                    act.wait_ge(*yatt_ready.at(b, 8 * kv + 8))
                    act.wait_ge(*unit_filled.at(b, UNIT[("br", 3 + kv, 7)] + 1))
                    act.activation(ys_hi[:, j, :], zbuf[:, j, :], ACT.Copy).then_inc(*yhi_ready.done())

                def softmax(a):
                    act.wait_ge(*nb_ready.at(b, a + 1))
                    act.wait_ge(*pT_filled.at(b, a - 1))
                    act.wait_ge(*rec_ready.at(b, a - 1))
                    for sl in range(4):
                        act.activation(pbuf[:, a % 2, sl, :], bank_x[:, P * sl:P * sl + P], ACT.Exp, scale=SCALE,
                                       bias=nbias[:, a % 2, sl:sl + 1], accum_out=rsum[:, a % 2, sl:sl + 1])
                    act.activation(esink[:, a % 2, :], nsink[:, a % 2, :], ACT.Exp).then_inc(*p_ready.done())

                for kv in range(KV):
                    for j in range(4):
                        rope_in(1 + 4 * kv + j, ("q", kv, j), "b_q", 4 * kv + j)
                    if kv:
                        for j in range(4):
                            attn_hi(kv - 1, j)
                    for j in range(4):
                        bank = filled(("gate", kv, j))
                        next_split(("gate", kv, j))
                        tanh(("gate", kv, j), bank, scale=0.5)
                    softmax(8 * kv)
                    for c in range(NCH):
                        a = 8 * kv + c
                        act.wait_ge(*pT_filled.at(b, a + 1))
                        act.wait_ge(*pv_filled.at(b, a - 1))
                        act.activation(ptb[:, a % 2, :, :], bank_y[:, :].rearrange("p (s k) -> p s k", k=P), ACT.Copy
                                       ).then_inc(*pt_ready.done())
                        if c < NCH - 1:
                            softmax(a + 1)
                        if c % 2:
                            next_split(("br", 3 + kv, c // 2))

                for j in range(4):
                    attn_hi(1, j)
                for m in range(KT):
                    bank = filled(("ms", m))
                    next_split(("ms", m))
                    tanh(("ms", m), bank, scale=0.5, bias=par("b_merge", 8 + m))
                for i in range(4):
                    next_split(("br", 5, i))

                def mix_in(m):
                    act.wait_ge(*mixf_ready.at(b, m + 1))
                    act.activation(mix_hi[:, m, :], acc_s[:, m, :], ACT.Copy).then_inc(*mixhi_ready.done())

                for m in range(KT):
                    bank = filled(("ma", m))
                    next_split(("ma", m))
                    tanh(("ma", m), bank, scale=0.5, bias=par("b_merge", m))
                    if m:
                        mix_in(m - 1)
                mix_in(KT - 1)
                for m in range(KT):
                    bank = filled(("out", m))
                    next_split(("out", m))
                    act.wait_ge(*outT_filled.at(b, m - 1))
                    act.activation(og[:, m % 2, :], bank, ACT.Copy, scale=ada[:, 16 + m:17 + m]).then_inc(*og_ready.done())
                act.wait_ge(*var_ready.at(b, 2))
                act.activation(std[:, :], mv[:, :, 1], ACT.Sqrt, bias=eps[:, :]).then_inc(*std_ready.done())

        @block.vector
        def _(dve):
            for s in dve_signals:
                dve.sem_inc(s.sem, s.credit)
            dve.memset(eps[:, :], EPS)
            dve.memset(one[:, :], 1.0)
            dve.memset(kz[:, :, :], 0.0)
            dve.wait_ge(setup_act, 2)
            dve.scalar_tensor_tensor(silu_c[:, :], silu_c[:, :], 1.0, par("c"), ALU.add, ALU.mult).then_inc(setup_dve2, 1)
            dve.wait_ge(setup_dve2, 1)
            dve.tensor_scalar(silu_c[:, :], silu_c[:, :], 0.5, None, ALU.mult).then_inc(setup_dve, 1)
            for name in ("conv_w", "conv_b", "b_merge", "norm_w", "b_v"):
                dve.tensor_scalar(par(name), par(name), 0.5, None, ALU.mult).then_inc(setup_dve, 1)
            dve.tensor_scalar(aneg[:, :], aneg[:, :], -1.0, None, ALU.mult).then_inc(setup_dve2, 1)
            dve.tensor_scalar(negsink[:, :, :].rearrange("p a b -> p (a b)"), par("sink"), -1.0, None, ALU.mult
                              ).then_inc(setup_dve2, 1)
            dve.wait_ge(ada_filled, 1)
            dve.tensor_tensor(ada[:, :], ubank[0][:, 0:24], par("b_ada"), ALU.add).then_inc(setup_dve2, 1)
            dve.wait_ge(setup_dve2, 4)
            dve.tensor_scalar(ada[:, 8:16], ada[:, 8:16], 1.0, None, ALU.add).then_inc(setup_dve, 1)
            dve.tensor_scalar(ada[:, 16:24], ada[:, 16:24], 0.5, None, ALU.mult).then_inc(setup_dve, 1)
            dve.wait_ge(setup_dve, 8)
            dve.wait_ge(const_landed, 96)
            dve.wait_ge(setup_pool, 3)

            with dve.Fori(0, NB) as b:
                chain = dve_chain
                link = [0]

                def done_link():
                    link[0] += 1
                    return chain.done()

                def after_link():
                    dve.wait_ge(*chain.at(b, link[0]))

                def norm(which, src_ready, out_signal):
                    dve.wait_ge(*src_ready)
                    for tt in range(NT):
                        for n in range(2):
                            dve.bn_stats(stats[:, tt, n, :], xres[:, tt, 512 * n:512 * n + 512]).then_inc(*done_link())
                    after_link()
                    dve.sem_inc(waited, 1)
                    for tt in range(NT):
                        last = dve.bn_aggr(mv[:, tt, :], stats[:, tt, :, :])
                    last.then_inc(*var_ready.done())
                    dve.wait_ge(*std_ready.at(b, which))
                    dve.reciprocal(rstd[:, :], std[:, :]).then_inc(*done_link())
                    after_link()
                    for tt in range(NT):
                        dve.tensor_scalar(xres[:, tt, :], xres[:, tt, :], mv[:, tt, 0:1], rstd[:, tt:tt + 1],
                                          ALU.subtract, ALU.mult).then_inc(*out_signal.done())

                norm(1, x_landed.at(b, 1), xn_ready)
                dve.wait_ge(*unit_filled.at(b, 0))
                for k in range(KT):
                    dve.wait_ge(*hf_ready.at(b, k + 1))
                    dve.tensor_copy(h_hi[:, k, :], hf[:, k % 2, :]).then_inc(*hhi_ready.done())
                dve.wait_ge(*dt_parts.at(b, 1))
                dve.tensor_tensor(dtmp[:, 1, :], dtmp[:, 0, :], dtmp[:, 1, :], ALU.add).then_inc(*dt_ready.done())
                dve.wait_ge(*dt_ready.at(b, 1))
                dve.tensor_scalar(dtmp[:, 0, :], dtmp[:, 1, :], aneg[:, :], None, ALU.mult).then_inc(*done_link())
                after_link()
                for c in range(NT):
                    last = dve.tensor_tensor_scan(dtmp[:, 2, P * c:P * c + P], one[:, :].to_broadcast([P, P]), dtmp[:, 0, P * c:P * c + P],
                                                  0.0, ALU.mult, ALU.add)
                last.then_inc(*cs_ready.done())

                def conv_taps(g, t):
                    n = 6 * g + t
                    ct = 4 * g + t if t < 4 else 16 + 4 * (t - 4) + g
                    dve.wait_ge(*conv_done.at(b, n - 1))
                    dve.wait_ge(*hist_out.at(b, n - 1))
                    dve.tensor_copy(u[:, n % 2, 0:3], hist[:, ct, :]).then_inc(*hist_in.done())
                    dve.wait_ge(*u_ready.at(b, n + 1))
                    dve.wait_ge(*hist_in.at(b, n + 1))
                    dve.tensor_copy(hist[:, ct, :], u[:, n % 2, T:T + 3]).then_inc(*hist_out.done())
                    for w in range(3):
                        ins = dve.scalar_tensor_tensor(conv[:, t, :], u[:, n % 2, w:w + T], par("conv_w", 4 * ct + w),
                                                       conv[:, t, :], ALU.mult, ALU.add)
                        if w < 2:
                            ins.then_inc(*done_link())
                            after_link()
                        else:
                            ins.then_inc(*conv_done.done())

                def gate(key, out_ap, src):
                    n = GATED[key]
                    dve.wait_ge(*th_ready.at(b, n + 1))
                    dve.scalar_tensor_tensor(out_ap, th[:, n % 2, :], 1.0, src, ALU.add, ALU.mult).then_inc(*gated.done())

                def pre_a(s):
                    g, c = divmod(s, NT)
                    heads = slice(HG * g, HG * g + HG)
                    dve.wait_ge(*csb_landed[s % 2].at(b, s // 2 + 1))
                    dve.wait_ge(*xw_ready.at(b, s - 1))
                    dve.wait_ge(*sdec_ready.at(b, s - 1))
                    dve.tensor_tensor(ends[:, s % 2, 0:HG], csb[:, s % 2, :, P - 1], tok[:, 1, c, heads], ALU.subtract)
                    dve.tensor_copy(ends[:, s % 2, HG:], csb[:, s % 2, :, P - 1]).then_inc(*ends_ready.done())
                    dve.wait_ge(*g_ready.at(b, s))
                    for h in range(HG):
                        last = dve.tensor_scalar(dif[:, h, :], csb[:, s % 2, h, :], tok[:, 1, c, HG * g + h:HG * g + h + 1],
                                                 0.0, ALU.subtract, ALU.min)
                    last.then_inc(*dif_ready.done())

                def heads3(ap):
                    return ap.rearrange("p (h d) -> p h d", d=HD)

                def over_heads(ap):
                    return ap.unsqueeze(2).to_broadcast([P, HG, HD])

                def pre_b(s):
                    g, c = divmod(s, NT)
                    heads = slice(HG * g, HG * g + HG)
                    dve.wait_ge(*xT_filled.at(b, s + 1))
                    dve.wait_ge(*ydiag_filled.at(b, s - 1))
                    dve.wait_ge(*xw_ready.at(b, s - 1))
                    dve.tensor_tensor(heads3(xdt[:, s % 2, :]), heads3(bank_x[:, :]), over_heads(tok[:, 0, c, heads]),
                                      ALU.mult).then_inc(*xdt_ready.done())
                    dve.wait_ge(*y2_ready.at(b, s - 1))
                    dve.tensor_tensor(heads3(xd[:, s % 2, :]), heads3(bank_x[:, :]), over_heads(par("d_skip", HG * g, HG)),
                                      ALU.mult).then_inc(*xd_ready.done())
                    dve.wait_ge(*bc_filled.at(b, s + 1))
                    dve.wait_ge(*new_filled.at(b, s - 1))
                    dve.tensor_copy(bts[:, s % 2, :], bank_s[:, 0:P]).then_inc(*bts_ready.done())
                    dve.wait_ge(*g_ready.at(b, s))
                    dve.tensor_tensor(cbm[:, :], bank_s[:, P:2 * P], causal[:, :], ALU.mult).then_inc(*cbm_ready.done())

                def add_branch(br, m):
                    key = ("br", br, m)
                    dve.wait_ge(*unit_filled.at(b, UNIT[key] + 1))
                    bank = ubank[UNIT[key] % UBANKS][:, :]
                    acc = (acc_s if br < GROUPS else acc_a)[:, m, :]
                    if br in (0, GROUPS):
                        dve.tensor_copy(acc, bank).then_inc(*acc_ready.done())
                    else:
                        dve.wait_ge(*acc_ready.at(b, BRANCH[("br", br - 1, m)] + 1))
                        dve.tensor_tensor(acc, acc, bank, ALU.add).then_inc(*acc_ready.done())

                def filler(g, c, half):
                    if c < 2:
                        if 2 * c + half == 3:
                            dve.wait_ge(*gate_done.at(b, 4 * g))
                            for tt in range(NT):
                                key = ("z", g, tt)
                                gate(key, zbuf[:, tt, :], ubank[UNIT[key] % UBANKS][:, :])
                    elif g:
                        add_branch(g - 1, 4 * (c - 2) + 2 * half)
                        add_branch(g - 1, 4 * (c - 2) + 2 * half + 1)

                def finish(g):
                    dve.wait_ge(*gstd_ready.at(b, g + 1))
                    dve.reciprocal(grs[:, :], gstd[:, :]).then_inc(*done_link())
                    after_link()
                    for c in range(NT):
                        dve.tensor_scalar(ybuf[:, c, :], ybuf[:, c, :], grs[:, c:c + 1], None, ALU.mult
                                          ).then_inc(*yn_ready.done())

                def finish_lo(g):
                    for t in range(4):
                        dve.wait_ge(*yhi_ready.at(b, 4 * g + t + 1))
                        dve.scalar_tensor_tensor(ys_lo[:, t, :], sbank[t][:, :], par("norm_w", 4 * g + t),
                                                 ys_hi[:, t, :].bitcast(F32), ALU.mult, ALU.subtract
                                                 ).then_inc(*ylo_ready.done())

                for g in range(GROUPS):
                    for t in range(6):
                        conv_taps(g, t)
                        if t:
                            dve.wait_ge(*conv_done.at(b, 6 * g + t))
                            gate(("x", g, t - 1), conv[:, t - 1, :], conv[:, t - 1, :])
                        if t == 1 and g:
                            finish_lo(g - 1)
                    dve.wait_ge(*conv_done.at(b, 6 * g + 6))
                    gate(("x", g, 5), conv[:, 5, :], conv[:, 5, :])
                    if g == 0:
                        dve.wait_ge(*unit_filled.at(b, UNIT[("dtT",)] + 1))
                        dve.tensor_copy(tok[:, :, :, :].rearrange("p a b c -> p (a b c)"),
                                        ubank[UNIT[("dtT",)] % UBANKS][:, 0:256]).then_inc(*tok_ready.done())
                        dve.wait_ge(*tok_ready.at(b, 1))
                        dve.wait_ge(*ecs_ready.at(b, 1))
                    pre_a(4 * g)
                    pre_b(4 * g)
                    for c in range(NT):
                        s = 4 * g + c
                        heads = slice(HG * g, HG * g + HG)
                        dve.wait_ge(*e_ready.at(b, s + 1))
                        dve.wait_ge(*cbm_ready.at(b, s + 1))
                        dve.wait_ge(*ydiag_filled.at(b, s))
                        dve.tensor_tensor(gmat[:, :, :], dif[:, :, :], cbm[:, :].unsqueeze(1).to_broadcast([P, HG, P]),
                                          ALU.mult).then_inc(*g_ready.done())
                        dve.wait_ge(*yoff_filled.at(b, s + 1))
                        if c == 0:
                            dve.wait_ge(*fin_filled.at(b, 4 * g))
                        dve.tensor_tensor(heads3(ybuf[:, c, :]), heads3(bank_o[:, :]), over_heads(ecs[:, c, heads]),
                                          ALU.mult).then_inc(*y1_ready.done())
                        if c < NT - 1:
                            pre_a(s + 1)
                            pre_b(s + 1)
                        dve.wait_ge(*ydiag_filled.at(b, s + 1))
                        dve.wait_ge(*y2_ready.at(b, s + 1))
                        dve.tensor_tensor(ybuf[:, c, :], ybuf[:, c, :], bank_y[:, :], ALU.add).then_inc(*y_ready.done())
                        filler(g, c, 0)
                        dve.wait_ge(*new_filled.at(b, s + 1))
                        dve.wait_ge(*sdec_ready.at(b, s + 1))
                        dve.tensor_tensor(state[:, g, :], state[:, g, :], bank_o[:, :], ALU.add
                                          ).then_inc(*state_ready.done())
                        filler(g, c, 1)
                    finish(g)

                def rotate_b(r):
                    dve.wait_ge(*perm_filled.at(b, r + 1))
                    dve.wait_ge(*rot_ready.at(b, r))
                    dve.tensor_tensor(rb[:, :], (bank_y, bank_s)[r % 2][:, :], trg[:, 1, :], ALU.mult).then_inc(*done_link())
                    dve.wait_ge(*ra_ready.at(b, r + 1))
                    after_link()

                dve.tensor_copy(kz[:, :, 0:CH], kz[:, :, T:T + CH]).then_inc(*done_link())
                after_link()
                finish_lo(3)
                dve.wait_ge(*trig_landed.at(b, 2))
                rotate_b(0)
                for kv in range(KV):
                    for half in range(2):
                        src = slice(HD * kv, HD * kv + HD)
                        dst = slice(HD * half, HD * half + HD)
                        ins = dve.tensor_tensor(kz[dst, 2 * kv + half, CH:], ra[src, 0, :], rb[src, :], ALU.add)
                ins.then_inc(*rot_ready.done())
                dve.wait_ge(*vz_ready.at(b, 1))
                for n, bk in enumerate((bank_x, bank_o)):
                    dve.wait_ge(*vT_filled.at(b, n + 1))
                    dst = vw[:, 4 * n:4 * n + 4, HD:5 * HD].rearrange("p c (v d) -> p c v d", d=2 * HD)[:, :, :, 0:HD]
                    dve.tensor_copy(dst, bk[:, :].rearrange("p (c v d) -> p c v d", v=2, d=HD)).then_inc(*vw_ready.done())

                def maxima(a):
                    kv, c = divmod(a, NCH)
                    dve.wait_ge(*score_filled.at(b, a + 1))
                    dve.wait_ge(*p_ready.at(b, a - 1))
                    view = bank_x[:, :].rearrange("p (s k) -> p s k", k=P)
                    if c == 0:
                        m = maskb[:, bass.ds(b, 1), :].to_broadcast([P, 4, CH])
                        dve.tensor_tensor(view[:, :, 0:CH], view[:, :, 0:CH], m, ALU.add).then_inc(*done_link())
                        after_link()
                    dve.tensor_reduce(top[:, a % 2, :], view, AX.X, ALU.max).then_inc(*done_link())
                    after_link()
                    dve.scalar_tensor_tensor(nbias[:, a % 2, :], top[:, a % 2, :], -SCALE, negsink[:, kv, :],
                                             ALU.mult, ALU.min).then_inc(*done_link())
                    after_link()
                    dve.tensor_tensor(nsink[:, a % 2, :], nbias[:, a % 2, :], negsink[:, kv, :], ALU.subtract
                                      ).then_inc(*nb_ready.done())

                def denominators(a):
                    dve.wait_ge(*p_ready.at(b, a + 1))
                    dve.wait_ge(*pn_ready.at(b, a - 1))
                    dve.tensor_tensor(rden[:, a % 2, :], rsum[:, a % 2, :], esink[:, a % 2, :], ALU.add).then_inc(*done_link())
                    after_link()
                    dve.reciprocal(rden[:, a % 2, :], rden[:, a % 2, :]).then_inc(*rec_ready.done())

                def attn_lo(kv):
                    for j in range(4):
                        n = 4 * (4 + kv) + j
                        dve.wait_ge(*yhi_ready.at(b, n + 1))
                        dve.tensor_tensor(ys_lo[:, j, :], zbuf[:, j, :], ys_hi[:, j, :].bitcast(F32), ALU.subtract
                                          ).then_inc(*ylo_ready.done())

                for kv in range(KV):
                    for j in range(4):
                        r = 1 + 4 * kv + j
                        if j == 0 and kv:
                            dve.wait_ge(*score_filled.at(b, 8 * kv))
                        rotate_b(r)
                        dve.tensor_tensor(qbuf[:, :, j, :], ra[:, r % 2, :].rearrange("p (c q) -> p c q", q=CH),
                                          rb[:, :].rearrange("p (c q) -> p c q", q=CH), ALU.add).then_inc(*rot_ready.done())
                    if kv:
                        attn_lo(kv - 1)
                        dve.wait_ge(*ylo_ready.at(b, 4 * (4 + kv)))
                    for j in range(4):
                        key = ("gate", kv, j)
                        gate(key, zbuf[:, j, :], ubank[UNIT[key] % UBANKS][:, :])
                    maxima(8 * kv)
                    denominators(8 * kv)
                    for c in range(NCH):
                        a = 8 * kv + c
                        if c < NCH - 1:
                            maxima(a + 1)
                        add_branch(3 + kv, c)
                        if c < NCH - 1:
                            denominators(a + 1)
                        dve.wait_ge(*pv_filled.at(b, a + 1))
                        part = zbuf[:, :, CH * c:CH * c + CH]
                        dve.tensor_tensor(part, bank_o[:, 0:256].rearrange("p (j q) -> p j q", q=CH), part, ALU.mult
                                          ).then_inc(*yatt_ready.done())
                attn_lo(1)
                for m in range(KT):
                    dve.wait_ge(*acc_ready.at(b, BRANCH[("br", 3, m)] + 1))
                    gate(("ms", m), acc_s[:, m, :], acc_s[:, m, :])
                for m in range(KT):
                    add_branch(5, m)

                def mix_lo_part(m):
                    dve.wait_ge(*mixhi_ready.at(b, m + 1))
                    dve.tensor_tensor(mix_lo[:, m, :], acc_s[:, m, :], mix_hi[:, m, :].bitcast(F32), ALU.subtract
                                      ).then_inc(*mixlo_ready.done())

                for m in range(KT):
                    dve.wait_ge(*acc_ready.at(b, BRANCH[("br", 5, m)] + 1))
                    gate(("ma", m), acc_a[:, m, :], acc_a[:, m, :])
                    if m:
                        mix_lo_part(m - 1)
                mix_lo_part(KT - 1)
                dve.wait_ge(*x_landed.at(b, 2))
                for m in range(KT):
                    dve.wait_ge(*outT_filled.at(b, m + 1))
                    part = xres[:, :, P * m:P * m + P]
                    dve.scalar_tensor_tensor(part, part, ALPHA, (bank_x, bank_y)[m % 2][:, :].rearrange(
                        "p (t n) -> p t n", n=P), ALU.mult, ALU.add).then_inc(*res_ready.done())
                norm(2, res_ready.at(b, KT), ln_ready)
                assert link[0] == chain.per_block, link[0]

        @block.gpsimd
        def _(pool):
            for s in pool_signals:
                pool.sem_inc(s.sem, s.credit)
            pool.sem_inc(out_stored.sem, 16)
            pool.memset(hist[:, :, :], 0.0).then_inc(setup_pool, 1)
            pool.memset(state[:, :, :], 0.0).then_inc(setup_pool, 1)
            pool.memset(vT[:, :], 0.0).then_inc(setup_pool, 1)
            pool.wait_ge(setup_pool, 3)

            with pool.Fori(0, NB) as b:
                def split(l):
                    n = width(l)
                    pool.wait_ge(*hi_ready.at(b, l + 1))
                    pool.tensor_tensor(w_lo[:, l % SPLIT, 0:n], w_raw[:, l % RAW, 0:n],
                                       w_hi[:, l % SPLIT, 0:n].bitcast(F32), ALU.subtract).then_inc(*lo_ready.done())

                def next_split(key):
                    if LOAD[key] + SPLIT < NL:
                        split(LOAD[key] + SPLIT)

                split(0)
                split(1)
                pool.wait_ge(*unit_filled.at(b, 0))
                for k in range(KT):
                    pool.wait_ge(*hhi_ready.at(b, k + 1))
                    pool.tensor_tensor(h_lo[:, k, :], hf[:, k % 2, :], h_hi[:, k, :].bitcast(F32), ALU.subtract
                                       ).then_inc(*hlo_ready.done())
                next_split(("dt", 0))
                next_split(("dt", 1))

                def heads3(ap):
                    return ap.rearrange("p (h d) -> p h d", d=HD)

                def over_heads(ap):
                    return ap.unsqueeze(2).to_broadcast([P, HG, HD])

                def weigh(s):
                    pool.wait_ge(*xdt_ready.at(b, s + 1))
                    pool.wait_ge(*decays_ready.at(b, s + 1))
                    pool.wait_ge(*new_filled.at(b, s))
                    pool.tensor_tensor(heads3(xw[:, :]), heads3(xdt[:, s % 2, :]), over_heads(ends[:, s % 2, 0:HG]),
                                       ALU.mult).then_inc(*xw_ready.done())

                def gate(s):
                    g, c = divmod(s, NT)
                    pool.wait_ge(*y_ready.at(b, s + 1))
                    pool.wait_ge(*gated.at(b, GATED[("z", g, c)] + 1))
                    pool.tensor_tensor(ybuf[:, c, :], ybuf[:, c, :], zbuf[:, c, :], ALU.mult).then_inc(*gate_done.done())

                def filler(g, c, half):
                    if c < 2:
                        next_split(("z", g, 2 * c + half))
                    elif g:
                        next_split(("br", g - 1, 2 * (c - 2) + half))

                for g in range(GROUPS):
                    for t in range(6):
                        next_split(("x", g, t))
                    for c in range(NT):
                        s = 4 * g + c
                        weigh(s)
                        pool.wait_ge(*y1_ready.at(b, s + 1))
                        pool.wait_ge(*xd_ready.at(b, s + 1))
                        pool.tensor_tensor(ybuf[:, c, :], ybuf[:, c, :], xd[:, s % 2, :], ALU.add).then_inc(*y2_ready.done())
                        pool.wait_ge(*yoff_filled.at(b, s + 1))
                        pool.wait_ge(*state_ready.at(b, s))
                        pool.tensor_tensor(heads3(state[:, g, :]), heads3(state[:, g, :]), over_heads(ends[:, s % 2, HG:]),
                                           ALU.mult).then_inc(*sdec_ready.done())
                        filler(g, c, 0)
                        filler(g, c, 1)
                        if c == 1:
                            gate(4 * g)
                            gate(4 * g + 1)
                        if c > 1:
                            gate(s)

                def rotate_a(r):
                    pool.wait_ge(*rf_ready.at(b, r + 1))
                    pool.wait_ge(*rot_ready.at(b, r - 1))
                    if r == 0:
                        pool.wait_ge(*trig_landed.at(b, 2))
                    pool.tensor_tensor(ra[:, r % 2, :], rf[:, r % 2, :], trg[:, 0, :], ALU.mult).then_inc(*ra_ready.done())

                next_split(("k",))
                rotate_a(0)
                pool.memset(vw[:, :, :], 0.0).then_inc(*vz_ready.done())
                next_split(("v",))

                def normalise(a):
                    pool.wait_ge(*rec_ready.at(b, a + 1))
                    pool.tensor_tensor(pbuf[:, a % 2, :, :], pbuf[:, a % 2, :, :],
                                       rden[:, a % 2, :].unsqueeze(2).to_broadcast([P, 4, P]), ALU.mult
                                       ).then_inc(*pn_ready.done())

                for kv in range(KV):
                    for j in range(4):
                        next_split(("q", kv, j))
                        rotate_a(1 + 4 * kv + j)
                    for j in range(4):
                        next_split(("gate", kv, j))
                    normalise(8 * kv)
                    for c in range(NCH):
                        if c < NCH - 1:
                            normalise(8 * kv + c + 1)
                        if c % 2:
                            next_split(("br", 3 + kv, c // 2))
                for m in range(KT):
                    next_split(("ms", m))
                for i in range(4):
                    next_split(("br", 5, i))
                for m in range(KT):
                    next_split(("ma", m))
                    pool.wait_ge(*gated.at(b, GATED[("ma", m)] + 1))
                    pool.tensor_tensor(acc_s[:, m, :], acc_s[:, m, :], acc_a[:, m, :], ALU.add).then_inc(*mixf_ready.done())
                for m in range(KT):
                    next_split(("out", m))
                for tt in range(NT):
                    pool.wait_ge(*ln_ready.at(b, tt + 1))
                    pool.tensor_tensor(xres[:, tt, :], xres[:, tt, :], lng[:, :], ALU.mult).then_inc(*lnw_ready.done())
                    pool.wait_ge(*lnw_ready.at(b, tt + 1))
                    pool.tensor_tensor(xres[:, tt, :], xres[:, tt, :], lnb[:, :], ALU.add).then_inc(*out_ready.done())

        for s in pe_signals + act_signals + dve_signals + pool_signals:
            assert s.seen == s.per_block, (s.sem, s.seen, s.per_block)


def kernel(x, c, w_ada, b_ada, w_in, b_qkv, b_merge, attn_sinks, conv_w, conv_b, dt_bias, a_log,
           d_skip, ssd_norm_w, w_branch_attn, w_branch_ssd, w_out, ln_g, ln_b):
    import numpy as np
    import concourse.bacc as bacc
    from concourse.bass_utils import run_bass_kernel_spmd

    f = np.float32

    def tiles(v):
        return np.ascontiguousarray(v).reshape(-1, P).T

    prm = np.zeros((P, NPARAM), f)

    def put(name, v):
        at, n = PARAMS[name]
        prm[:v.shape[0], at:at + n] = v

    c, b_ada, b_qkv, b_merge, attn_sinks, conv_w, conv_b, dt_bias, a_log, d_skip, ssd_norm_w = (
        np.asarray(v) for v in (c, b_ada, b_qkv, b_merge, attn_sinks, conv_w, conv_b, dt_bias, a_log, d_skip, ssd_norm_w))
    put("c", tiles(c[0]))
    put("b_ada", tiles(b_ada[0]))
    put("b_q", tiles(b_qkv[0, :1024]))
    put("b_k", tiles(b_qkv[0, 1024:1152]))
    put("b_v", tiles(b_qkv[0, 1152:]))
    put("b_merge", tiles(b_merge[0]))
    put("conv_w", conv_w[0].reshape(4, CONVT, P).transpose(2, 1, 0).reshape(P, CONVT * 4))
    put("conv_b", tiles(conv_b[0]))
    put("norm_w", tiles(ssd_norm_w[0]))
    put("dt_bias", dt_bias[0][:, None])
    put("a_log", a_log[0][:, None])
    sink = attn_sinks[0].reshape(KV, 2, 2, 2)
    put("sink", np.repeat(sink.transpose(2, 0, 3, 1).reshape(2, 8), 64, axis=0))
    put("d_skip", np.broadcast_to(d_skip[0], (P, 32)))

    consts = np.zeros((3, P, P), f)
    consts[0] = np.eye(P)
    consts[1] = np.triu(np.ones((P, P)))
    for p in range(P):
        if p % HD < 16:
            consts[2, p + 8 if p % HD < 8 else p - 8, p] = 1.0
    half = 8
    inv = np.power(f(500000.0), -np.arange(half, dtype=f) / f(half)).astype(f)
    ang = (np.arange(SEQ, dtype=f)[:, None] * inv[None, :]).astype(f)
    trig = np.zeros((2, P, SEQ), f)
    trig[0] = 1.0
    for p in range(P):
        d = p % HD
        if d < 16:
            trig[0, p] = np.cos(ang[:, d % 8])
            trig[1, p] = np.sin(ang[:, d % 8]) * (-1.0 if d < 8 else 1.0)
    kmask = np.zeros((P, NB, CH), f)
    kmask[:, 0, :] = -1e30

    arrays = {"x": x, "params": prm, "w_ada": w_ada, "w_in": w_in, "w_br_attn": w_branch_attn,
              "w_br_ssd": w_branch_ssd, "w_out": w_out, "ln_g": np.asarray(ln_g)[0], "ln_b": np.asarray(ln_b)[0],
              "consts": consts, "trig": trig, "kmask": kmask}
    arrays = {n: np.ascontiguousarray(a) for n, a in arrays.items()}
    nc = bacc.Bacc("TRN2", target_bir_lowering=False, num_devices=1)
    args = [nc.dram_tensor(n, a.shape, mybir.dt.from_np(a.dtype), kind="ExternalInput").ap() for n, a in arrays.items()]
    args.append(nc.dram_tensor("out", (1, SEQ, D), F32, kind="ExternalOutput").ap())
    program(nc, *args)
    r = run_bass_kernel_spmd(nc, [arrays], core_ids=[0])
    return r.results[0]["out"]
```

```python
from contextlib import ExitStack

import concourse.bass as bass
from concourse import mybir

ALU = mybir.AluOpType
ACT = mybir.ActivationFunctionType
AX = mybir.AxisListType
F32 = mybir.dt.float32
F32R = mybir.dt.float32r

P = 128
D = 1024
SEQ = 2048
T = 512
NB = SEQ // T
NT = T // P
KT = D // P
CH = 64
NCH = T // CH
HD = 64
KV = 2
GROUPS = 4
HG = 8
CONVT = 24
COL_Q, COL_K, COL_V, COL_GATE = 0, 1024, 1152, 1280
COL_Z, COL_XBC, COL_DT, COL_MERGE = 2304, 4352, 7424, 7456
ALPHA = 2.0 ** 0.25
EPS = 1e-5
SCALE = HD ** -0.5

PARAMS = {}
_at = 0
for _name, _n in (("c", KT), ("b_ada", 24), ("b_q", 8), ("b_k", 1), ("b_v", 1), ("b_merge", 16),
                  ("conv_w", 4 * CONVT), ("conv_b", CONVT), ("norm_w", 16), ("dt_bias", 1), ("a_log", 1),
                  ("sink", 8), ("d_skip", 32)):
    PARAMS[_name] = (_at, _n)
    _at += _n
NPARAM = _at


def plan_units():
    units, loads = [], []

    def unit(*key):
        units.append(key)

    def branch(br):
        for m in range(KT):
            unit("br", br, m)
        loads.extend(("br", br, i) for i in range(4))

    unit("dt")
    loads.extend([("dt", 0), ("dt", 1)])
    for g in range(GROUPS):
        for t in range(6):
            unit("x", g, t)
            loads.append(("x", g, t))
            if g == 0 and t == 2:
                unit("dtT")
        for tt in range(NT):
            unit("z", g, tt)
        loads.extend(("z", g, i) for i in range(4))
        if g:
            branch(g - 1)
    for key in (("k",), ("v",)):
        unit(*key)
        loads.append(key)
    for kv in range(KV):
        for kind in ("q", "gate"):
            for j in range(4):
                unit(kind, kv, j)
                loads.append((kind, kv, j))
        branch(3 + kv)
    for m in range(KT):
        unit("ms", m)
        loads.append(("ms", m))
    branch(5)
    for kind in ("ma", "out"):
        for m in range(KT):
            unit(kind, m)
            loads.append((kind, m))
    return units, loads


UNITS, LOADS = plan_units()


def fillers(g, c, half):
    if g == 0:
        return {(0, 0): [("z", 1)], (1, 0): [("z", 2)], (2, 0): [("z", 3)]}.get((c, half), [])
    return {(0, 0): [("z", 1)], (0, 1): [("z", 2)], (1, 0): [("z", 3)], (1, 1): [("br", 0), ("br", 1)],
            (2, 0): [("br", 2), ("br", 3)], (2, 1): [("br", 4), ("br", 5)], (3, 0): [("br", 6)], (3, 1): [("br", 7)]}[c, half]


def z_step(g):
    return 1 if g else 2


UNIT = {key: n for n, key in enumerate(UNITS)}
LOAD = {key: n for n, key in enumerate(LOADS)}
NU, NL = len(UNITS), len(LOADS)
RAW, SPLIT, UBANKS = 3, 2, 4
assert NU % UBANKS == 0 and NL % (RAW * SPLIT) == 0
GATED = {key: n for n, key in enumerate(k for k in UNITS if k[0] in ("x", "z", "gate", "ms", "ma"))}
BRANCH = {key: n for n, key in enumerate(k for k in UNITS if k[0] == "br")}
PARTS = {key: n for n, key in enumerate(
    [("dt", 0)] + [("z", g, i) for g in range(GROUPS) for i in range(3)])}


def program(nc, x, params, w_ada, w_in, w_br_attn, w_br_ssd, w_out, ln_g, ln_b, consts, trig, kmask, out):
    ctx = ExitStack()
    with ctx:
        base = [(nc.sbuf_base + 63) // 64 * 64]

        def place(name, shape, dt=F32, at=None):
            size = 4
            for n in shape[1:]:
                size *= n
            if at is None:
                at = base[0]
                base[0] += (size + 31) // 32 * 32
            return nc.alloc_sbuf_tensor_at(name, list(shape), dt, offset=at)

        class Signal:

            def __init__(self, name, per_block, credit=1):
                self.sem = ctx.enter_context(nc.semaphore(name))
                self.per_block, self.credit, self.seen = per_block, credit, 0

            def at(self, b, n, ahead=0):
                n += ahead * self.per_block
                assert n + self.credit >= 1, (self.sem, n)
                return self.sem, b * self.per_block + (n + self.credit)

            def done(self):
                self.seen += 1
                return self.sem, 1

        class Landed:

            def __init__(self, name, per_block, before=0):
                self.sem = ctx.enter_context(nc.semaphore(name))
                self.per_block, self.before = per_block, before

            def at(self, b, n, ahead=0):
                return self.sem, b * (16 * self.per_block) + 16 * (n + ahead * self.per_block + self.before)

            def done(self):
                return self.sem, 16

        o_h = base[0]
        h_hi = place("h_hi", [P, KT, T], F32R)
        h_lo = place("h_lo", [P, KT, T], F32R)
        acc_s = place("acc_s", [P, KT, T])
        o_acc_a = base[0]
        acc_a = place("acc_a", [P, KT, T])
        res = place("res", [P, NT, D], at=o_acc_a)
        w_raw = place("w_raw", [P, RAW, KT * P])
        w_hi = place("w_hi", [P, SPLIT, KT * P], F32R)
        w_lo = place("w_lo", [P, SPLIT, KT * P], F32R)
        o_xz = base[0]
        conv = place("conv", [P, 6, T])
        zbuf = place("zbuf", [P, NT, T])
        xn = place("xn", [P, NT, D], at=o_xz)
        o_ys = base[0]
        ys_hi = place("ys_hi", [P, 4, T], F32R)
        ys_lo = place("ys_lo", [P, 4, T], F32R)
        kz = place("kz", [P, 4, CH + T])
        state = place("state", [P, GROUPS, HG * HD])
        vT = place("vT", [P, CH + T])
        th = place("th", [P, 2, T])
        ident = place("ident", [P, P])
        causal = place("causal", [P, P])
        partner = place("partner", [P, P])
        lng = place("lng", [P, D])
        lnb = place("lnb", [P, D])
        maskb = place("maskb", [P, NB, CH])
        prm = place("prm", [P, NPARAM])
        ada = place("ada", [P, 24])
        aneg = place("aneg", [P, 1])
        eps = place("eps", [P, 1])
        one = place("one", [P, 1])
        negsink = place("negsink", [P, KV, 4])
        hist = place("hist", [P, CONVT, 3])
        tok = place("tok", [P, 2, NT, 32])
        ecs = place("ecs", [P, NT, 32])
        stats = place("stats", [P, 2, NT, 2, 6])
        mv = place("mv", [P, 2, NT, 2])
        std = place("std", [P, 2, NT])
        rstd = place("rstd", [P, 2, NT])
        ss = place("ss", [P, NT])
        gstd = place("gstd", [P, NT])
        grs = place("grs", [P, NT])
        ends = place("ends", [P, 4, 2 * HG])
        top = place("top", [P, 2, 4])
        nbias = place("nbias", [P, 2, 4])
        nsink = place("nsink", [P, 2, 4])
        rsum = place("rsum", [P, 2, 4])
        esink = place("esink", [P, 2, 4])
        rden = place("rden", [P, 2, 4])
        o_r = base[0]
        K = 1024
        gmat = place("gmat", [P, HG, P], at=o_r)
        dif = place("dif", [P, HG, P], at=o_r + 4 * K)
        xdt = place("xdt", [P, 2, HG * HD], at=o_r + 8 * K)
        xd = place("xd", [P, 2, HG * HD], at=o_r + 12 * K)
        xw = place("xw", [P, HG * HD], at=o_r + 16 * K)
        bts = place("bts", [P, 2, P], at=o_r + 18 * K)
        cbm = place("cbm", [P, P], at=o_r + 19 * K)
        csb = place("csb", [P, 2, HG, P], at=o_r + 20 * K)
        u = place("u", [P, 2, T + 4], at=o_r + 28 * K)
        junk = place("junk", [P, T], at=o_r + 28 * K + 8 * (T + 4))
        o_y = o_r + 28 * K + 8 * (T + 4) + 4 * T
        ybuf = place("ybuf", [P, NT, HG * HD], at=o_y)
        silu_c = place("silu_c", [P, KT], at=o_y)
        dtmp = place("dtmp", [P, 3, T], at=o_y)
        rf = place("rf", [P, 2, T], at=o_r)
        ra = place("ra", [P, 2, T], at=o_r + 4 * K)
        rb = place("rb", [P, T], at=o_r + 8 * K)
        pbuf = place("pbuf", [P, 2, 4, P], at=o_r + 10 * K)
        ptb = place("ptb", [P, 2, 4, P], at=o_r + 14 * K)
        trg = place("trg", [P, 2, T], at=o_r + 20 * K)
        vw = place("vw", [P, NCH, 5 * HD], at=o_r + 24 * K)
        qbuf = place("qbuf", [P, NCH, 4, CH], at=o_y)
        mix_hi = place("mix_hi", [P, KT, T], F32R, at=o_r)
        mix_lo = place("mix_lo", [P, KT, T], F32R, at=o_r + 16 * K)
        og = place("og", [P, 2, T], at=o_r + 32 * K)
        hf = place("hf", [P, 2, T], at=o_r + 36 * K)
        ada_w = [place(f"ada_w{n}", [P, KT, T], at=a) for n, a in enumerate(
            [o_h + 16 * K * n for n in range(4)] + [o_ys, o_r])]
        end = o_y + 8 * K
        assert end <= nc.sbuf_usable_end, (end, nc.sbuf_usable_end)

        ubank = [ctx.enter_context(nc.psum_tensor(f"ubank{n}", [P, T], F32)) for n in range(UBANKS)]
        bank_x, bank_s, bank_y, bank_o = sbank = [
            ctx.enter_context(nc.psum_tensor(f"bank_{n}", [P, T], F32)) for n in "xsyo"]
        cs_dram = nc.dram_tensor("cs_dram", [NB, 32, T], F32, kind="Internal").ap()

        def par(name, n=None, m=None):
            at, size = PARAMS[name]
            if n is None:
                return prm[:, at:at + size]
            return prm[:, at + n:at + n + (m or 1)]

        sem = lambda name: ctx.enter_context(nc.semaphore(name))
        prm_landed, const_landed = sem("prm_landed"), sem("const_landed")
        setup_dve2, waited, ada_sum, ada_chain = sem("setup_dve2"), sem("waited"), sem("ada_sum"), sem("ada_chain")
        ada_landed = [sem(f"ada_landed{n}") for n in range(6)]
        setup_dve, setup_act, setup_pool, ada_filled = (sem(n) for n in ("setup_dve", "setup_act", "setup_pool", "ada_filled"))
        unit_filled = Signal("unit_filled", NU, 2)
        part_used = Signal("part_used", len(PARTS), 2)
        ht_filled = Signal("ht_filled", KT)
        xT_filled, bc_filled, yoff_filled, ydiag_filled, new_filled, fin_filled = (
            Signal(n, 16, 2) for n in ("xT_filled", "bc_filled", "yoff_filled", "ydiag_filled", "new_filled", "fin_filled"))
        perm_filled = Signal("perm_filled", 9, 2)
        vT_filled = Signal("vT_filled", 2)
        score_filled, pT_filled, pv_filled = (Signal(n, 16, 2) for n in ("score_filled", "pT_filled", "pv_filled"))
        outT_filled = Signal("outT_filled", KT, 2)
        pe_signals = [unit_filled, part_used, ht_filled, xT_filled, bc_filled, yoff_filled, ydiag_filled,
                      new_filled, fin_filled, perm_filled, vT_filled, score_filled, pT_filled, pv_filled, outT_filled]
        hi_ready = Signal("hi_ready", NL)
        hf_ready = Signal("hf_ready", KT)
        hstd_ready, lstd_ready = Signal("hstd_ready", 1), Signal("lstd_ready", 1)
        dt_parts = Signal("dt_parts", 1)
        ecs_ready = Signal("ecs_ready", 1)
        u_ready, tap_ready = Signal("u_ready", CONVT), Signal("tap_ready", CONVT)
        th_ready = Signal("th_ready", len(GATED), 2)
        decays_ready, e_ready, sq_ready = (Signal(n, 16, 2) for n in ("decays_ready", "e_ready", "sq_ready"))
        gstd_ready = Signal("gstd_ready", GROUPS)
        yhi_ready = Signal("yhi_ready", 24)
        rf_ready = Signal("rf_ready", 9)
        v_ready = Signal("v_ready", 1)
        p_ready, pt_ready = Signal("p_ready", 16, 2), Signal("pt_ready", 16, 2)
        mixhi_ready = Signal("mixhi_ready", KT)
        og_ready = Signal("og_ready", KT, 4)
        act_chain = Signal("act_chain", 4)
        act_signals = [hi_ready, hf_ready, hstd_ready, lstd_ready, dt_parts, ecs_ready, u_ready, tap_ready, th_ready, decays_ready, e_ready,
                       sq_ready, gstd_ready, yhi_ready, rf_ready, v_ready, p_ready, pt_ready, mixhi_ready, og_ready,
                       act_chain]
        hvar_ready, lvar_ready, x_chain = Signal("hvar_ready", 1), Signal("lvar_ready", 1), Signal("x_chain", 9)
        xn_ready = Signal("xn_ready", NT)
        hhi_ready = Signal("hhi_ready", KT, 2)
        dt_ready, cs_ready, tok_ready = Signal("dt_ready", 1), Signal("cs_ready", 1), Signal("tok_ready", 1)
        conv_done = Signal("conv_done", CONVT, 2)
        hist_in, hist_out = Signal("hist_in", CONVT, 2), Signal("hist_out", CONVT, 2)
        gated = Signal("gated", len(GATED), 2)
        dif_ready, ends_ready = Signal("dif_ready", 16, 2), Signal("ends_ready", 16, 2)
        xdt_ready, xd_ready, bts_ready, cbm_ready = (
            Signal(n, 16, 2) for n in ("xdt_ready", "xd_ready", "bts_ready", "cbm_ready"))
        g_ready, y1_ready, y_ready, state_ready = (
            Signal(n, 16, 2) for n in ("g_ready", "y1_ready", "y_ready", "state_ready"))
        yn_ready = Signal("yn_ready", 16)
        ylo_ready = Signal("ylo_ready", 24)
        acc_ready = Signal("acc_ready", len(BRANCH), 1)
        rot_ready = Signal("rot_ready", 9, 2)
        vw_ready = Signal("vw_ready", 2)
        nb_ready, rec_ready, yatt_ready = (Signal(n, 16, 2) for n in ("nb_ready", "rec_ready", "yatt_ready"))
        mixlo_ready = Signal("mixlo_ready", KT)
        res_ready = Signal("res_ready", KT, 2)
        out_ready = Signal("out_ready", NT)
        dve_chain = Signal("dve_chain", 126)
        dve_signals = [hvar_ready, lvar_ready, x_chain, xn_ready, hhi_ready, dt_ready, cs_ready, tok_ready, conv_done, hist_in, hist_out, gated, dif_ready,
                       ends_ready, xdt_ready, xd_ready, bts_ready, cbm_ready, g_ready, y1_ready, y_ready,
                       state_ready, yn_ready, ylo_ready, acc_ready, rot_ready, vw_ready, nb_ready, rec_ready,
                       yatt_ready, mixlo_ready, res_ready, out_ready, dve_chain]
        lo_ready = Signal("lo_ready", NL, 3)
        hlo_ready = Signal("hlo_ready", KT, 2)
        xw_ready, sdec_ready, y2_ready, gate_done = (
            Signal(n, 16, 4) for n in ("xw_ready", "sdec_ready", "y2_ready", "gate_done"))
        ra_ready = Signal("ra_ready", 9, 2)
        vz_ready = Signal("vz_ready", 1)
        pn_ready = Signal("pn_ready", 16, 2)
        mixf_ready = Signal("mixf_ready", KT)
        pool_signals = [lo_ready, hlo_ready, xw_ready, sdec_ready, y2_ready, gate_done, ra_ready,
                        vz_ready, pn_ready, mixf_ready]
        w_landed = [Landed(f"w_landed{n}", NL // RAW) for n in range(RAW)]
        x_landed, res_landed = Landed("x_landed", 1), Landed("res_landed", 1)
        cs_stored = Landed("cs_stored", 1)
        csb_landed = [Landed(f"csb_landed{n}", 8) for n in range(2)]
        trig_landed = Landed("trig_landed", 2)
        out_stored = Landed("out_stored", NT, 1)

        def release(l):
            if l < 0:
                n = UNIT[LOADS[NL + l]] + 1 - NU
                return unit_filled, n
            key = LOADS[l]
            if key in PARTS:
                return part_used, PARTS[key] + 1
            if key[0] == "dt":
                return unit_filled, UNIT[("dt",)] + 1
            if key[0] == "z":
                return unit_filled, UNIT[("z", key[1], 3)] + 1
            if key[0] == "br":
                return unit_filled, UNIT[("br", key[1], 2 * key[2] + 1)] + 1
            return unit_filled, UNIT[key] + 1

        def drained(n):
            if n < 0:
                return og_ready, UNITS[NU + n][1] + 1 - KT
            key = UNITS[n]
            kind = key[0]
            if kind == "dt":
                return dt_parts, 1
            if kind == "dtT":
                return tok_ready, 1
            if kind == "x":
                return u_ready, key[1] * 6 + key[2] + 1
            if kind in ("z", "gate"):
                return gated, GATED[key] + 1
            if kind in ("ms", "ma"):
                return th_ready, GATED[key] + 1
            if kind == "k":
                return rf_ready, 1
            if kind == "q":
                return rf_ready, 2 + 4 * key[1] + key[2]
            if kind == "v":
                return v_ready, 1
            if kind == "br":
                return acc_ready, BRANCH[key] + 1
            return og_ready, key[1] + 1

        block = ctx.enter_context(nc.Block())
        w_in_t = w_in[0].rearrange("(k p) n -> p k n", p=P)
        w_ada_t = w_ada[0].rearrange("(k p) n -> p k n", p=P)
        w_out_t = w_out[0].rearrange("(k p) n -> p k n", p=P)
        w_bra_t = w_br_attn[0].rearrange("(k p) n -> p k n", p=P)
        w_brs_t = w_br_ssd[0].rearrange("(k p) n -> p k n", p=P)

        def raw_view(l):
            key = LOADS[l]
            kind = key[0]
            slot = w_raw[:, l % RAW, :]
            if kind == "dt":
                return slot[:, 0:512].rearrange("p (k n) -> p k n", n=P), w_in_t[:, 4 * key[1]:4 * key[1] + 4, COL_DT:COL_DT + P]
            if kind == "z":
                c = COL_Z + 512 * key[1]
                return slot.rearrange("p (k n) -> p k n", n=512), w_in_t[:, 2 * key[2]:2 * key[2] + 2, c:c + 512]
            if kind == "br":
                br, i = key[1], key[2]
                src = w_brs_t[:, 4 * br:4 * br + 4] if br < GROUPS else w_bra_t[:, 4 * (br - GROUPS):4 * (br - GROUPS) + 4]
                return slot.rearrange("p (k n) -> p k n", n=256), src[:, :, 256 * i:256 * i + 256]
            slot = slot.rearrange("p (k n) -> p k n", n=P)
            if kind == "out":
                return slot, w_out_t[:, :, P * key[1]:P * key[1] + P]
            c = {"x": lambda: COL_XBC + P * (4 * key[1] + key[2] if key[2] < 4 else 16 + 4 * (key[2] - 4) + key[1]),
                 "k": lambda: COL_K, "v": lambda: COL_V,
                 "q": lambda: COL_Q + P * (4 * key[1] + key[2]), "gate": lambda: COL_GATE + P * (4 * key[1] + key[2]),
                 "ma": lambda: COL_MERGE + P * key[1], "ms": lambda: COL_MERGE + D + P * key[1]}[kind]()
            return slot, w_in_t[:, :, c:c + P]

        def width(l):
            return 512 if LOADS[l][0] == "dt" else KT * P

        @block.sync
        def _(sp):
            def load_x(dst, row, signal):
                sp.dma_start(dst[:, :, :], x[0, bass.ds(row, T), :].rearrange("(t p) d -> p t d", p=P)).then_inc(*signal.done())

            sp.dma_start(prm[:, :], params).then_inc(prm_landed, 16)
            load_x(xn, 0, x_landed)
            for n, t in enumerate((ident, causal, partner)):
                sp.dma_start(t[:, :], consts[n]).then_inc(const_landed, 16)
            for n in range(6):
                sp.dma_start(ada_w[n][:, :, :], w_ada_t[:, :, T * n:T * n + T]).then_inc(ada_landed[n], 16)
            sp.dma_start(maskb[:, :, :], kmask).then_inc(const_landed, 16)
            sp.dma_start(lng[:, :], ln_g.partition_broadcast(P)).then_inc(const_landed, 16)
            sp.dma_start(lnb[:, :], ln_b.partition_broadcast(P)).then_inc(const_landed, 16)

            def load(b, l, ahead):
                slot, src = raw_view(l)
                sp.wait_ge(*lo_ready.at(b, l - RAW + 1, ahead))
                sp.dma_start(slot, src).then_inc(*w_landed[l % RAW].done())

            for l in range(RAW):
                load(0, l, 0)

            def body(b, last):
                snap = (lambda v: v) if last else sp.snap
                for l in range(RAW, NL):
                    if LOADS[l] == ("ms", 5) and not last:
                        row = snap(b * T + T)
                        sp.wait_ge(*ylo_ready.at(b, 24))
                        load_x(xn, row, x_landed)
                    if LOADS[l] == ("out", 2):
                        row = snap(b * T)
                        sp.wait_ge(*mixf_ready.at(b, KT))
                        load_x(res, row, res_landed)
                    load(b, l, 0)
                if not last:
                    for l in range(RAW):
                        load(b, l, 1)
                for tt in range(NT):
                    row = snap(b * T + tt * P)
                    sp.wait_ge(*out_ready.at(b, tt + 1))
                    sp.dma_start(out[0, bass.ds(row, P), :], res[:, tt, :]).then_inc(*out_stored.done())

            with sp.Fori(0, NB - 1) as b:
                body(b, False)
            body(NB - 1, True)
            sp.wait_ge(out_stored.sem, 16 * (NT * NB + 1))

        @block.tensor
        def _(pe):
            def turn_h(b, ahead, k):
                if k >= 4:
                    pe.wait_ge(*hf_ready.at(b, k - 3, ahead))
                for tt in range(NT):
                    mm = pe.transpose(sbank[k % 4][:, P * tt:P * tt + P], xn[:, tt, P * k:P * k + P], ident[:, :])
                mm.then_inc(*ht_filled.done())

            for s in pe_signals:
                pe.sem_inc(s.sem, s.credit)
            for n in range(6):
                pe.wait_ge(ada_sum, n + 1)
                for t in range(4):
                    mm = pe.matmul(ubank[3][:, 4 * n + t:4 * n + t + 1], th[:, n % 2, P * t:P * t + P], one[:, :],
                                   start=True, stop=True)
                mm.then_inc(ada_filled, 1)
                if n == 3:
                    pe.wait_ge(const_landed, 96)
                    pe.wait_ge(setup_pool, 3)
                    pe.wait_ge(*xn_ready.at(0, NT))
                    for k in range(KT):
                        turn_h(0, 0, k)

            def body(b, last):
                def three(out_ap, a_hi, a_lo, m_hi, m_lo, first, last):
                    pe.matmul(out_ap, a_hi, m_hi, start=first, stop=False)
                    pe.matmul(out_ap, a_hi, m_lo, start=False, stop=False)
                    return pe.matmul(out_ap, a_lo, m_hi, start=False, stop=last)

                def bank_for(key):
                    n = UNIT[key]
                    s, at = drained(n - UBANKS)
                    pe.wait_ge(*s.at(b, at))
                    if n == 3:
                        pe.wait_ge(setup_dve, 9)
                    return ubank[n % UBANKS][:, :]

                def split_slot(l, n):
                    pe.wait_ge(*lo_ready.at(b, l + 1))
                    view = lambda w: w[:, l % SPLIT, :].rearrange("p (k n) -> p k n", n=n)
                    return view(w_hi), view(w_lo)

                def project(key, m_hi=h_hi, m_lo=h_lo):
                    bank = bank_for(key)
                    hi, lo = split_slot(LOAD[key], P)
                    for k in range(KT):
                        mm = three(bank, hi[:, k, :], lo[:, k, :], m_hi[:, k, :], m_lo[:, k, :], k == 0, k == KT - 1)
                    mm.then_inc(*unit_filled.done())

                def z_part(g, i):
                    banks = [bank_for(("z", g, tt)) for tt in range(NT)] if i == 0 else [
                        ubank[UNIT[("z", g, tt)] % UBANKS][:, :] for tt in range(NT)]
                    hi, lo = split_slot(LOAD[("z", g, i)], 512)
                    for j in range(2):
                        k = 2 * i + j
                        for tt in range(NT):
                            tk = slice(P * tt, P * tt + P)
                            pe.matmul(banks[tt], h_hi[:, k, tk], hi[:, j, :], start=(k == 0), stop=False)
                            pe.matmul(banks[tt], h_hi[:, k, tk], lo[:, j, :], start=False, stop=False)
                            mm = pe.matmul(banks[tt], h_lo[:, k, tk], hi[:, j, :], start=False, stop=(k == KT - 1))
                            if k == KT - 1:
                                mm.then_inc(*unit_filled.done())
                    if i < 3:
                        mm.then_inc(*part_used.done())

                def branch(br, m):
                    bank = bank_for(("br", br, m))
                    hi, lo = split_slot(LOAD[("br", br, m // 2)], 256)
                    if m == 0:
                        pe.wait_ge(*ylo_ready.at(b, 4 * br + 4))
                    cols = slice(P * (m % 2), P * (m % 2) + P)
                    for k in range(4):
                        mm = three(bank, hi[:, k, cols], lo[:, k, cols], ys_hi[:, k, :], ys_lo[:, k, :], k == 0, k == 3)
                    mm.then_inc(*unit_filled.done())

                pe.wait_ge(*hlo_ready.at(b, KT))
                bank = bank_for(("dt",))
                for i in range(2):
                    hi, lo = split_slot(LOAD[("dt", i)], P)
                    for k in range(4):
                        mm = three(bank, hi[:, k, :], lo[:, k, :], h_hi[:, 4 * i + k, :], h_lo[:, 4 * i + k, :],
                                   i == 0 and k == 0, i == 1 and k == 3)
                    mm.then_inc(*(unit_filled if i else part_used).done())

                def pre(s):
                    g, c = divmod(s, NT)
                    tk = slice(P * c, P * c + P)
                    if c == 0:
                        pe.wait_ge(*gated.at(b, GATED[("x", g, 5)] + 1))
                        pe.wait_ge(*ylo_ready.at(b, 4 * g))
                        pe.wait_ge(*hlo_ready.at(b, KT))
                    pe.wait_ge(*xd_ready.at(b, s))
                    for t in range(4):
                        mm = pe.transpose(bank_x[:, P * t:P * t + P], conv[:, t, tk], ident[:, :])
                    mm.then_inc(*xT_filled.done())
                    pe.wait_ge(*cbm_ready.at(b, s))
                    pe.transpose(bank_s[:, 0:P], conv[:, 4, tk], ident[:, :])
                    pe.matmul(bank_s[:, P:2 * P], conv[:, 4, tk], conv[:, 5, tk], start=True, stop=True
                              ).then_inc(*bc_filled.done())

                def finish(g):
                    pe.wait_ge(*yn_ready.at(b, 4 * g + 4))
                    for t in range(4):
                        for c in range(NT):
                            mm = pe.transpose(sbank[t][:, P * c:P * c + P], ybuf[:, c, P * t:P * t + P], ident[:, :])
                        mm.then_inc(*fin_filled.done())

                def filler(g, c, half):
                    for kind, n in fillers(g, c, half):
                        if kind == "z":
                            z_part(g, n)
                        else:
                            branch(g - 1, n)

                for g in range(GROUPS):
                    for t in range(6):
                        project(("x", g, t))
                        if t == 1 and g:
                            finish(g - 1)
                        if g == 0 and t == 2:
                            bank = bank_for(("dtT",))
                            pe.wait_ge(*cs_ready.at(b, 1))
                            for n, src in enumerate((1, 2)):
                                for c in range(NT):
                                    mm = pe.matmul(bank[:, P * n + 32 * c:P * n + 32 * c + 32],
                                                   dtmp[:, src, P * c:P * c + P], ident[:, 0:32], start=True, stop=True)
                            mm.then_inc(*unit_filled.done())
                    z_part(g, 0)
                    pre(4 * g)
                    for c in range(NT):
                        s = 4 * g + c
                        pe.wait_ge(*state_ready.at(b, s))
                        pe.matmul(bank_o[:, :], conv[:, 5, P * c:P * c + P], state[:, g, :], start=True, stop=True
                                  ).then_inc(*yoff_filled.done())
                        pe.wait_ge(*g_ready.at(b, s + 1))
                        pe.wait_ge(*y_ready.at(b, s))
                        for h in range(HG):
                            mm = pe.matmul(bank_y[:, HD * h:HD * h + HD], gmat[:, h, :],
                                           xdt[:, s % 2, HD * h:HD * h + HD], start=True, stop=True)
                        mm.then_inc(*ydiag_filled.done())
                        if c < NT - 1:
                            pre(s + 1)
                        filler(g, c, 0)
                        pe.wait_ge(*y1_ready.at(b, s + 1))
                        pe.wait_ge(*xw_ready.at(b, s + 1))
                        pe.matmul(bank_o[:, :], bts[:, s % 2, :], xw[:, :], start=True, stop=True
                                  ).then_inc(*new_filled.done())
                        filler(g, c, 1)

                project(("k",))
                project(("v",))
                finish(3)

                def partners(r):
                    pe.wait_ge(*rf_ready.at(b, r + 1))
                    pe.wait_ge(*rot_ready.at(b, r - 1))
                    if r == 0:
                        pe.wait_ge(*ylo_ready.at(b, 16))
                    pe.matmul((bank_y, bank_s)[r % 2][:, :], partner[:, :], rf[:, r % 2, :], start=True, stop=True
                              ).then_inc(*perm_filled.done())

                def turn_v():
                    pe.wait_ge(*v_ready.at(b, 1))
                    for n, bk in enumerate((bank_x, bank_o)):
                        for c in range(4):
                            w0 = CH * (4 * n + c)
                            mm = pe.transpose(bk[:, P * c:P * c + P], vT[:, w0:w0 + P], ident[:, :])
                        mm.then_inc(*vT_filled.done())

                def scores(a):
                    kv, c = divmod(a, NCH)
                    pe.wait_ge(*rot_ready.at(b, 5 + 4 * kv))
                    pe.wait_ge(*p_ready.at(b, a - 1))
                    pe.wait_ge(*vw_ready.at(b, 2))
                    for sl in range(4):
                        half, pair = divmod(sl, 2)
                        mm = pe.matmul((bank_x, bank_s)[a % 2][:, P * sl:P * sl + P], qbuf[:, c, 2 * pair:2 * pair + 2, :],
                                       kz[:, 2 * kv + half, CH * c:CH * c + P], start=True, stop=True)
                    mm.then_inc(*score_filled.done())

                for kv in range(KV):
                    for j in range(4):
                        project(("q", kv, j))
                        if kv == 0 and j == 0:
                            partners(0)
                            turn_v()
                        if j:
                            partners(4 * kv + j)
                    for j in range(4):
                        project(("gate", kv, j))
                        if j == 0:
                            partners(4 * kv + 4)
                    scores(8 * kv)
                    scores(8 * kv + 1)
                    for c in range(NCH):
                        a = 8 * kv + c
                        if 0 < c < NCH - 1:
                            scores(a + 1)
                        pe.wait_ge(*pn_ready.at(b, a + 1))
                        pe.wait_ge(*pt_ready.at(b, a))
                        for sl in range(4):
                            mm = pe.transpose(bank_y[:, P * sl:P * sl + P], pbuf[:, a % 2, sl, :], ident[:, :])
                        mm.then_inc(*pT_filled.done())
                        branch(3 + kv, c)
                        pe.wait_ge(*pt_ready.at(b, a + 1))
                        pe.wait_ge(*yatt_ready.at(b, a))
                        for half in range(2):
                            v0 = HD * (2 * kv + 1 - half)
                            mm = pe.matmul(bank_o[:, 0:256], vw[:, c, v0:v0 + P], ptb[:, a % 2, 2 * half:2 * half + 2, :],
                                           start=(half == 0), stop=(half == 1))
                        mm.then_inc(*pv_filled.done())

                for m in range(KT):
                    project(("ms", m))
                for m in range(KT):
                    branch(5, m)
                for m in range(KT):
                    project(("ma", m))

                def back(m):
                    pe.wait_ge(*og_ready.at(b, m + 1))
                    pe.wait_ge(*res_ready.at(b, m - 1))
                    for tt in range(NT):
                        mm = pe.transpose((bank_x, bank_y)[m % 2][:, P * tt:P * tt + P], og[:, m % 2, P * tt:P * tt + P],
                                          ident[:, :])
                    mm.then_inc(*outT_filled.done())

                if not last:
                    pe.wait_ge(*xn_ready.at(b, NT, 1))
                    for k in range(4):
                        turn_h(b, 1, k)
                pe.wait_ge(*mixlo_ready.at(b, KT))
                for m in range(KT):
                    project(("out", m), mix_hi, mix_lo)
                    if m == 0 and not last:
                        for k in range(4, KT):
                            turn_h(b, 1, k)
                    if m == 1 and not last:
                        pe.wait_ge(*hf_ready.at(b, KT, 1))
                    if m:
                        back(m - 1)
                back(KT - 1)

            with pe.Fori(0, NB - 1) as b:
                body(b, False)
            body(NB - 1, True)

        @block.scalar
        def _(act):
            for s in act_signals:
                act.sem_inc(s.sem, s.credit)
            act.wait_ge(prm_landed, 16)
            act.activation(silu_c[:, :], par("c"), ACT.Tanh, scale=0.5).then_inc(setup_act, 1)
            act.activation(aneg[:, :], par("a_log"), ACT.Exp).then_inc(setup_act, 1)
            def split(b, l):
                ahead, l = divmod(l, NL)
                act.wait_ge(*w_landed[l % RAW].at(b, l // RAW + 1, ahead))
                s, at = release(l - SPLIT)
                act.wait_ge(*s.at(b, at, ahead))
                n = width(l)
                act.activation(w_hi[:, l % SPLIT, 0:n], w_raw[:, l % RAW, 0:n], ACT.Copy).then_inc(*hi_ready.done())

            def h_std(b, ahead):
                act.wait_ge(*hvar_ready.at(b, 1, ahead))
                act.activation(std[:, 0, :], mv[:, 0, :, 1], ACT.Sqrt, bias=eps[:, :]).then_inc(*hstd_ready.done())

            def h_full(b, ahead, k):
                act.wait_ge(*ht_filled.at(b, k + 1, ahead))
                act.wait_ge(*hhi_ready.at(b, k - 1, ahead))
                act.wait_ge(*hlo_ready.at(b, k - 1, ahead))
                act.activation(hf[:, k % 2, :], sbank[k % 4][:, :], ACT.Identity, scale=ada[:, 8 + k:9 + k],
                               bias=ada[:, k:k + 1]).then_inc(*hf_ready.done())

            act.wait_ge(setup_dve, 6)
            h_std(0, 0)
            split(0, 0)
            split(0, 1)
            act.wait_ge(setup_dve, 8)
            for k in range(KT):
                h_full(0, 0, k)

            def body(b, last):
                chain = act_chain

                def next_split(key):
                    if LOAD[key] + SPLIT < NL or not last:
                        split(b, LOAD[key] + SPLIT)

                def filled(key):
                    act.wait_ge(*unit_filled.at(b, UNIT[key] + 1))
                    return ubank[UNIT[key] % UBANKS][:, :]

                def tanh(key, src, **kw):
                    n = GATED[key]
                    act.wait_ge(*gated.at(b, n - 1))
                    act.activation(th[:, n % 2, :], src, ACT.Tanh, **kw).then_inc(*th_ready.done())

                next_split(("dt", 0))
                bank = filled(("dt",))
                next_split(("dt", 1))
                act.activation(dtmp[:, 0, :], bank, ACT.Abs, bias=par("dt_bias")).then_inc(*chain.done())
                act.activation(dtmp[:, 1, :], bank, ACT.Relu, bias=par("dt_bias")).then_inc(*chain.done())
                act.wait_ge(*chain.at(b, 1))
                act.activation(dtmp[:, 0, :], dtmp[:, 0, :], ACT.Exp, scale=-1.0).then_inc(*chain.done())
                act.wait_ge(*chain.at(b, 3))
                act.activation(dtmp[:, 0, :], dtmp[:, 0, :], ACT.Ln, bias=one[:, :]).then_inc(*dt_parts.done())

                def load_csb(s):
                    g, c = divmod(s, NT)
                    src = cs_dram[bass.ds(b, 1), HG * g:HG * g + HG, P * c:P * c + P].rearrange("a h t -> (a h) t")
                    act.dma_start(csb[:, s % 2, :, :], src.partition_broadcast(P)).then_inc(*csb_landed[s % 2].done())

                def decays(s):
                    act.wait_ge(*ends_ready.at(b, s + 1))
                    act.activation(ends[:, s % 4, :], ends[:, s % 4, :], ACT.Exp).then_inc(*decays_ready.done())
                    act.wait_ge(*dif_ready.at(b, s + 1))
                    act.activation(dif[:, :, :], dif[:, :, :], ACT.Exp).then_inc(*e_ready.done())
                    if s + 2 < 16:
                        load_csb(s + 2)

                def square(s):
                    g, c = divmod(s, NT)
                    act.wait_ge(*gate_done.at(b, s + 1))
                    act.wait_ge(*sq_ready.at(b, s))
                    act.activation(junk[:, :], ybuf[:, c, :], ACT.Square, accum_out=ss[:, c:c + 1]
                                   ).then_inc(*sq_ready.done())

                def finish(g):
                    act.wait_ge(*sq_ready.at(b, 4 * g + 4))
                    act.activation(gstd[:, :], ss[:, :], ACT.Sqrt, scale=0.25 / 512, bias=eps[:, :]
                                   ).then_inc(*gstd_ready.done())

                def finish_hi(g):
                    if g:
                        act.wait_ge(*unit_filled.at(b, UNIT[("br", g - 1, 7)] + 1))
                    for t in range(4):
                        act.wait_ge(*fin_filled.at(b, 4 * g + t + 1))
                        act.activation(ys_hi[:, t, :], sbank[t][:, :], ACT.Copy, scale=par("norm_w", 4 * g + t)
                                       ).then_inc(*yhi_ready.done())

                def conv_in(g, t):
                    n = 6 * g + t
                    ct = 4 * g + t if t < 4 else 16 + 4 * (t - 4) + g
                    bank = filled(("x", g, t))
                    next_split(("x", g, t))
                    act.wait_ge(*conv_done.at(b, n - 1))
                    act.wait_ge(*hist_out.at(b, n - 1))
                    act.activation(conv[:, t, :], bank, ACT.Identity, scale=par("conv_w", 4 * ct + 3),
                                   bias=par("conv_b", ct)).then_inc(*tap_ready.done())
                    act.activation(u[:, n % 2, 3:3 + T], bank, ACT.Copy).then_inc(*u_ready.done())

                def conv_tanh(g, t):
                    act.wait_ge(*conv_done.at(b, 6 * g + t + 1))
                    tanh(("x", g, t), conv[:, t, :])

                def filler(g, c, half):
                    for kind, n in fillers(g, c, half):
                        if kind == "z":
                            next_split(("z", g, n))
                            if n == 3:
                                for tt in range(NT):
                                    tanh(("z", g, tt), filled(("z", g, tt)), scale=0.5)
                        elif n % 2:
                            next_split(("br", g - 1, n // 2))

                for g in range(GROUPS):
                    for t in range(6):
                        if t == 0 and g:
                            act.wait_ge(*yoff_filled.at(b, 4 * g))
                        conv_in(g, t)
                        if t:
                            conv_tanh(g, t - 1)
                        if t == 1 and g:
                            finish_hi(g - 1)
                        if g == 0 and t == 2:
                            act.wait_ge(*cs_ready.at(b, 1))
                            act.dma_start(cs_dram[bass.ds(b, 1), :, :].rearrange("a h t -> (a h) t"), dtmp[0:32, 2, :]
                                          ).then_inc(*cs_stored.done())
                        if g == 0 and t == 4:
                            act.wait_ge(*tok_ready.at(b, 1))
                            act.activation(ecs[:, :, :], tok[:, 1, :, :], ACT.Exp).then_inc(*ecs_ready.done())
                            act.wait_ge(*cs_stored.at(b, 1))
                            load_csb(0)
                            load_csb(1)
                    conv_tanh(g, 5)
                    next_split(("z", g, 0))
                    if g == 0:
                        decays(0)
                    decays(4 * g + 1)
                    for c in range(NT):
                        s = 4 * g + c
                        if c < NT - 1 and s + 2 < 16:
                            decays(s + 2)
                        filler(g, c, 0)
                        filler(g, c, 1)
                        if c == z_step(g):
                            for n in range(c):
                                square(4 * g + n)
                        if c >= z_step(g):
                            square(s)
                    finish(g)

                def rope_in(r, key, name, n):
                    bank = filled(key)
                    next_split(key)
                    act.wait_ge(*ra_ready.at(b, r - 1))
                    act.wait_ge(*perm_filled.at(b, r - 1))
                    act.activation(rf[:, r % 2, :], bank, ACT.Identity, bias=par(name, n)).then_inc(*rf_ready.done())

                for n in range(2):
                    src = trig[n][:, bass.ds(b * T, T)]
                    act.dma_start(trg[:, n, :], src).then_inc(*trig_landed.done())
                rope_in(0, ("k",), "b_k", 0)
                act.activation(vT[:, 0:CH], vT[:, T:T + CH], ACT.Copy).then_inc(*chain.done())
                bank = filled(("v",))
                next_split(("v",))
                act.wait_ge(*chain.at(b, 4))
                act.activation(vT[:, CH:], bank, ACT.Identity, scale=0.5, bias=par("b_v")).then_inc(*v_ready.done())
                finish_hi(3)

                def attn_hi(kv, j):
                    act.wait_ge(*yatt_ready.at(b, 8 * kv + 8))
                    act.wait_ge(*unit_filled.at(b, UNIT[("br", 3 + kv, 7)] + 1))
                    act.activation(ys_hi[:, j, :], zbuf[:, j, :], ACT.Copy).then_inc(*yhi_ready.done())

                def softmax(a):
                    act.wait_ge(*nb_ready.at(b, a + 1))
                    act.wait_ge(*pT_filled.at(b, a - 1))
                    act.wait_ge(*rec_ready.at(b, a - 1))
                    for sl in range(4):
                        act.activation(pbuf[:, a % 2, sl, :], (bank_x, bank_s)[a % 2][:, P * sl:P * sl + P], ACT.Exp, scale=SCALE,
                                       bias=nbias[:, a % 2, sl:sl + 1], accum_out=rsum[:, a % 2, sl:sl + 1])
                    act.activation(esink[:, a % 2, :], nsink[:, a % 2, :], ACT.Exp).then_inc(*p_ready.done())

                for kv in range(KV):
                    for j in range(4):
                        rope_in(1 + 4 * kv + j, ("q", kv, j), "b_q", 4 * kv + j)
                    if kv:
                        for j in range(4):
                            attn_hi(kv - 1, j)
                    for j in range(4):
                        bank = filled(("gate", kv, j))
                        next_split(("gate", kv, j))
                        tanh(("gate", kv, j), bank, scale=0.5)
                    softmax(8 * kv)
                    softmax(8 * kv + 1)
                    for c in range(NCH):
                        a = 8 * kv + c
                        act.wait_ge(*pT_filled.at(b, a + 1))
                        act.wait_ge(*pv_filled.at(b, a - 1))
                        act.activation(ptb[:, a % 2, :, :], bank_y[:, :].rearrange("p (s k) -> p s k", k=P), ACT.Copy
                                       ).then_inc(*pt_ready.done())
                        if c % 2:
                            next_split(("br", 3 + kv, c // 2))
                        if c < NCH - 2:
                            softmax(a + 2)

                for j in range(4):
                    attn_hi(1, j)
                for m in range(KT):
                    bank = filled(("ms", m))
                    next_split(("ms", m))
                    tanh(("ms", m), bank, scale=0.5, bias=par("b_merge", 8 + m))
                for i in range(4):
                    next_split(("br", 5, i))
                if not last:
                    h_std(b, 1)

                def mix_in(m):
                    act.wait_ge(*mixf_ready.at(b, m + 1))
                    act.activation(mix_hi[:, m, :], acc_s[:, m, :], ACT.Copy).then_inc(*mixhi_ready.done())

                for m in range(KT):
                    bank = filled(("ma", m))
                    next_split(("ma", m))
                    tanh(("ma", m), bank, scale=0.5, bias=par("b_merge", m))
                    if m:
                        mix_in(m - 1)
                mix_in(KT - 1)
                if not last:
                    for k in range(4):
                        h_full(b, 1, k)
                for m in range(KT):
                    if m == 1 and not last:
                        for k in range(4, KT):
                            h_full(b, 1, k)
                    bank = filled(("out", m))
                    next_split(("out", m))
                    act.wait_ge(*outT_filled.at(b, m - 1))
                    act.activation(og[:, m % 2, :], bank, ACT.Copy, scale=ada[:, 16 + m:17 + m]).then_inc(*og_ready.done())
                act.wait_ge(*lvar_ready.at(b, 1))
                act.activation(std[:, 1, :], mv[:, 1, :, 1], ACT.Sqrt, bias=eps[:, :]).then_inc(*lstd_ready.done())

            with act.Fori(0, NB - 1) as b:
                body(b, False)
            body(NB - 1, True)

        @block.vector
        def _(dve):
            for s in dve_signals:
                dve.sem_inc(s.sem, s.credit)
            dve.memset(eps[:, :], EPS)
            dve.memset(one[:, :], 1.0)
            dve.memset(kz[:, :, :], 0.0)
            dve.wait_ge(setup_act, 2)
            dve.scalar_tensor_tensor(silu_c[:, :], silu_c[:, :], 1.0, par("c"), ALU.add, ALU.mult).then_inc(setup_dve2, 1)
            dve.wait_ge(setup_dve2, 1)
            dve.tensor_scalar(silu_c[:, :], silu_c[:, :], 0.5, None, ALU.mult).then_inc(setup_dve, 1)
            for name in ("conv_w", "conv_b", "b_merge", "norm_w", "b_v"):
                dve.tensor_scalar(par(name), par(name), 0.5, None, ALU.mult).then_inc(setup_dve, 1)
            dve.tensor_scalar(aneg[:, :], aneg[:, :], -1.0, None, ALU.mult).then_inc(setup_dve2, 1)
            dve.tensor_scalar(negsink[:, :, :].rearrange("p a b -> p (a b)"), par("sink"), -1.0, None, ALU.mult
                              ).then_inc(setup_dve2, 1)
            def x_norm(b, ahead):
                dve.wait_ge(*x_landed.at(b, 1, ahead))
                for tt in range(NT):
                    for n in range(2):
                        dve.bn_stats(stats[:, 0, tt, n, :], xn[:, tt, 512 * n:512 * n + 512]).then_inc(*x_chain.done())
                dve.wait_ge(*x_chain.at(b, 8, ahead))
                dve.sem_inc(waited, 1)
                for tt in range(NT):
                    ins = dve.bn_aggr(mv[:, 0, tt, :], stats[:, 0, tt, :, :])
                ins.then_inc(*hvar_ready.done())
                dve.wait_ge(*hstd_ready.at(b, 1, ahead))
                dve.reciprocal(rstd[:, 0, :], std[:, 0, :]).then_inc(*x_chain.done())
                dve.wait_ge(*x_chain.at(b, 9, ahead))
                for tt in range(NT):
                    dve.tensor_scalar(xn[:, tt, :], xn[:, tt, :], mv[:, 0, tt, 0:1], rstd[:, 0, tt:tt + 1],
                                      ALU.subtract, ALU.mult).then_inc(*xn_ready.done())

            def h_high(b, ahead, k):
                dve.wait_ge(*hf_ready.at(b, k + 1, ahead))
                dve.tensor_copy(h_hi[:, k, :], hf[:, k % 2, :]).then_inc(*hhi_ready.done())

            def ada_chunk(n):
                dve.wait_ge(ada_landed[n], 16)
                if n > 1:
                    dve.wait_ge(ada_filled, n - 1)
                dve.tensor_scalar(th[:, n % 2, :], ada_w[n][:, 0, :], silu_c[:, 0:1], None, ALU.mult).then_inc(ada_chain, 1)
                for k in range(1, KT):
                    dve.wait_ge(ada_chain, (KT - 1) * n + k)
                    dve.scalar_tensor_tensor(th[:, n % 2, :], ada_w[n][:, k, :], silu_c[:, k:k + 1], th[:, n % 2, :],
                                             ALU.mult, ALU.add).then_inc(ada_chain if k < KT - 1 else ada_sum, 1)

            dve.wait_ge(setup_dve, 6)
            x_norm(0, 0)
            for n in range(4):
                ada_chunk(n)
            dve.wait_ge(ada_filled, 4)
            dve.tensor_tensor(ada[:, 0:16], ubank[3][:, 0:16], par("b_ada")[:, 0:16], ALU.add).then_inc(setup_dve2, 1)
            dve.wait_ge(setup_dve2, 4)
            dve.tensor_scalar(ada[:, 8:16], ada[:, 8:16], 1.0, None, ALU.add).then_inc(setup_dve, 2)
            for k in range(KT):
                h_high(0, 0, k)
            for n in (4, 5):
                ada_chunk(n)
            dve.wait_ge(ada_filled, 6)
            dve.tensor_tensor(ada[:, 16:24], ubank[3][:, 16:24], par("b_ada")[:, 16:24], ALU.add).then_inc(setup_dve2, 1)
            dve.wait_ge(setup_dve2, 5)
            dve.tensor_scalar(ada[:, 16:24], ada[:, 16:24], 0.5, None, ALU.mult).then_inc(setup_dve, 1)
            dve.wait_ge(setup_dve, 9)
            dve.wait_ge(const_landed, 96)
            dve.wait_ge(setup_pool, 3)

            def body(b, last):
                chain = dve_chain
                link = [0]

                def done_link():
                    link[0] += 1
                    return chain.done()

                def after_link():
                    dve.wait_ge(*chain.at(b, link[0]))

                dve.wait_ge(*dt_parts.at(b, 1))
                dve.tensor_tensor(dtmp[:, 1, :], dtmp[:, 0, :], dtmp[:, 1, :], ALU.add).then_inc(*dt_ready.done())
                dve.wait_ge(*dt_ready.at(b, 1))
                dve.tensor_scalar(dtmp[:, 0, :], dtmp[:, 1, :], aneg[:, :], None, ALU.mult).then_inc(*done_link())
                after_link()
                for c in range(NT):
                    ins = dve.tensor_tensor_scan(dtmp[:, 2, P * c:P * c + P], one[:, :].to_broadcast([P, P]), dtmp[:, 0, P * c:P * c + P],
                                                  0.0, ALU.mult, ALU.add)
                ins.then_inc(*cs_ready.done())

                def conv_taps(g, t):
                    n = 6 * g + t
                    ct = 4 * g + t if t < 4 else 16 + 4 * (t - 4) + g
                    dve.wait_ge(*conv_done.at(b, n - 1))
                    dve.wait_ge(*hist_out.at(b, n - 1))
                    dve.tensor_copy(u[:, n % 2, 0:3], hist[:, ct, :]).then_inc(*hist_in.done())
                    dve.wait_ge(*u_ready.at(b, n + 1))
                    dve.wait_ge(*hist_in.at(b, n + 1))
                    dve.tensor_copy(hist[:, ct, :], u[:, n % 2, T:T + 3]).then_inc(*hist_out.done())
                    for w in range(3):
                        ins = dve.scalar_tensor_tensor(conv[:, t, :], u[:, n % 2, w:w + T], par("conv_w", 4 * ct + w),
                                                       conv[:, t, :], ALU.mult, ALU.add)
                        if w < 2:
                            ins.then_inc(*done_link())
                            after_link()
                        else:
                            ins.then_inc(*conv_done.done())

                def gate(key, out_ap, src):
                    n = GATED[key]
                    dve.wait_ge(*th_ready.at(b, n + 1))
                    dve.scalar_tensor_tensor(out_ap, th[:, n % 2, :], 1.0, src, ALU.add, ALU.mult).then_inc(*gated.done())

                def pre_a(s):
                    g, c = divmod(s, NT)
                    heads = slice(HG * g, HG * g + HG)
                    dve.wait_ge(*csb_landed[s % 2].at(b, s // 2 + 1))
                    dve.wait_ge(*xw_ready.at(b, s - 3))
                    dve.wait_ge(*sdec_ready.at(b, s - 3))
                    dve.tensor_tensor(ends[:, s % 4, 0:HG], csb[:, s % 2, :, P - 1], tok[:, 1, c, heads], ALU.subtract)
                    dve.tensor_copy(ends[:, s % 4, HG:], csb[:, s % 2, :, P - 1]).then_inc(*ends_ready.done())
                    dve.wait_ge(*g_ready.at(b, s))
                    for h in range(HG):
                        ins = dve.tensor_scalar(dif[:, h, :], csb[:, s % 2, h, :], tok[:, 1, c, HG * g + h:HG * g + h + 1],
                                                 0.0, ALU.subtract, ALU.min)
                    ins.then_inc(*dif_ready.done())

                def heads3(ap):
                    return ap.rearrange("p (h d) -> p h d", d=HD)

                def over_heads(ap):
                    return ap.unsqueeze(2).to_broadcast([P, HG, HD])

                def pre_b(s):
                    g, c = divmod(s, NT)
                    heads = slice(HG * g, HG * g + HG)
                    dve.wait_ge(*xT_filled.at(b, s + 1))
                    dve.wait_ge(*ydiag_filled.at(b, s - 1))
                    dve.wait_ge(*xw_ready.at(b, s - 1))
                    dve.tensor_tensor(heads3(xdt[:, s % 2, :]), heads3(bank_x[:, :]), over_heads(tok[:, 0, c, heads]),
                                      ALU.mult).then_inc(*xdt_ready.done())
                    dve.wait_ge(*y2_ready.at(b, s - 1))
                    dve.tensor_tensor(heads3(xd[:, s % 2, :]), heads3(bank_x[:, :]), over_heads(par("d_skip", HG * g, HG)),
                                      ALU.mult).then_inc(*xd_ready.done())
                    dve.wait_ge(*bc_filled.at(b, s + 1))
                    dve.wait_ge(*new_filled.at(b, s - 1))
                    dve.tensor_copy(bts[:, s % 2, :], bank_s[:, 0:P]).then_inc(*bts_ready.done())
                    dve.wait_ge(*g_ready.at(b, s))
                    dve.tensor_tensor(cbm[:, :], bank_s[:, P:2 * P], causal[:, :], ALU.mult).then_inc(*cbm_ready.done())

                def add_branch(br, m):
                    key = ("br", br, m)
                    dve.wait_ge(*unit_filled.at(b, UNIT[key] + 1))
                    bank = ubank[UNIT[key] % UBANKS][:, :]
                    acc = (acc_s if br < GROUPS else acc_a)[:, m, :]
                    if br in (0, GROUPS):
                        dve.tensor_copy(acc, bank).then_inc(*acc_ready.done())
                    else:
                        dve.wait_ge(*acc_ready.at(b, BRANCH[("br", br - 1, m)] + 1))
                        dve.tensor_tensor(acc, acc, bank, ALU.add).then_inc(*acc_ready.done())

                def filler(g, c, half):
                    for kind, n in fillers(g, c, half):
                        if kind == "br":
                            add_branch(g - 1, n)
                        elif n == 3:
                            dve.wait_ge(*gate_done.at(b, 4 * g))
                            for tt in range(NT):
                                key = ("z", g, tt)
                                gate(key, zbuf[:, tt, :], ubank[UNIT[key] % UBANKS][:, :])

                def g_matrix(s):
                    dve.wait_ge(*e_ready.at(b, s + 1))
                    dve.wait_ge(*cbm_ready.at(b, s + 1))
                    dve.wait_ge(*ydiag_filled.at(b, s))
                    dve.tensor_tensor(gmat[:, :, :], dif[:, :, :], cbm[:, :].unsqueeze(1).to_broadcast([P, HG, P]),
                                      ALU.mult).then_inc(*g_ready.done())

                def finish(g):
                    dve.wait_ge(*gstd_ready.at(b, g + 1))
                    dve.reciprocal(grs[:, :], gstd[:, :]).then_inc(*done_link())
                    after_link()
                    for c in range(NT):
                        dve.tensor_scalar(ybuf[:, c, :], ybuf[:, c, :], grs[:, c:c + 1], None, ALU.mult
                                          ).then_inc(*yn_ready.done())

                def finish_lo(g):
                    for t in range(4):
                        dve.wait_ge(*yhi_ready.at(b, 4 * g + t + 1))
                        dve.scalar_tensor_tensor(ys_lo[:, t, :], sbank[t][:, :], par("norm_w", 4 * g + t),
                                                 ys_hi[:, t, :].bitcast(F32), ALU.mult, ALU.subtract
                                                 ).then_inc(*ylo_ready.done())

                for g in range(GROUPS):
                    for t in range(6):
                        conv_taps(g, t)
                        if t:
                            dve.wait_ge(*conv_done.at(b, 6 * g + t))
                            gate(("x", g, t - 1), conv[:, t - 1, :], conv[:, t - 1, :])
                        if t == 1 and g:
                            finish_lo(g - 1)
                        if g == 0 and t == 3:
                            dve.wait_ge(*unit_filled.at(b, UNIT[("dtT",)] + 1))
                            dve.tensor_copy(tok[:, :, :, :].rearrange("p a b c -> p (a b c)"),
                                            ubank[UNIT[("dtT",)] % UBANKS][:, 0:256]).then_inc(*tok_ready.done())
                    dve.wait_ge(*conv_done.at(b, 6 * g + 6))
                    gate(("x", g, 5), conv[:, 5, :], conv[:, 5, :])
                    if g == 0:
                        dve.wait_ge(*tok_ready.at(b, 1))
                        dve.wait_ge(*ecs_ready.at(b, 1))
                        pre_a(0)
                    pre_b(4 * g)
                    g_matrix(4 * g)
                    pre_a(4 * g + 1)
                    for c in range(NT):
                        s = 4 * g + c
                        heads = slice(HG * g, HG * g + HG)
                        dve.wait_ge(*yoff_filled.at(b, s + 1))
                        if c == 0:
                            dve.wait_ge(*fin_filled.at(b, 4 * g))
                        dve.tensor_tensor(heads3(ybuf[:, c, :]), heads3(bank_o[:, :]), over_heads(ecs[:, c, heads]),
                                          ALU.mult).then_inc(*y1_ready.done())
                        dve.wait_ge(*ydiag_filled.at(b, s + 1))
                        dve.wait_ge(*y1_ready.at(b, s + 1))
                        dve.tensor_tensor(ybuf[:, c, :], ybuf[:, c, :], bank_y[:, :], ALU.add).then_inc(*y_ready.done())
                        if c:
                            filler(g, c - 1, 1)
                        if c < NT - 1:
                            pre_b(s + 1)
                            g_matrix(s + 1)
                            if s + 2 < 16:
                                pre_a(s + 2)
                        dve.wait_ge(*new_filled.at(b, s + 1))
                        dve.wait_ge(*sdec_ready.at(b, s + 1))
                        dve.tensor_tensor(state[:, g, :], state[:, g, :], bank_o[:, :], ALU.add
                                          ).then_inc(*state_ready.done())
                        filler(g, c, 0)
                    filler(g, 3, 1)
                    finish(g)

                def rotate_b(r):
                    dve.wait_ge(*perm_filled.at(b, r + 1))
                    dve.wait_ge(*rot_ready.at(b, r))
                    dve.tensor_tensor(rb[:, :], (bank_y, bank_s)[r % 2][:, :], trg[:, 1, :], ALU.mult).then_inc(*done_link())
                    dve.wait_ge(*ra_ready.at(b, r + 1))
                    after_link()

                dve.tensor_copy(kz[:, :, 0:CH], kz[:, :, T:T + CH]).then_inc(*done_link())
                after_link()
                finish_lo(3)
                dve.wait_ge(*trig_landed.at(b, 2))
                rotate_b(0)
                for kv in range(KV):
                    for half in range(2):
                        src = slice(HD * kv, HD * kv + HD)
                        dst = slice(HD * half, HD * half + HD)
                        ins = dve.tensor_tensor(kz[dst, 2 * kv + half, CH:], ra[src, 0, :], rb[src, :], ALU.add)
                ins.then_inc(*rot_ready.done())
                dve.wait_ge(*vz_ready.at(b, 1))
                for n, bk in enumerate((bank_x, bank_o)):
                    dve.wait_ge(*vT_filled.at(b, n + 1))
                    dst = vw[:, 4 * n:4 * n + 4, HD:5 * HD].rearrange("p c (v d) -> p c v d", d=2 * HD)[:, :, :, 0:HD]
                    dve.tensor_copy(dst, bk[:, :].rearrange("p (c v d) -> p c v d", v=2, d=HD)).then_inc(*vw_ready.done())

                def maxima(a):
                    kv, c = divmod(a, NCH)
                    dve.wait_ge(*score_filled.at(b, a + 1))
                    dve.wait_ge(*p_ready.at(b, a - 1))
                    view = (bank_x, bank_s)[a % 2][:, :].rearrange("p (s k) -> p s k", k=P)
                    if c == 0:
                        m = maskb[:, bass.ds(b, 1), :].to_broadcast([P, 4, CH])
                        dve.tensor_tensor(view[:, :, 0:CH], view[:, :, 0:CH], m, ALU.add).then_inc(*done_link())
                        after_link()
                    dve.tensor_reduce(top[:, a % 2, :], view, AX.X, ALU.max).then_inc(*done_link())
                    after_link()
                    dve.scalar_tensor_tensor(nbias[:, a % 2, :], top[:, a % 2, :], -SCALE, negsink[:, kv, :],
                                             ALU.mult, ALU.min).then_inc(*done_link())
                    after_link()
                    dve.tensor_tensor(nsink[:, a % 2, :], nbias[:, a % 2, :], negsink[:, kv, :], ALU.subtract
                                      ).then_inc(*nb_ready.done())

                def denominators(a):
                    dve.wait_ge(*p_ready.at(b, a + 1))
                    dve.wait_ge(*pn_ready.at(b, a - 1))
                    dve.tensor_tensor(rden[:, a % 2, :], rsum[:, a % 2, :], esink[:, a % 2, :], ALU.add).then_inc(*done_link())
                    after_link()
                    dve.reciprocal(rden[:, a % 2, :], rden[:, a % 2, :]).then_inc(*rec_ready.done())

                def attn_lo(kv):
                    for j in range(4):
                        n = 4 * (4 + kv) + j
                        dve.wait_ge(*yhi_ready.at(b, n + 1))
                        dve.tensor_tensor(ys_lo[:, j, :], zbuf[:, j, :], ys_hi[:, j, :].bitcast(F32), ALU.subtract
                                          ).then_inc(*ylo_ready.done())

                for kv in range(KV):
                    for j in range(4):
                        r = 1 + 4 * kv + j
                        if j == 0 and kv:
                            dve.wait_ge(*score_filled.at(b, 8 * kv))
                        rotate_b(r)
                        dve.tensor_tensor(qbuf[:, :, j, :], ra[:, r % 2, :].rearrange("p (c q) -> p c q", q=CH),
                                          rb[:, :].rearrange("p (c q) -> p c q", q=CH), ALU.add).then_inc(*rot_ready.done())
                    if kv:
                        attn_lo(kv - 1)
                        dve.wait_ge(*ylo_ready.at(b, 4 * (4 + kv)))
                    for j in range(4):
                        key = ("gate", kv, j)
                        gate(key, zbuf[:, j, :], ubank[UNIT[key] % UBANKS][:, :])
                    maxima(8 * kv)
                    maxima(8 * kv + 1)
                    denominators(8 * kv)
                    denominators(8 * kv + 1)
                    for c in range(NCH):
                        a = 8 * kv + c
                        if 0 < c < NCH - 1:
                            maxima(a + 1)
                        add_branch(3 + kv, c)
                        if 0 < c < NCH - 1:
                            denominators(a + 1)
                        dve.wait_ge(*pv_filled.at(b, a + 1))
                        part = zbuf[:, :, CH * c:CH * c + CH]
                        dve.tensor_tensor(part, bank_o[:, 0:256].rearrange("p (j q) -> p j q", q=CH), part, ALU.mult
                                          ).then_inc(*yatt_ready.done())
                attn_lo(1)
                for m in range(KT):
                    dve.wait_ge(*acc_ready.at(b, BRANCH[("br", 3, m)] + 1))
                    gate(("ms", m), acc_s[:, m, :], acc_s[:, m, :])
                for m in range(KT):
                    add_branch(5, m)
                if not last:
                    x_norm(b, 1)

                def mix_lo_part(m):
                    dve.wait_ge(*mixhi_ready.at(b, m + 1))
                    dve.tensor_tensor(mix_lo[:, m, :], acc_s[:, m, :], mix_hi[:, m, :].bitcast(F32), ALU.subtract
                                      ).then_inc(*mixlo_ready.done())

                for m in range(KT):
                    dve.wait_ge(*acc_ready.at(b, BRANCH[("br", 5, m)] + 1))
                    gate(("ma", m), acc_a[:, m, :], acc_a[:, m, :])
                    if m:
                        mix_lo_part(m - 1)
                mix_lo_part(KT - 1)
                if not last:
                    for k in range(4):
                        h_high(b, 1, k)
                dve.wait_ge(*res_landed.at(b, 1))
                for m in range(KT):
                    if m == 0 and not last:
                        for k in range(4, KT):
                            h_high(b, 1, k)
                    dve.wait_ge(*outT_filled.at(b, m + 1))
                    part = res[:, :, P * m:P * m + P]
                    dve.scalar_tensor_tensor(part, part, ALPHA, (bank_x, bank_y)[m % 2][:, :].rearrange(
                        "p (t n) -> p t n", n=P), ALU.mult, ALU.add).then_inc(*res_ready.done())
                    if m % 4 == 3:
                        dve.wait_ge(*res_ready.at(b, m + 1))
                        for tt in range(NT):
                            dve.bn_stats(stats[:, 1, tt, m // 4, :], res[:, tt, 512 * (m // 4):512 * (m // 4) + 512]
                                         ).then_inc(*done_link())
                after_link()
                dve.sem_inc(waited, 1)
                for tt in range(NT):
                    ins = dve.bn_aggr(mv[:, 1, tt, :], stats[:, 1, tt, :, :])
                ins.then_inc(*lvar_ready.done())
                dve.wait_ge(*lvar_ready.at(b, 1))
                for tt in range(NT):
                    dve.scalar_tensor_tensor(res[:, tt, :], res[:, tt, :], mv[:, 1, tt, 0:1], lng[:, :],
                                             ALU.subtract, ALU.mult).then_inc(*done_link())
                dve.wait_ge(*lstd_ready.at(b, 1))
                dve.reciprocal(rstd[:, 1, :], std[:, 1, :]).then_inc(*done_link())
                after_link()
                for tt in range(NT):
                    dve.scalar_tensor_tensor(res[:, tt, :], res[:, tt, :], rstd[:, 1, tt:tt + 1], lnb[:, :],
                                             ALU.mult, ALU.add).then_inc(*out_ready.done())
                assert link[0] == chain.per_block, link[0]

            with dve.Fori(0, NB - 1) as b:
                body(b, False)
            body(NB - 1, True)

        @block.gpsimd
        def _(pool):
            for s in pool_signals:
                pool.sem_inc(s.sem, s.credit)
            pool.sem_inc(out_stored.sem, 16)
            pool.memset(hist[:, :, :], 0.0).then_inc(setup_pool, 1)
            pool.memset(state[:, :, :], 0.0).then_inc(setup_pool, 1)
            pool.memset(vT[:, :], 0.0).then_inc(setup_pool, 1)
            pool.wait_ge(setup_pool, 3)

            def split(b, l):
                ahead, l = divmod(l, NL)
                n = width(l)
                pool.wait_ge(*hi_ready.at(b, l + 1, ahead))
                pool.tensor_tensor(w_lo[:, l % SPLIT, 0:n], w_raw[:, l % RAW, 0:n],
                                   w_hi[:, l % SPLIT, 0:n].bitcast(F32), ALU.subtract).then_inc(*lo_ready.done())

            def h_low(b, ahead, k):
                pool.wait_ge(*hhi_ready.at(b, k + 1, ahead))
                pool.tensor_tensor(h_lo[:, k, :], hf[:, k % 2, :], h_hi[:, k, :].bitcast(F32), ALU.subtract
                                   ).then_inc(*hlo_ready.done())

            split(0, 0)
            split(0, 1)
            for k in range(KT):
                h_low(0, 0, k)

            def body(b, last):
                def next_split(key):
                    if LOAD[key] + SPLIT < NL or not last:
                        split(b, LOAD[key] + SPLIT)

                next_split(("dt", 0))
                next_split(("dt", 1))

                def heads3(ap):
                    return ap.rearrange("p (h d) -> p h d", d=HD)

                def over_heads(ap):
                    return ap.unsqueeze(2).to_broadcast([P, HG, HD])

                def weigh(s):
                    pool.wait_ge(*xdt_ready.at(b, s + 1))
                    pool.wait_ge(*decays_ready.at(b, s + 1))
                    pool.wait_ge(*new_filled.at(b, s))
                    pool.tensor_tensor(heads3(xw[:, :]), heads3(xdt[:, s % 2, :]), over_heads(ends[:, s % 4, 0:HG]),
                                       ALU.mult).then_inc(*xw_ready.done())

                def gate(s):
                    g, c = divmod(s, NT)
                    pool.wait_ge(*y2_ready.at(b, s + 1))
                    pool.wait_ge(*gated.at(b, GATED[("z", g, c)] + 1))
                    pool.tensor_tensor(ybuf[:, c, :], ybuf[:, c, :], zbuf[:, c, :], ALU.mult).then_inc(*gate_done.done())

                def filler(g, c, half):
                    for kind, n in fillers(g, c, half):
                        if kind == "z":
                            next_split(("z", g, n))
                        elif n % 2:
                            next_split(("br", g - 1, n // 2))

                for g in range(GROUPS):
                    for t in range(6):
                        next_split(("x", g, t))
                    next_split(("z", g, 0))
                    for c in range(NT):
                        s = 4 * g + c
                        weigh(s)
                        pool.wait_ge(*yoff_filled.at(b, s + 1))
                        pool.wait_ge(*state_ready.at(b, s))
                        pool.tensor_tensor(heads3(state[:, g, :]), heads3(state[:, g, :]), over_heads(ends[:, s % 4, HG:]),
                                           ALU.mult).then_inc(*sdec_ready.done())
                        pool.wait_ge(*y_ready.at(b, s + 1))
                        pool.wait_ge(*xd_ready.at(b, s + 1))
                        pool.tensor_tensor(ybuf[:, c, :], ybuf[:, c, :], xd[:, s % 2, :], ALU.add).then_inc(*y2_ready.done())
                        filler(g, c, 0)
                        filler(g, c, 1)
                        if c == z_step(g):
                            for n in range(c):
                                gate(4 * g + n)
                        if c >= z_step(g):
                            gate(s)

                def rotate_a(r):
                    pool.wait_ge(*rf_ready.at(b, r + 1))
                    pool.wait_ge(*rot_ready.at(b, r - 1))
                    if r == 0:
                        pool.wait_ge(*trig_landed.at(b, 2))
                    pool.tensor_tensor(ra[:, r % 2, :], rf[:, r % 2, :], trg[:, 0, :], ALU.mult).then_inc(*ra_ready.done())

                next_split(("k",))
                rotate_a(0)
                pool.memset(vw[:, :, :], 0.0).then_inc(*vz_ready.done())
                next_split(("v",))

                def normalise(a):
                    pool.wait_ge(*rec_ready.at(b, a + 1))
                    pool.tensor_tensor(pbuf[:, a % 2, :, :], pbuf[:, a % 2, :, :],
                                       rden[:, a % 2, :].unsqueeze(2).to_broadcast([P, 4, P]), ALU.mult
                                       ).then_inc(*pn_ready.done())

                for kv in range(KV):
                    for j in range(4):
                        next_split(("q", kv, j))
                        rotate_a(1 + 4 * kv + j)
                    for j in range(4):
                        next_split(("gate", kv, j))
                    normalise(8 * kv)
                    normalise(8 * kv + 1)
                    for c in range(NCH):
                        if c % 2:
                            next_split(("br", 3 + kv, c // 2))
                        if c < NCH - 2:
                            normalise(8 * kv + c + 2)
                for m in range(KT):
                    next_split(("ms", m))
                for i in range(4):
                    next_split(("br", 5, i))
                for m in range(KT):
                    next_split(("ma", m))
                    pool.wait_ge(*gated.at(b, GATED[("ma", m)] + 1))
                    pool.tensor_tensor(acc_s[:, m, :], acc_s[:, m, :], acc_a[:, m, :], ALU.add).then_inc(*mixf_ready.done())
                if not last:
                    for k in range(4):
                        h_low(b, 1, k)
                for m in range(KT):
                    next_split(("out", m))
                    if m == 0 and not last:
                        for k in range(4, KT):
                            h_low(b, 1, k)

            with pool.Fori(0, NB - 1) as b:
                body(b, False)
            body(NB - 1, True)

        for s in pe_signals + act_signals + dve_signals + pool_signals:
            assert s.seen == 2 * s.per_block, (s.sem, s.seen, s.per_block)


def kernel(x, c, w_ada, b_ada, w_in, b_qkv, b_merge, attn_sinks, conv_w, conv_b, dt_bias, a_log,
           d_skip, ssd_norm_w, w_branch_attn, w_branch_ssd, w_out, ln_g, ln_b):
    import numpy as np
    import concourse.bacc as bacc
    from concourse.bass_utils import run_bass_kernel_spmd

    f = np.float32

    def tiles(v):
        return np.ascontiguousarray(v).reshape(-1, P).T

    prm = np.zeros((P, NPARAM), f)

    def put(name, v):
        at, n = PARAMS[name]
        prm[:v.shape[0], at:at + n] = v

    c, b_ada, b_qkv, b_merge, attn_sinks, conv_w, conv_b, dt_bias, a_log, d_skip, ssd_norm_w = (
        np.asarray(v) for v in (c, b_ada, b_qkv, b_merge, attn_sinks, conv_w, conv_b, dt_bias, a_log, d_skip, ssd_norm_w))
    put("c", tiles(c[0]))
    put("b_ada", tiles(b_ada[0]))
    put("b_q", tiles(b_qkv[0, :1024]))
    put("b_k", tiles(b_qkv[0, 1024:1152]))
    put("b_v", tiles(b_qkv[0, 1152:]))
    put("b_merge", tiles(b_merge[0]))
    put("conv_w", conv_w[0].reshape(4, CONVT, P).transpose(2, 1, 0).reshape(P, CONVT * 4))
    put("conv_b", tiles(conv_b[0]))
    put("norm_w", tiles(ssd_norm_w[0]))
    put("dt_bias", dt_bias[0][:, None])
    put("a_log", a_log[0][:, None])
    sink = attn_sinks[0].reshape(KV, 2, 2, 2)
    put("sink", np.repeat(sink.transpose(2, 0, 3, 1).reshape(2, 8), 64, axis=0))
    put("d_skip", np.broadcast_to(d_skip[0], (P, 32)))

    consts = np.zeros((3, P, P), f)
    consts[0] = np.eye(P)
    consts[1] = np.triu(np.ones((P, P)))
    for p in range(P):
        if p % HD < 16:
            consts[2, p + 8 if p % HD < 8 else p - 8, p] = 1.0
    half = 8
    inv = np.power(f(500000.0), -np.arange(half, dtype=f) / f(half)).astype(f)
    ang = (np.arange(SEQ, dtype=f)[:, None] * inv[None, :]).astype(f)
    trig = np.zeros((2, P, SEQ), f)
    trig[0] = 1.0
    for p in range(P):
        d = p % HD
        if d < 16:
            trig[0, p] = np.cos(ang[:, d % 8])
            trig[1, p] = np.sin(ang[:, d % 8]) * (-1.0 if d < 8 else 1.0)
    kmask = np.zeros((P, NB, CH), f)
    kmask[:, 0, :] = -1e30

    arrays = {"x": x, "params": prm, "w_ada": w_ada, "w_in": w_in, "w_br_attn": w_branch_attn,
              "w_br_ssd": w_branch_ssd, "w_out": w_out, "ln_g": np.asarray(ln_g)[0], "ln_b": np.asarray(ln_b)[0],
              "consts": consts, "trig": trig, "kmask": kmask}
    arrays = {n: np.ascontiguousarray(a) for n, a in arrays.items()}
    nc = bacc.Bacc("TRN2", target_bir_lowering=False, num_devices=1)
    args = [nc.dram_tensor(n, a.shape, mybir.dt.from_np(a.dtype), kind="ExternalInput").ap() for n, a in arrays.items()]
    args.append(nc.dram_tensor("out", (1, SEQ, D), F32, kind="ExternalOutput").ap())
    program(nc, *args)
    r = run_bass_kernel_spmd(nc, [arrays], core_ids=[0])
    return r.results[0]["out"]
```

```python
from contextlib import ExitStack

import concourse.bass as bass
from concourse import mybir

ALU = mybir.AluOpType
ACT = mybir.ActivationFunctionType
AX = mybir.AxisListType
F32 = mybir.dt.float32
F32R = mybir.dt.float32r

P = 128
D = 1024
SEQ = 2048
T = 512
NB = SEQ // T
NT = T // P
KT = D // P
CH = 64
NCH = T // CH
HD = 64
KV = 2
GROUPS = 4
HG = 8
CONVT = 24
COL_Q, COL_K, COL_V, COL_GATE = 0, 1024, 1152, 1280
COL_Z, COL_XBC, COL_DT, COL_MERGE = 2304, 4352, 7424, 7456
ALPHA = 2.0 ** 0.25
EPS = 1e-5
SCALE = HD ** -0.5

PARAMS = {}
_at = 0
for _name, _n in (("c", KT), ("b_ada", 24), ("b_q", 8), ("b_k", 1), ("b_v", 1), ("b_merge", 16),
                  ("conv_w", 4 * CONVT), ("conv_b", CONVT), ("norm_w", 16), ("dt_bias", 1), ("a_log", 1),
                  ("sink", 8), ("d_skip", 32)):
    PARAMS[_name] = (_at, _n)
    _at += _n
NPARAM = _at


def plan_units():
    units, loads = [], []

    def unit(*key):
        units.append(key)

    def branch(br):
        for m in range(KT):
            unit("br", br, m)
        loads.extend(("br", br, i) for i in range(4))

    for g in range(GROUPS):
        for t in range(6):
            unit("x", g, t)
            loads.append(("x", g, t))
            if g == 0 and t == 0:
                unit("dt")
                loads.extend([("dt", 0), ("dt", 1)])
            if g == 0 and t == 3:
                unit("dtT")
        for tt in range(NT):
            unit("z", g, tt)
        loads.extend(("z", g, i) for i in range(4))
        if g:
            branch(g - 1)
    for key in (("k",), ("v",)):
        unit(*key)
        loads.append(key)
    for kv in range(KV):
        for kind in ("q", "gate"):
            for j in range(4):
                unit(kind, kv, j)
                loads.append((kind, kv, j))
        branch(3 + kv)
    for m in range(KT):
        unit("ms", m)
        loads.append(("ms", m))
    branch(5)
    for kind in ("ma", "out"):
        for m in range(KT):
            unit(kind, m)
            loads.append((kind, m))
    return units, loads


UNITS, LOADS = plan_units()


def fillers(g, c):
    if g == 0:
        return [("z", c + 1)] if c < 3 else []
    return [[("z", n) for n in (2, 3)], [("br", m) for m in (0, 1)], [("br", m) for m in (2, 3, 4)],
            [("br", m) for m in (5, 6, 7)]][c]


def z_before(g):
    return 2 if g else 1


def z_step(g):
    return 0 if g else 3


def conv_tile(g, t):
    return (16 + g, 20 + g)[t] if t < 2 else 4 * g + t - 2


UNIT = {key: n for n, key in enumerate(UNITS)}
LOAD = {key: n for n, key in enumerate(LOADS)}
NU, NL = len(UNITS), len(LOADS)
NH = GROUPS * HG
DT_TILES = (2, 6)
RAW, SPLIT, UBANKS = 3, 2, 4
H_BANK = (0, 1, 2, 3, 1, 3, 1, 3)
EARLY = RAW + 4
assert NU % UBANKS == 0 and NL % (RAW * SPLIT) == 0
GATED = {key: n for n, key in enumerate(k for k in UNITS if k[0] in ("x", "z", "gate", "ms", "ma"))}
BRANCH = {key: n for n, key in enumerate(k for k in UNITS if k[0] == "br")}
PARTS = {key: n for n, key in enumerate(
    [("dt", 0)] + [("z", g, i) for g in range(GROUPS) for i in range(3)])}


def program(nc, x, params, w_ada, w_in, w_br_attn, w_br_ssd, w_out, ln_g, ln_b, consts, trig, kmask, out):
    ctx = ExitStack()
    with ctx:
        base = [(nc.sbuf_base + 63) // 64 * 64]

        def place(name, shape, dt=F32, at=None):
            size = 4
            for n in shape[1:]:
                size *= n
            if at is None:
                at = base[0]
                base[0] += (size + 31) // 32 * 32
            return nc.alloc_sbuf_tensor_at(name, list(shape), dt, offset=at)

        class Signal:

            def __init__(self, name, per_block, credit=1):
                self.sem = ctx.enter_context(nc.semaphore(name))
                self.per_block, self.credit, self.seen = per_block, credit, 0

            def at(self, b, n, ahead=0):
                n += ahead * self.per_block
                assert n + self.credit >= 1, (self.sem, n)
                return self.sem, b * self.per_block + (n + self.credit)

            def done(self):
                self.seen += 1
                return self.sem, 1

        class Landed:

            def __init__(self, name, per_block, before=0):
                self.sem = ctx.enter_context(nc.semaphore(name))
                self.per_block, self.before = per_block, before

            def at(self, b, n, ahead=0):
                return self.sem, b * (16 * self.per_block) + 16 * (n + ahead * self.per_block + self.before)

            def done(self):
                return self.sem, 16

        o_h = base[0]
        h_hi = place("h_hi", [P, KT, T], F32R)
        h_lo = place("h_lo", [P, KT, T], F32R)
        acc_s = place("acc_s", [P, KT, T])
        o_acc_a = base[0]
        acc_a = place("acc_a", [P, KT, T])
        res = place("res", [P, NT, D], at=o_acc_a)
        w_raw = place("w_raw", [P, RAW, KT * P])
        w_hi = place("w_hi", [P, SPLIT, KT * P], F32R)
        w_lo = place("w_lo", [P, SPLIT, KT * P], F32R)
        o_xz = base[0]
        conv = place("conv", [P, 6, T])
        zbuf = place("zbuf", [P, NT, T])
        xn = place("xn", [P, NT, D], at=o_xz)
        gate_part = place("gate_part", [P, 2, T], at=o_xz + 4 * NT * D)
        o_ys = base[0]
        ys_hi = place("ys_hi", [P, 4, T], F32R)
        ys_lo = place("ys_lo", [P, 4, T], F32R)
        kz = place("kz", [P, 4, CH + T])
        state = place("state", [P, GROUPS, HG * HD])
        vT = place("vT", [P, CH + T])
        th = place("th", [P, 2, T])
        ident = place("ident", [P, P])
        causal = place("causal", [P, P])
        partner = place("partner", [P, P], F32R)
        lng = place("lng", [P, D])
        lnb = place("lnb", [P, D])
        maskb = place("maskb", [P, NB, CH])
        prm = place("prm", [P, NPARAM])
        ada = place("ada", [P, 24])
        aneg = place("aneg", [P, 1])
        eps = place("eps", [P, 1])
        one = place("one", [P, 1])
        silu_c = place("silu_c", [P, KT])
        negsink = place("negsink", [P, KV, 4])
        hist = place("hist", [P, CONVT, 3])
        tok = place("tok", [P, 2, NT, NH])
        ecs = place("ecs", [P, NT, NH])
        stats = place("stats", [P, 2, NT, 2, 6])
        mv = place("mv", [P, 2, NT, 2])
        std = place("std", [P, 2, NT])
        rstd = place("rstd", [P, 2, NT])
        ss = place("ss", [P, NT])
        gstd = place("gstd", [P, NT])
        grs = place("grs", [P, NT])
        ends = place("ends", [P, 4, 2 * HG])
        top = place("top", [P, 2, 4])
        nbias = place("nbias", [P, 2, 4])
        nsink = place("nsink", [P, 2, 4])
        rsum = place("rsum", [P, 2, 4])
        esink = place("esink", [P, 2, 4])
        rden = place("rden", [P, 2, 4])
        o_r = base[0]
        K = 1024
        gmat = place("gmat", [P, HG, P], at=o_r)
        dif = place("dif", [P, HG, P], at=o_r + 4 * K)
        xdt = place("xdt", [P, 2, HG * HD], at=o_r + 8 * K)
        xd = place("xd", [P, 2, HG * HD], at=o_r + 12 * K)
        xw = place("xw", [P, HG * HD], at=o_r + 16 * K)
        bts = place("bts", [P, 2, P], at=o_r + 18 * K)
        cbm = place("cbm", [P, P], at=o_r + 19 * K)
        csb = place("csb", [P, 2, HG, P], at=o_r + 20 * K)
        u = place("u", [P, 2, T + 4], at=o_r + 28 * K)
        junk = place("junk", [P, T], at=o_r + 28 * K + 8 * (T + 4))
        o_y = o_r + 28 * K + 8 * (T + 4) + 4 * T
        ybuf = place("ybuf", [P, NT, HG * HD], at=o_y)
        dtmp = place("dtmp", [NH, 3, T], at=o_y)
        rf = place("rf", [P, 2, T], at=o_r)
        ra = place("ra", [P, 2, T], at=o_r + 4 * K)
        rb = place("rb", [P, T], at=o_r + 8 * K)
        rf_hi = place("rf_hi", [P, T], F32R, at=o_r + 10 * K)
        rf_lo = place("rf_lo", [P, T], F32R, at=o_r + 12 * K)
        pbuf = place("pbuf", [P, 2, 4, P], at=o_r + 10 * K)
        ptb_hi = place("ptb_hi", [P, 2, 4, P], F32R, at=o_r + 14 * K)
        ptb_lo = place("ptb_lo", [P, 4, P], F32R, at=o_r + 18 * K)
        trg = place("trg", [P, 2, T], at=o_r + 20 * K)
        vw_hi = place("vw_hi", [P, NCH, 5 * HD], F32R, at=o_r + 24 * K)
        vw_lo = place("vw_lo", [P, NCH, 5 * HD], F32R, at=o_xz)
        qbuf = place("qbuf", [P, NCH, 4, CH], at=o_y)
        mix_hi = place("mix_hi", [P, KT, T], F32R, at=o_r)
        mix_lo = place("mix_lo", [P, KT, T], F32R, at=o_r + 16 * K)
        og = place("og", [P, 2, T], at=o_r + 32 * K)
        hf = place("hf", [P, 2, T], at=o_r + 36 * K)
        ada_w = [place(f"ada_w{n}", [P, KT, T], at=a) for n, a in enumerate(
            [o_h, o_h + 16 * K, o_ys, o_r, o_h + 32 * K, o_acc_a])]
        end = o_y + 8 * K
        assert end <= nc.sbuf_usable_end, (end, nc.sbuf_usable_end)

        ubank = [ctx.enter_context(nc.psum_tensor(f"ubank{n}", [P, T], F32)) for n in range(UBANKS)]
        bank_x, bank_s, bank_y, bank_o = sbank = [
            ctx.enter_context(nc.psum_tensor(f"bank_{n}", [P, T], F32)) for n in "xsyo"]
        cs_dram = nc.dram_tensor("cs_dram", [NB, NH, T], F32, kind="Internal").ap()

        def par(name, n=None, m=None):
            at, size = PARAMS[name]
            if n is None:
                return prm[:, at:at + size]
            return prm[:, at + n:at + n + (m or 1)]

        sem = lambda name: ctx.enter_context(nc.semaphore(name))
        prm_landed, const_landed, late_landed = sem("prm_landed"), sem("const_landed"), sem("late_landed")
        setup_dve2, waited = sem("setup_dve2"), sem("waited")
        ada_sum, ada_chain = sem("ada_sum"), sem("ada_chain")
        ada_landed = [sem(f"ada_landed{n}") for n in range(len(ada_w))]
        setup_dve, setup_act, setup_pool, ada_filled = (sem(n) for n in ("setup_dve", "setup_act", "setup_pool", "ada_filled"))
        unit_filled = Signal("unit_filled", NU, 2)
        part_used = Signal("part_used", len(PARTS), 2)
        ht_filled = Signal("ht_filled", KT)
        xT_filled, bc_filled, yoff_filled, ydiag_filled, new_filled, fin_filled = (
            Signal(n, 16, 2) for n in ("xT_filled", "bc_filled", "yoff_filled", "ydiag_filled", "new_filled", "fin_filled"))
        perm_filled = Signal("perm_filled", 9, 2)
        vT_filled = Signal("vT_filled", 2)
        score_filled, pT_filled, pv_filled = (Signal(n, 16, 2) for n in ("score_filled", "pT_filled", "pv_filled"))
        outT_filled = Signal("outT_filled", KT, 2)
        pe_signals = [unit_filled, part_used, ht_filled, xT_filled, bc_filled, yoff_filled, ydiag_filled,
                      new_filled, fin_filled, perm_filled, vT_filled, score_filled, pT_filled, pv_filled, outT_filled]
        hi_ready = Signal("hi_ready", NL)
        hf_ready = Signal("hf_ready", KT)
        hstd_ready, lstd_ready = Signal("hstd_ready", 1), Signal("lstd_ready", 1)
        dt_parts = Signal("dt_parts", 1)
        ecs_ready = Signal("ecs_ready", 1)
        u_ready, tap_ready = Signal("u_ready", CONVT), Signal("tap_ready", CONVT)
        th_ready = Signal("th_ready", len(GATED), 2)
        decays_ready, e_ready, sq_ready = (Signal(n, 16, 2) for n in ("decays_ready", "e_ready", "sq_ready"))
        gstd_ready = Signal("gstd_ready", GROUPS)
        yhi_ready = Signal("yhi_ready", 24)
        rf_ready, rfhi_ready = Signal("rf_ready", 9), Signal("rfhi_ready", 9)
        v_ready = Signal("v_ready", 1)
        p_ready, pt_ready = Signal("p_ready", 16, 2), Signal("pt_ready", 16, 2)
        mixhi_ready = Signal("mixhi_ready", KT)
        og_ready = Signal("og_ready", KT, 4)
        act_chain = Signal("act_chain", 4)
        act_signals = [hi_ready, hf_ready, hstd_ready, lstd_ready, dt_parts, ecs_ready, u_ready, tap_ready,
                       th_ready, decays_ready, e_ready, sq_ready, gstd_ready, yhi_ready, rf_ready, rfhi_ready,
                       v_ready, p_ready, pt_ready, mixhi_ready, og_ready, act_chain]
        hvar_ready, lvar_ready, x_chain = Signal("hvar_ready", 1), Signal("lvar_ready", 1), Signal("x_chain", 9)
        xn_ready = Signal("xn_ready", NT)
        hhi_ready = Signal("hhi_ready", KT, 2)
        dt_ready, cs_ready, tok_ready = Signal("dt_ready", 1), Signal("cs_ready", 1), Signal("tok_ready", 1)
        conv_done = Signal("conv_done", CONVT, 2)
        hist_in, hist_out = Signal("hist_in", CONVT, 2), Signal("hist_out", CONVT, 2)
        gated = Signal("gated", len(GATED), 2)
        dif_ready, ends_ready = Signal("dif_ready", 16, 2), Signal("ends_ready", 16, 2)
        xdt_ready, xd_ready, bts_ready, cbm_ready = (
            Signal(n, 16, 2) for n in ("xdt_ready", "xd_ready", "bts_ready", "cbm_ready"))
        g_ready, y1_ready, y_ready, state_ready = (
            Signal(n, 16, 2) for n in ("g_ready", "y1_ready", "y_ready", "state_ready"))
        yn_ready = Signal("yn_ready", 16)
        ylo_ready = Signal("ylo_ready", 24)
        acc_ready = Signal("acc_ready", len(BRANCH), 1)
        rflo_ready, rot_ready = Signal("rflo_ready", 9), Signal("rot_ready", 9, 2)
        vw_ready = Signal("vw_ready", 4)
        nb_ready, rec_ready, pn_ready, ptlo_ready, yatt_ready = (
            Signal(n, 16, 2) for n in ("nb_ready", "rec_ready", "pn_ready", "ptlo_ready", "yatt_ready"))
        mixlo_ready = Signal("mixlo_ready", KT)
        res_ready = Signal("res_ready", KT, 2)
        out_ready = Signal("out_ready", NT)
        dve_chain = Signal("dve_chain", 126)
        dve_signals = [hvar_ready, lvar_ready, x_chain, xn_ready, hhi_ready, dt_ready, cs_ready, tok_ready,
                       conv_done, hist_in, hist_out, gated, dif_ready, ends_ready, xdt_ready, xd_ready,
                       bts_ready, cbm_ready, g_ready, y1_ready, y_ready, state_ready, yn_ready, ylo_ready,
                       acc_ready, rflo_ready, rot_ready, vw_ready, nb_ready, rec_ready, pn_ready, ptlo_ready,
                       yatt_ready, mixlo_ready, res_ready, out_ready, dve_chain]
        lo_ready = Signal("lo_ready", NL, 3)
        hlo_ready = Signal("hlo_ready", KT, 2)
        xw_ready, sdec_ready, y2_ready, gate_done = (
            Signal(n, 16, 4) for n in ("xw_ready", "sdec_ready", "y2_ready", "gate_done"))
        ra_ready = Signal("ra_ready", 9, 2)
        vz_ready = Signal("vz_ready", 2)
        mixf_ready = Signal("mixf_ready", KT)
        pool_signals = [lo_ready, hlo_ready, xw_ready, sdec_ready, y2_ready, gate_done, ra_ready,
                        vz_ready, mixf_ready]
        w_landed = [Landed(f"w_landed{n}", NL // RAW) for n in range(RAW)]
        x_landed, res_landed = Landed("x_landed", 1), Landed("res_landed", 1)
        cs_stored = Landed("cs_stored", 1)
        csb_landed = [Landed(f"csb_landed{n}", 8) for n in range(2)]
        trig_landed = Landed("trig_landed", 2)
        out_stored = Landed("out_stored", NT, 1)

        def release(l):
            if l < 0:
                n = UNIT[LOADS[NL + l]] + 1 - NU
                return unit_filled, n
            key = LOADS[l]
            if key in PARTS:
                return part_used, PARTS[key] + 1
            if key[0] == "dt":
                return unit_filled, UNIT[("dt",)] + 1
            if key[0] == "z":
                return unit_filled, UNIT[("z", key[1], 3)] + 1
            if key[0] == "br":
                return unit_filled, UNIT[("br", key[1], 2 * key[2] + 1)] + 1
            return unit_filled, UNIT[key] + 1

        def drained(n):
            if n < 0:
                return og_ready, UNITS[NU + n][1] + 1 - KT
            key = UNITS[n]
            kind = key[0]
            if kind == "dt":
                return dt_parts, 1
            if kind == "dtT":
                return tok_ready, 1
            if kind == "x":
                return u_ready, key[1] * 6 + key[2] + 1
            if kind in ("z", "gate"):
                return gated, GATED[key] + 1
            if kind in ("ms", "ma"):
                return th_ready, GATED[key] + 1
            if kind == "k":
                return rf_ready, 1
            if kind == "q":
                return rf_ready, 2 + 4 * key[1] + key[2]
            if kind == "v":
                return v_ready, 1
            if kind == "br":
                return acc_ready, BRANCH[key] + 1
            return og_ready, key[1] + 1

        block = ctx.enter_context(nc.Block())
        w_in_t = w_in[0].rearrange("(k p) n -> p k n", p=P)
        w_ada_t = w_ada[0].rearrange("(k p) n -> p k n", p=P)
        w_out_t = w_out[0].rearrange("(k p) n -> p k n", p=P)
        w_bra_t = w_br_attn[0].rearrange("(k p) n -> p k n", p=P)
        w_brs_t = w_br_ssd[0].rearrange("(k p) n -> p k n", p=P)

        def raw_view(l):
            key = LOADS[l]
            kind = key[0]
            slot = w_raw[:, l % RAW, :]
            if kind == "dt":
                n, k0 = DT_TILES[key[1]], key[1] * DT_TILES[0]
                return slot[:, 0:NH * n].rearrange("p (k n) -> p k n", n=NH), w_in_t[:, k0:k0 + n, COL_DT:COL_DT + NH]
            if kind == "z":
                c = COL_Z + 512 * key[1]
                return slot.rearrange("p (k n) -> p k n", n=512), w_in_t[:, 2 * key[2]:2 * key[2] + 2, c:c + 512]
            if kind == "br":
                br, i = key[1], key[2]
                src = w_brs_t[:, 4 * br:4 * br + 4] if br < GROUPS else w_bra_t[:, 4 * (br - GROUPS):4 * (br - GROUPS) + 4]
                return slot.rearrange("p (k n) -> p k n", n=256), src[:, :, 256 * i:256 * i + 256]
            slot = slot.rearrange("p (k n) -> p k n", n=P)
            if kind == "out":
                return slot, w_out_t[:, :, P * key[1]:P * key[1] + P]
            c = {"x": lambda: COL_XBC + P * conv_tile(*key[1:]),
                 "k": lambda: COL_K, "v": lambda: COL_V,
                 "q": lambda: COL_Q + P * (4 * key[1] + key[2]), "gate": lambda: COL_GATE + P * (4 * key[1] + key[2]),
                 "ma": lambda: COL_MERGE + P * key[1], "ms": lambda: COL_MERGE + D + P * key[1]}[kind]()
            return slot, w_in_t[:, :, c:c + P]

        def width(l):
            return NH * DT_TILES[LOADS[l][1]] if LOADS[l][0] == "dt" else KT * P

        @block.sync
        def _(sp):
            def load_x(dst, row, signal):
                sp.dma_start(dst[:, :, :], x[0, bass.ds(row, T), :].rearrange("(t p) d -> p t d", p=P)).then_inc(*signal.done())

            sp.dma_start(prm[:, :], params).then_inc(prm_landed, 16)
            load_x(xn, 0, x_landed)
            for n, t in enumerate((ident, causal)):
                sp.dma_start(t[:, :], consts[n]).then_inc(const_landed, 16)
            sp.dma_start(junk[:, 0:P], consts[2]).then_inc(const_landed, 16)

            def load_ada(n):
                sp.dma_start(ada_w[n][:, :, :], w_ada_t[:, :, T * n:T * n + T]).then_inc(ada_landed[n], 16)

            for n in range(4):
                load_ada(n)

            def load(b, l, ahead):
                slot, src = raw_view(l)
                sp.wait_ge(*lo_ready.at(b, l - RAW + 1, ahead))
                sp.dma_start(slot, src).then_inc(*w_landed[l % RAW].done())

            for l in range(RAW + 2):
                load(0, l, 0)
            for n in (4, 5):
                load_ada(n)
            for l in range(RAW + 2, EARLY):
                load(0, l, 0)
            sp.dma_start(maskb[:, :, :], kmask).then_inc(late_landed, 16)
            sp.dma_start(lng[:, :], ln_g.partition_broadcast(P)).then_inc(late_landed, 16)
            sp.dma_start(lnb[:, :], ln_b.partition_broadcast(P)).then_inc(late_landed, 16)

            def body(b, last):
                snap = (lambda v: v) if type(b) is int else sp.snap
                for l in range(EARLY, NL):
                    if LOADS[l] == ("ms", 5) and not last:
                        row = snap(b * T + T)
                        sp.wait_ge(*ylo_ready.at(b, 24))
                        load_x(xn, row, x_landed)
                    if LOADS[l] == ("out", 4):
                        row = snap(b * T)
                        sp.wait_ge(*mixf_ready.at(b, KT))
                        load_x(res, row, res_landed)
                    load(b, l, 0)
                if not last:
                    for l in range(EARLY):
                        load(b, l, 1)
                for tt in range(NT):
                    row = snap(b * T + tt * P)
                    sp.wait_ge(*out_ready.at(b, tt + 1))
                    sp.dma_start(out[0, bass.ds(row, P), :], res[:, tt, :]).then_inc(*out_stored.done())

            body(0, False)
            with sp.Fori(1, NB - 1) as b:
                body(b, False)
            body(NB - 1, True)
            sp.wait_ge(out_stored.sem, 16 * (NT * NB + 1))

        @block.tensor
        def _(pe):
            def turn_h(b, ahead, k):
                for j in range(k):
                    if H_BANK[j] == H_BANK[k]:
                        pe.wait_ge(*hf_ready.at(b, j + 1, ahead))
                for tt in range(NT):
                    mm = pe.transpose(sbank[H_BANK[k]][:, P * tt:P * tt + P], xn[:, tt, P * k:P * k + P], ident[:, :])
                mm.then_inc(*ht_filled.done())

            for s in pe_signals:
                pe.sem_inc(s.sem, s.credit)
            def ada_sums(n, bank, partial):
                pe.wait_ge(ada_sum, n)
                for t in range(4):
                    mm = pe.matmul(bank[:, 4 * n + t:4 * n + t + 1], partial[:, P * t:P * t + P], one[:, :],
                                   start=True, stop=True)
                mm.then_inc(ada_filled, 1)

            pe.wait_ge(setup_dve, 1)
            pe.wait_ge(ada_landed[0], 16)
            for t in range(4):
                for k in range(KT):
                    pe.matmul(ubank[3][:, t:t + 1], ada_w[0][:, k, P * t:P * t + P], silu_c[:, k:k + 1],
                              start=(k == 0), stop=(k == KT - 1))
            pe.wait_ge(const_landed, 48)
            pe.wait_ge(*xn_ready.at(0, NT))
            for k in range(4):
                turn_h(0, 0, k)
            for n in (1, 2, 3):
                ada_sums(n, ubank[3], th[:, n % 2, :])
            for k in range(4, KT):
                turn_h(0, 0, k)

            def body(b, last):
                def three(out_ap, a_hi, a_lo, m_hi, m_lo, first, last):
                    pe.matmul(out_ap, a_hi, m_hi, start=first, stop=False)
                    pe.matmul(out_ap, a_hi, m_lo, start=False, stop=False)
                    return pe.matmul(out_ap, a_lo, m_hi, start=False, stop=last)

                def bank_for(key):
                    n = UNIT[key]
                    s, at = drained(n - UBANKS)
                    pe.wait_ge(*s.at(b, at))
                    if n == 3:
                        pe.wait_ge(setup_dve, 8)
                    return ubank[n % UBANKS][:, :]

                def split_slot(l, n):
                    pe.wait_ge(*lo_ready.at(b, l + 1))
                    view = lambda w: w[:, l % SPLIT, :].rearrange("p (k n) -> p k n", n=n)
                    return view(w_hi), view(w_lo)

                def project(key, m_hi=h_hi, m_lo=h_lo):
                    bank = bank_for(key)
                    hi, lo = split_slot(LOAD[key], P)
                    for k in range(KT):
                        if key == UNITS[0]:
                            pe.wait_ge(*hlo_ready.at(b, k + 1))
                        if key == ("out", 0):
                            pe.wait_ge(*mixlo_ready.at(b, k + 1))
                        mm = three(bank, hi[:, k, :], lo[:, k, :], m_hi[:, k, :], m_lo[:, k, :], k == 0, k == KT - 1)
                    mm.then_inc(*unit_filled.done())

                def z_part(g, i):
                    banks = [ubank[UNIT[("z", g, tt)] % UBANKS][:, :] for tt in range(NT)]
                    hi, lo = split_slot(LOAD[("z", g, i)], 512)
                    for j in range(2):
                        k = 2 * i + j
                        for tt in range(NT):
                            if k == 0:
                                bank_for(("z", g, tt))
                            tk = slice(P * tt, P * tt + P)
                            pe.matmul(banks[tt], h_hi[:, k, tk], hi[:, j, :], start=(k == 0), stop=False)
                            pe.matmul(banks[tt], h_hi[:, k, tk], lo[:, j, :], start=False, stop=False)
                            mm = pe.matmul(banks[tt], h_lo[:, k, tk], hi[:, j, :], start=False, stop=(k == KT - 1))
                            if k == KT - 1:
                                mm.then_inc(*unit_filled.done())
                    if i < 3:
                        mm.then_inc(*part_used.done())

                def branch(br, m, first=0, end=4):
                    bank = bank_for(("br", br, m)) if first == 0 else ubank[UNIT[("br", br, m)] % UBANKS][:, :]
                    hi, lo = split_slot(LOAD[("br", br, m // 2)], 256)
                    if m == 0:
                        pe.wait_ge(*ylo_ready.at(b, 4 * br + 4))
                    cols = slice(P * (m % 2), P * (m % 2) + P)
                    for k in range(first, end):
                        mm = three(bank, hi[:, k, cols], lo[:, k, cols], ys_hi[:, k, :], ys_lo[:, k, :], k == 0, k == 3)
                    if end == 4:
                        mm.then_inc(*unit_filled.done())

                def project_dt():
                    bank = bank_for(("dt",))[0:NH, :]
                    for i, n in enumerate(DT_TILES):
                        hi, lo = split_slot(LOAD[("dt", i)], NH)
                        for j in range(n):
                            k = i * DT_TILES[0] + j
                            mm = three(bank, hi[:, j, :], lo[:, j, :], h_hi[:, k, :], h_lo[:, k, :], k == 0, k == KT - 1)
                        mm.then_inc(*(unit_filled if i else part_used).done())

                def turn_dt():
                    bank = bank_for(("dtT",))
                    pe.wait_ge(*cs_ready.at(b, 1))
                    for n, src in enumerate((1, 2)):
                        for c in range(NT):
                            mm = pe.matmul(bank[:, P * n + NH * c:P * n + NH * c + NH],
                                           dtmp[:, src, P * c:P * c + P], ident[0:NH, 0:NH], start=True, stop=True)
                    mm.then_inc(*unit_filled.done())

                def pre_bc(s):
                    g, c = divmod(s, NT)
                    tk = slice(P * c, P * c + P)
                    if c == 0:
                        pe.wait_ge(*gated.at(b, GATED[("x", g, 1)] + 1))
                        pe.wait_ge(*ylo_ready.at(b, 4 * g))
                    pe.wait_ge(*cbm_ready.at(b, s))
                    pe.transpose(bank_s[:, 0:P], conv[:, 0, tk], ident[:, :])
                    pe.matmul(bank_s[:, P:2 * P], conv[:, 0, tk], conv[:, 1, tk], start=True, stop=True
                              ).then_inc(*bc_filled.done())

                def pre_x(s):
                    g, c = divmod(s, NT)
                    if c == 0:
                        pe.wait_ge(*gated.at(b, GATED[("x", g, 5)] + 1))
                    pe.wait_ge(*xd_ready.at(b, s))
                    for t in range(4):
                        mm = pe.transpose(bank_x[:, P * t:P * t + P], conv[:, 2 + t, P * c:P * c + P], ident[:, :])
                    mm.then_inc(*xT_filled.done())

                def finish(g):
                    pe.wait_ge(*yn_ready.at(b, 4 * g + 4))
                    for t in range(4):
                        for c in range(NT):
                            mm = pe.transpose(sbank[t][:, P * c:P * c + P], ybuf[:, c, P * t:P * t + P], ident[:, :])
                        mm.then_inc(*fin_filled.done())

                for g in range(GROUPS):
                    for t in range(6):
                        project(("x", g, t))
                        if g == 0 and t == 0:
                            project_dt()
                        if g == 0 and t == 3:
                            turn_dt()
                        if t == 2 and g:
                            finish(g - 1)
                        if t == 4:
                            pre_bc(4 * g)
                        if type(b) is int and b == g == 0 and t == 5:
                            for n in (4, 5):
                                ada_sums(n, bank_x, gate_part[:, n - 4, :])
                    for i in range(z_before(g)):
                        z_part(g, i)
                    pre_x(4 * g)
                    for c in range(NT):
                        s = 4 * g + c
                        pe.wait_ge(*state_ready.at(b, s))
                        pe.matmul(bank_o[:, :], conv[:, 1, P * c:P * c + P], state[:, g, :], start=True, stop=True
                                  ).then_inc(*yoff_filled.done())
                        pe.wait_ge(*g_ready.at(b, s + 1))
                        pe.wait_ge(*xdt_ready.at(b, s + 1))
                        pe.wait_ge(*y_ready.at(b, s))
                        for h in range(HG):
                            mm = pe.matmul(bank_y[:, HD * h:HD * h + HD], gmat[:, h, :],
                                           xdt[:, s % 2, HD * h:HD * h + HD], start=True, stop=True)
                        mm.then_inc(*ydiag_filled.done())
                        if c < NT - 1:
                            pre_x(s + 1)
                            pre_bc(s + 1)
                        pe.wait_ge(*y1_ready.at(b, s + 1))
                        pe.wait_ge(*xw_ready.at(b, s + 1))
                        pe.matmul(bank_o[:, :], bts[:, s % 2, :], xw[:, :], start=True, stop=True
                                  ).then_inc(*new_filled.done())
                        for kind, n in fillers(g, c):
                            if kind == "z":
                                z_part(g, n)
                            else:
                                branch(g - 1, n)

                project(("k",))
                project(("v",))
                finish(3)

                def partners(r):
                    pe.wait_ge(*rflo_ready.at(b, r + 1))
                    pe.wait_ge(*rot_ready.at(b, r - 1))
                    if r == 0:
                        pe.wait_ge(*ylo_ready.at(b, 16))
                    bank = (bank_y, bank_s)[r % 2][:, :]
                    pe.matmul(bank, partner[:, :], rf_hi[:, :], start=True, stop=False)
                    pe.matmul(bank, partner[:, :], rf_lo[:, :], start=False, stop=True).then_inc(*perm_filled.done())

                def turn_v():
                    pe.wait_ge(*v_ready.at(b, 1))
                    for n, bk in enumerate((bank_x, bank_o)):
                        for c in range(4):
                            w0 = CH * (4 * n + c)
                            mm = pe.transpose(bk[:, P * c:P * c + P], vT[:, w0:w0 + P], ident[:, :])
                        mm.then_inc(*vT_filled.done())

                def scores(a):
                    kv, c = divmod(a, NCH)
                    pe.wait_ge(*rot_ready.at(b, 5 + 4 * kv))
                    pe.wait_ge(*p_ready.at(b, a - 1))
                    pe.wait_ge(*vw_ready.at(b, 4))
                    for sl in range(4):
                        half, pair = divmod(sl, 2)
                        mm = pe.matmul((bank_x, bank_s)[a % 2][:, P * sl:P * sl + P], qbuf[:, c, 2 * pair:2 * pair + 2, :],
                                       kz[:, 2 * kv + half, CH * c:CH * c + P], start=True, stop=True)
                    mm.then_inc(*score_filled.done())

                for kv in range(KV):
                    for j in range(4):
                        project(("q", kv, j))
                        if kv == 0 and j == 0:
                            partners(0)
                            turn_v()
                        if j:
                            partners(4 * kv + j)
                    for j in range(4):
                        project(("gate", kv, j))
                        if j == 0:
                            partners(4 * kv + 4)
                        if j in (1, 2):
                            scores(8 * kv + j - 1)
                    for c in range(NCH):
                        a = 8 * kv + c
                        if 0 < c < NCH - 1:
                            scores(a + 1)
                        begun = 2 if c == NCH - 1 else 0
                        if begun:
                            branch(3 + kv, c, 0, begun)
                        pe.wait_ge(*pn_ready.at(b, a + 1))
                        pe.wait_ge(*ptlo_ready.at(b, a))
                        for sl in range(4):
                            mm = pe.transpose(bank_y[:, P * sl:P * sl + P], pbuf[:, a % 2, sl, :], ident[:, :])
                        mm.then_inc(*pT_filled.done())
                        branch(3 + kv, c, begun)
                        pe.wait_ge(*ptlo_ready.at(b, a + 1))
                        pe.wait_ge(*yatt_ready.at(b, a))
                        for half in range(2):
                            v0 = HD * (2 * kv + 1 - half)
                            heads = slice(2 * half, 2 * half + 2)
                            mm = three(bank_o[:, 0:256], vw_hi[:, c, v0:v0 + P], vw_lo[:, c, v0:v0 + P],
                                       ptb_hi[:, a % 2, heads, :], ptb_lo[:, heads, :], half == 0, half == 1)
                        mm.then_inc(*pv_filled.done())

                for m in range(KT):
                    project(("ms", m))
                for m in range(KT):
                    branch(5, m)
                for m in range(KT):
                    project(("ma", m))

                def back(m):
                    pe.wait_ge(*og_ready.at(b, m + 1))
                    pe.wait_ge(*res_ready.at(b, m - 1))
                    for tt in range(NT):
                        mm = pe.transpose((bank_x, bank_y)[m % 2][:, P * tt:P * tt + P], og[:, m % 2, P * tt:P * tt + P],
                                          ident[:, :])
                    mm.then_inc(*outT_filled.done())

                if not last:
                    pe.wait_ge(*xn_ready.at(b, NT, 1))
                    for k in range(4):
                        turn_h(b, 1, k)
                for m in range(KT):
                    project(("out", m), mix_hi, mix_lo)
                    if m < 4 and not last:
                        turn_h(b, 1, 4 + m)
                    if m == 1 and not last:
                        pe.wait_ge(*hf_ready.at(b, 4, 1))
                    if m:
                        back(m - 1)
                back(KT - 1)

            body(0, False)
            with pe.Fori(1, NB - 1) as b:
                body(b, False)
            body(NB - 1, True)

        @block.scalar
        def _(act):
            for s in act_signals:
                act.sem_inc(s.sem, s.credit)
            act.wait_ge(prm_landed, 16)
            act.activation(silu_c[:, :], par("c"), ACT.Tanh, scale=0.5).then_inc(setup_act, 1)
            act.activation(aneg[:, :], par("a_log"), ACT.Exp).then_inc(setup_act, 1)
            def split(b, l):
                ahead, l = divmod(l, NL)
                act.wait_ge(*w_landed[l % RAW].at(b, l // RAW + 1, ahead))
                s, at = release(l - SPLIT)
                act.wait_ge(*s.at(b, at, ahead))
                n = width(l)
                act.activation(w_hi[:, l % SPLIT, 0:n], w_raw[:, l % RAW, 0:n], ACT.Copy).then_inc(*hi_ready.done())

            def h_std(b, ahead):
                act.wait_ge(*hvar_ready.at(b, 1, ahead))
                act.activation(std[:, 0, :], mv[:, 0, :, 1], ACT.Sqrt, bias=eps[:, :]).then_inc(*hstd_ready.done())

            def h_full(b, ahead, k):
                act.wait_ge(*ht_filled.at(b, k + 1, ahead))
                act.wait_ge(*hhi_ready.at(b, k - 1, ahead))
                act.wait_ge(*hlo_ready.at(b, k - 1, ahead))
                act.activation(hf[:, k % 2, :], sbank[H_BANK[k]][:, :], ACT.Identity, scale=ada[:, 8 + k:9 + k],
                               bias=ada[:, k:k + 1]).then_inc(*hf_ready.done())

            act.wait_ge(setup_dve, 6)
            h_std(0, 0)
            split(0, 0)
            split(0, 1)
            act.wait_ge(setup_dve, 8)
            for k in range(KT):
                h_full(0, 0, k)

            def body(b, last):
                chain = act_chain

                def next_split(key):
                    if LOAD[key] + SPLIT < NL or not last:
                        split(b, LOAD[key] + SPLIT)

                def filled(key):
                    act.wait_ge(*unit_filled.at(b, UNIT[key] + 1))
                    return ubank[UNIT[key] % UBANKS][:, :]

                def tanh(key, src, **kw):
                    n = GATED[key]
                    act.wait_ge(*gated.at(b, n - 1))
                    act.activation(th[:, n % 2, :], src, ACT.Tanh, **kw).then_inc(*th_ready.done())

                def softplus():
                    next_split(("dt", 0))
                    bank = filled(("dt",))[0:NH, :]
                    next_split(("dt", 1))
                    act.activation(dtmp[:, 0, :], bank, ACT.Abs, bias=par("dt_bias")[0:NH]).then_inc(*chain.done())
                    act.activation(dtmp[:, 1, :], bank, ACT.Relu, bias=par("dt_bias")[0:NH]).then_inc(*chain.done())
                    act.wait_ge(*chain.at(b, 1))
                    act.activation(dtmp[:, 0, :], dtmp[:, 0, :], ACT.Exp, scale=-1.0).then_inc(*chain.done())
                    act.wait_ge(*chain.at(b, 3))
                    act.activation(dtmp[:, 0, :], dtmp[:, 0, :], ACT.Ln, bias=one[0:NH, :]).then_inc(*dt_parts.done())

                def load_csb(s):
                    g, c = divmod(s, NT)
                    src = cs_dram[bass.ds(b, 1), HG * g:HG * g + HG, P * c:P * c + P].rearrange("a h t -> (a h) t")
                    act.dma_start(csb[:, s % 2, :, :], src.partition_broadcast(P)).then_inc(*csb_landed[s % 2].done())

                def decays(s):
                    act.wait_ge(*ends_ready.at(b, s + 1))
                    act.activation(ends[:, s % 4, :], ends[:, s % 4, :], ACT.Exp).then_inc(*decays_ready.done())
                    act.wait_ge(*dif_ready.at(b, s + 1))
                    act.activation(dif[:, :, :], dif[:, :, :], ACT.Exp).then_inc(*e_ready.done())
                    if s + 2 < 16:
                        load_csb(s + 2)

                def square(s):
                    g, c = divmod(s, NT)
                    act.wait_ge(*gate_done.at(b, s + 1))
                    act.wait_ge(*sq_ready.at(b, s))
                    act.activation(junk[:, :], ybuf[:, c, :], ACT.Square, accum_out=ss[:, c:c + 1]
                                   ).then_inc(*sq_ready.done())

                def finish(g):
                    for s in range(4 * g if z_step(g) == NT - 1 else 4 * g + NT - 1, 4 * g + NT):
                        square(s)
                    act.wait_ge(*sq_ready.at(b, 4 * g + 4))
                    act.activation(gstd[:, :], ss[:, :], ACT.Sqrt, scale=0.25 / 512, bias=eps[:, :]
                                   ).then_inc(*gstd_ready.done())

                def finish_hi(g):
                    if g:
                        act.wait_ge(*unit_filled.at(b, UNIT[("br", g - 1, 7)] + 1))
                    for t in range(4):
                        act.wait_ge(*fin_filled.at(b, 4 * g + t + 1))
                        act.activation(ys_hi[:, t, :], sbank[t][:, :], ACT.Copy, scale=par("norm_w", 4 * g + t)
                                       ).then_inc(*yhi_ready.done())

                def conv_in(g, t):
                    n = 6 * g + t
                    ct = conv_tile(g, t)
                    bank = filled(("x", g, t))
                    if t < 5:
                        next_split(("x", g, t))
                    act.wait_ge(*conv_done.at(b, n - 1))
                    act.wait_ge(*hist_out.at(b, n - 1))
                    act.activation(conv[:, t, :], bank, ACT.Identity, scale=par("conv_w", 4 * ct + 3),
                                   bias=par("conv_b", ct)).then_inc(*tap_ready.done())
                    act.activation(u[:, n % 2, 3:3 + T], bank, ACT.Copy).then_inc(*u_ready.done())
                    if t == 5:
                        next_split(("x", g, t))

                def conv_tanh(g, t):
                    act.wait_ge(*conv_done.at(b, 6 * g + t + 1))
                    tanh(("x", g, t), conv[:, t, :])

                def filler(g, c):
                    for kind, n in fillers(g, c):
                        if kind == "z":
                            if n < 3:
                                next_split(("z", g, n))
                                continue
                            for tt in range(NT):
                                key = ("z", g, tt)
                                tanh(key, filled(key), scale=0.5)
                                if tt == 1:
                                    next_split(("z", g, n))
                        elif n % 2:
                            next_split(("br", g - 1, n // 2))

                for g in range(GROUPS):
                    for t in range(6):
                        if t == 0 and g:
                            act.wait_ge(*yoff_filled.at(b, 4 * g))
                        conv_in(g, t)
                        if g == 0 and t == 0:
                            softplus()
                        if t == 0 and g:
                            finish(g - 1)
                        if g == 0 and t == 5:
                            act.wait_ge(*tok_ready.at(b, 1))
                            act.activation(ecs[:, :, :], tok[:, 1, :, :], ACT.Exp).then_inc(*ecs_ready.done())
                            decays(0)
                        if t:
                            conv_tanh(g, t - 1)
                        if t == 2 and g:
                            finish_hi(g - 1)
                        if g == 0 and t == 2:
                            act.wait_ge(*cs_ready.at(b, 1))
                            act.dma_start(cs_dram[bass.ds(b, 1), :, :].rearrange("a h t -> (a h) t"), dtmp[:, 2, :]
                                          ).then_inc(*cs_stored.done())
                        if g == 0 and t == 3:
                            act.wait_ge(*cs_stored.at(b, 1))
                            load_csb(0)
                            load_csb(1)
                    conv_tanh(g, 5)
                    for i in range(z_before(g)):
                        next_split(("z", g, i))
                    decays(4 * g + 1)
                    for c in range(NT):
                        s = 4 * g + c
                        if c < NT - 1 and s + 2 < 16:
                            decays(s + 2)
                        filler(g, c)
                        if z_step(g) <= c < NT - 1:
                            square(s)
                finish(3)

                def rope_in(r, key, name, n):
                    bank = filled(key)
                    next_split(key)
                    act.wait_ge(*ra_ready.at(b, r - 1))
                    act.wait_ge(*perm_filled.at(b, r - 1))
                    act.activation(rf[:, r % 2, :], bank, ACT.Identity, bias=par(name, n)).then_inc(*rf_ready.done())
                    act.wait_ge(*rf_ready.at(b, r + 1))
                    act.wait_ge(*perm_filled.at(b, r))
                    act.activation(rf_hi[:, :], rf[:, r % 2, :], ACT.Copy).then_inc(*rfhi_ready.done())

                for n in range(2):
                    src = trig[n][:, bass.ds(b * T, T)]
                    act.dma_start(trg[:, n, :], src).then_inc(*trig_landed.done())
                rope_in(0, ("k",), "b_k", 0)
                act.activation(vT[:, 0:CH], vT[:, T:T + CH], ACT.Copy).then_inc(*chain.done())
                bank = filled(("v",))
                next_split(("v",))
                act.wait_ge(*chain.at(b, 4))
                act.activation(vT[:, CH:], bank, ACT.Identity, scale=0.5, bias=par("b_v")).then_inc(*v_ready.done())
                finish_hi(3)

                def attn_hi(kv, j):
                    act.wait_ge(*yatt_ready.at(b, 8 * kv + 8))
                    act.wait_ge(*unit_filled.at(b, UNIT[("br", 3 + kv, 7)] + 1))
                    act.activation(ys_hi[:, j, :], zbuf[:, j, :], ACT.Copy).then_inc(*yhi_ready.done())

                def softmax(a):
                    act.wait_ge(*nb_ready.at(b, a + 1))
                    act.wait_ge(*pT_filled.at(b, a - 1))
                    act.wait_ge(*rec_ready.at(b, a - 1))
                    for sl in range(4):
                        act.activation(pbuf[:, a % 2, sl, :], (bank_x, bank_s)[a % 2][:, P * sl:P * sl + P], ACT.Exp, scale=SCALE,
                                       bias=nbias[:, a % 2, sl:sl + 1], accum_out=rsum[:, a % 2, sl:sl + 1])
                    act.activation(esink[:, a % 2, :], nsink[:, a % 2, :], ACT.Exp).then_inc(*p_ready.done())

                for kv in range(KV):
                    for j in range(4):
                        rope_in(1 + 4 * kv + j, ("q", kv, j), "b_q", 4 * kv + j)
                    if kv:
                        for j in range(4):
                            attn_hi(kv - 1, j)
                    for j in range(4):
                        if j > 1:
                            softmax(8 * kv + j - 2)
                        bank = filled(("gate", kv, j))
                        if j < 3:
                            next_split(("gate", kv, j))
                        tanh(("gate", kv, j), bank, scale=0.5)
                    next_split(("gate", kv, 3))
                    for c in range(NCH):
                        a = 8 * kv + c
                        act.wait_ge(*pT_filled.at(b, a + 1))
                        act.wait_ge(*pv_filled.at(b, a - 1))
                        act.activation(ptb_hi[:, a % 2, :, :], bank_y[:, :].rearrange("p (s k) -> p s k", k=P), ACT.Copy
                                       ).then_inc(*pt_ready.done())
                        if 0 < c < NCH - 1:
                            softmax(a + 1)
                        if c % 2:
                            next_split(("br", 3 + kv, c // 2))

                for j in range(4):
                    attn_hi(1, j)
                for m in range(KT):
                    bank = filled(("ms", m))
                    next_split(("ms", m))
                    tanh(("ms", m), bank, scale=0.5, bias=par("b_merge", 8 + m))
                for i in range(4):
                    next_split(("br", 5, i))
                if not last:
                    h_std(b, 1)

                def mix_in(m):
                    act.wait_ge(*mixf_ready.at(b, m + 1))
                    act.activation(mix_hi[:, m, :], acc_s[:, m, :], ACT.Copy).then_inc(*mixhi_ready.done())

                for m in range(KT):
                    bank = filled(("ma", m))
                    if m < KT - 1:
                        next_split(("ma", m))
                    tanh(("ma", m), bank, scale=0.5, bias=par("b_merge", m))
                    if m:
                        mix_in(m - 1)
                next_split(("ma", KT - 1))
                mix_in(KT - 1)
                if not last:
                    for k in range(4):
                        h_full(b, 1, k)
                for m in range(KT):
                    bank = filled(("out", m))
                    if m < KT - 1:
                        next_split(("out", m))
                    act.wait_ge(*outT_filled.at(b, m - 1))
                    act.activation(og[:, m % 2, :], bank, ACT.Copy, scale=ada[:, 16 + m:17 + m]).then_inc(*og_ready.done())
                    if m < 4 and not last:
                        h_full(b, 1, 4 + m)
                next_split(("out", KT - 1))
                act.wait_ge(*lvar_ready.at(b, 1))
                act.activation(std[:, 1, :], mv[:, 1, :, 1], ACT.Sqrt, bias=eps[:, :]).then_inc(*lstd_ready.done())

            body(0, False)
            with act.Fori(1, NB - 1) as b:
                body(b, False)
            body(NB - 1, True)

        @block.vector
        def _(dve):
            for s in dve_signals:
                dve.sem_inc(s.sem, s.credit)
            dve.memset(eps[:, :], EPS)
            dve.memset(one[:, :], 1.0)
            dve.memset(kz[:, :, :], 0.0)
            dve.wait_ge(setup_act, 2)
            dve.scalar_tensor_tensor(silu_c[:, :], silu_c[:, :], 1.0, par("c"), ALU.add, ALU.mult).then_inc(setup_dve2, 1)
            dve.wait_ge(setup_dve2, 1)
            dve.tensor_scalar(silu_c[:, :], silu_c[:, :], 0.5, None, ALU.mult).then_inc(setup_dve, 1)
            for name in ("conv_w", "conv_b", "b_merge", "norm_w", "b_v"):
                dve.tensor_scalar(par(name), par(name), 0.5, None, ALU.mult).then_inc(setup_dve, 1)
            dve.tensor_scalar(aneg[:, :], aneg[:, :], -1.0, None, ALU.mult).then_inc(setup_dve2, 1)
            dve.tensor_scalar(negsink[:, :, :].rearrange("p a b -> p (a b)"), par("sink"), -1.0, None, ALU.mult
                              ).then_inc(setup_dve2, 1)
            def x_norm(b, ahead):
                dve.wait_ge(*x_landed.at(b, 1, ahead))
                for tt in range(NT):
                    for n in range(2):
                        dve.bn_stats(stats[:, 0, tt, n, :], xn[:, tt, 512 * n:512 * n + 512]).then_inc(*x_chain.done())
                dve.wait_ge(*x_chain.at(b, 8, ahead))
                dve.sem_inc(waited, 1)
                for tt in range(NT):
                    ins = dve.bn_aggr(mv[:, 0, tt, :], stats[:, 0, tt, :, :])
                ins.then_inc(*hvar_ready.done())
                dve.wait_ge(*hstd_ready.at(b, 1, ahead))
                dve.reciprocal(rstd[:, 0, :], std[:, 0, :]).then_inc(*x_chain.done())
                dve.wait_ge(*x_chain.at(b, 9, ahead))
                for tt in range(NT):
                    dve.tensor_scalar(xn[:, tt, :], xn[:, tt, :], mv[:, 0, tt, 0:1], rstd[:, 0, tt:tt + 1],
                                      ALU.subtract, ALU.mult).then_inc(*xn_ready.done())

            def h_high(b, ahead, k):
                dve.wait_ge(*hf_ready.at(b, k + 1, ahead))
                dve.tensor_copy(h_hi[:, k, :], hf[:, k % 2, :]).then_inc(*hhi_ready.done())

            def ada_chunk(n, partial, first=0, last=KT):
                if first == 0:
                    dve.wait_ge(ada_landed[n], 16)
                    if n == 3:
                        dve.wait_ge(ada_filled, 1)
                for k in range(first, last):
                    if k == 0:
                        ins = dve.tensor_scalar(partial, ada_w[n][:, 0, :], silu_c[:, 0:1], None, ALU.mult)
                    else:
                        dve.wait_ge(ada_chain, (KT - 1) * (n - 1) + k)
                        ins = dve.scalar_tensor_tensor(partial, ada_w[n][:, k, :], silu_c[:, k:k + 1], partial,
                                                       ALU.mult, ALU.add)
                    ins.then_inc(ada_chain if k < KT - 1 else ada_sum, 1)

            dve.wait_ge(setup_dve, 6)
            x_norm(0, 0)
            for n in (1, 2, 3):
                ada_chunk(n, th[:, n % 2, :])
            dve.wait_ge(ada_filled, 3)
            dve.tensor_tensor(ada[:, 0:16], ubank[3][:, 0:16], par("b_ada")[:, 0:16], ALU.add).then_inc(setup_dve2, 1)
            dve.wait_ge(setup_dve2, 4)
            dve.tensor_scalar(ada[:, 8:16], ada[:, 8:16], 1.0, None, ALU.add).then_inc(setup_dve, 2)
            for k in range(KT):
                h_high(0, 0, k)
            dve.wait_ge(const_landed, 48)
            dve.tensor_copy(partner[:, :], junk[:, 0:P])
            dve.wait_ge(setup_pool, 3)

            def body(b, last):
                chain = dve_chain
                link = [0]
                first = type(b) is int and b == 0

                def done_link():
                    link[0] += 1
                    return chain.done()

                def after_link():
                    dve.wait_ge(*chain.at(b, link[0]))

                def cumulate():
                    dve.wait_ge(*dt_parts.at(b, 1))
                    dve.tensor_tensor(dtmp[:, 1, :], dtmp[:, 0, :], dtmp[:, 1, :], ALU.add).then_inc(*dt_ready.done())
                    dve.wait_ge(*dt_ready.at(b, 1))
                    dve.tensor_scalar(dtmp[:, 0, :], dtmp[:, 1, :], aneg[0:NH, :], None, ALU.mult).then_inc(*done_link())
                    after_link()
                    for c in range(NT):
                        ins = dve.tensor_tensor_scan(dtmp[:, 2, P * c:P * c + P], one[0:NH, :].to_broadcast([NH, P]),
                                                     dtmp[:, 0, P * c:P * c + P], 0.0, ALU.mult, ALU.add)
                    ins.then_inc(*cs_ready.done())

                def conv_taps(g, t):
                    n = 6 * g + t
                    ct = conv_tile(g, t)
                    dve.wait_ge(*conv_done.at(b, n - 1))
                    dve.wait_ge(*hist_out.at(b, n - 1))
                    dve.tensor_copy(u[:, n % 2, 0:3], hist[:, ct, :]).then_inc(*hist_in.done())
                    dve.wait_ge(*u_ready.at(b, n + 1))
                    dve.wait_ge(*hist_in.at(b, n + 1))
                    dve.tensor_copy(hist[:, ct, :], u[:, n % 2, T:T + 3]).then_inc(*hist_out.done())
                    for w in range(3):
                        ins = dve.scalar_tensor_tensor(conv[:, t, :], u[:, n % 2, w:w + T], par("conv_w", 4 * ct + w),
                                                       conv[:, t, :], ALU.mult, ALU.add)
                        if w < 2:
                            ins.then_inc(*done_link())
                            after_link()
                        else:
                            ins.then_inc(*conv_done.done())

                def gate(key, out_ap, src):
                    n = GATED[key]
                    dve.wait_ge(*th_ready.at(b, n + 1))
                    dve.scalar_tensor_tensor(out_ap, th[:, n % 2, :], 1.0, src, ALU.add, ALU.mult).then_inc(*gated.done())

                def pre_a(s):
                    g, c = divmod(s, NT)
                    heads = slice(HG * g, HG * g + HG)
                    dve.wait_ge(*csb_landed[s % 2].at(b, s // 2 + 1))
                    dve.wait_ge(*xw_ready.at(b, s - 3))
                    dve.wait_ge(*sdec_ready.at(b, s - 3))
                    dve.tensor_tensor(ends[:, s % 4, 0:HG], csb[:, s % 2, :, P - 1], tok[:, 1, c, heads], ALU.subtract)
                    dve.tensor_copy(ends[:, s % 4, HG:], csb[:, s % 2, :, P - 1]).then_inc(*ends_ready.done())
                    dve.wait_ge(*g_ready.at(b, s))
                    for h in range(HG):
                        ins = dve.tensor_scalar(dif[:, h, :], csb[:, s % 2, h, :], tok[:, 1, c, HG * g + h:HG * g + h + 1],
                                                 0.0, ALU.subtract, ALU.min)
                    ins.then_inc(*dif_ready.done())

                ada_parts = [[(4, 0, 4)], [(4, 4, 8)], [(5, 0, 3)], [(5, 3, 6)], [(5, 6, 8)], []]

                def ada_gate():
                    dve.wait_ge(ada_filled, 5)
                    dve.tensor_tensor(ada[:, 16:24], bank_x[:, 16:24], par("b_ada")[:, 16:24], ALU.add).then_inc(setup_dve2, 1)
                    dve.wait_ge(setup_dve2, 5)
                    dve.tensor_scalar(ada[:, 16:24], ada[:, 16:24], 0.5, None, ALU.mult).then_inc(setup_dve, 1)

                def heads3(ap):
                    return ap.rearrange("p (h d) -> p h d", d=HD)

                def over_heads(ap):
                    return ap.unsqueeze(2).to_broadcast([P, HG, HD])

                def take_x(s):
                    g, c = divmod(s, NT)
                    heads = slice(HG * g, HG * g + HG)
                    dve.wait_ge(*xT_filled.at(b, s + 1))
                    dve.wait_ge(*ydiag_filled.at(b, s - 1))
                    dve.wait_ge(*xw_ready.at(b, s - 1))
                    dve.tensor_tensor(heads3(xdt[:, s % 2, :]), heads3(bank_x[:, :]), over_heads(tok[:, 0, c, heads]),
                                      ALU.mult).then_inc(*xdt_ready.done())
                    dve.wait_ge(*y2_ready.at(b, s - 1))
                    dve.tensor_tensor(heads3(xd[:, s % 2, :]), heads3(bank_x[:, :]), over_heads(par("d_skip", HG * g, HG)),
                                      ALU.mult).then_inc(*xd_ready.done())

                def take_bc(s):
                    dve.wait_ge(*bc_filled.at(b, s + 1))
                    dve.wait_ge(*new_filled.at(b, s - 1))
                    dve.tensor_copy(bts[:, s % 2, :], bank_s[:, 0:P]).then_inc(*bts_ready.done())
                    dve.wait_ge(*g_ready.at(b, s))
                    dve.tensor_tensor(cbm[:, :], bank_s[:, P:2 * P], causal[:, :], ALU.mult).then_inc(*cbm_ready.done())

                def add_branch(br, m):
                    key = ("br", br, m)
                    dve.wait_ge(*unit_filled.at(b, UNIT[key] + 1))
                    bank = ubank[UNIT[key] % UBANKS][:, :]
                    acc = (acc_s if br < GROUPS else acc_a)[:, m, :]
                    if br in (0, GROUPS):
                        dve.tensor_copy(acc, bank).then_inc(*acc_ready.done())
                    else:
                        dve.wait_ge(*acc_ready.at(b, BRANCH[("br", br - 1, m)] + 1))
                        dve.tensor_tensor(acc, acc, bank, ALU.add).then_inc(*acc_ready.done())

                def read_fillers(g, c, later):
                    if ("z", 3) in fillers(g, c):
                        dve.wait_ge(*gate_done.at(b, 4 * g))
                        for tt in (2, 3) if later else (0, 1):
                            key = ("z", g, tt)
                            gate(key, zbuf[:, tt, :], ubank[UNIT[key] % UBANKS][:, :])
                    tiles = [m for kind, m in fillers(g, c) if kind == "br"]
                    if c < NT - 1:
                        tiles = tiles[-1:] if later else tiles[:-1]
                    for m in tiles:
                        add_branch(g - 1, m)

                def g_matrix(s):
                    dve.wait_ge(*e_ready.at(b, s + 1))
                    dve.wait_ge(*cbm_ready.at(b, s + 1))
                    dve.wait_ge(*ydiag_filled.at(b, s))
                    dve.tensor_tensor(gmat[:, :, :], dif[:, :, :], cbm[:, :].unsqueeze(1).to_broadcast([P, HG, P]),
                                      ALU.mult).then_inc(*g_ready.done())

                def finish(g):
                    dve.wait_ge(*gstd_ready.at(b, g + 1))
                    dve.reciprocal(grs[:, :], gstd[:, :]).then_inc(*done_link())
                    after_link()
                    for c in range(NT):
                        dve.tensor_scalar(ybuf[:, c, :], ybuf[:, c, :], grs[:, c:c + 1], None, ALU.mult
                                          ).then_inc(*yn_ready.done())

                def finish_lo(g):
                    for t in range(4):
                        dve.wait_ge(*yhi_ready.at(b, 4 * g + t + 1))
                        dve.scalar_tensor_tensor(ys_lo[:, t, :], sbank[t][:, :], par("norm_w", 4 * g + t),
                                                 ys_hi[:, t, :].bitcast(F32), ALU.mult, ALU.subtract
                                                 ).then_inc(*ylo_ready.done())

                for g in range(GROUPS):
                    for t in range(6):
                        if t == 5:
                            take_bc(4 * g)
                            if g:
                                g_matrix(4 * g)
                        if g == 0 and t == 4:
                            dve.wait_ge(*unit_filled.at(b, UNIT[("dtT",)] + 1))
                            dve.tensor_copy(tok[:, :, :, :].rearrange("p a b c -> p (a b c)"),
                                            ubank[UNIT[("dtT",)] % UBANKS][:, 0:256]).then_inc(*tok_ready.done())
                        conv_taps(g, t)
                        if first and g == 0:
                            for n, k, k_end in ada_parts[t]:
                                ada_chunk(n, gate_part[:, n - 4, :], k, k_end)
                        if g == 0 and t == 0:
                            cumulate()
                        if t == 0 and g:
                            finish(g - 1)
                        if t:
                            dve.wait_ge(*conv_done.at(b, 6 * g + t))
                            gate(("x", g, t - 1), conv[:, t - 1, :], conv[:, t - 1, :])
                        if t == 2 and g:
                            finish_lo(g - 1)
                        if g == 0 and t == 4:
                            dve.wait_ge(*tok_ready.at(b, 1))
                            pre_a(0)
                    if first and g == 0:
                        ada_gate()
                    dve.wait_ge(*conv_done.at(b, 6 * g + 6))
                    gate(("x", g, 5), conv[:, 5, :], conv[:, 5, :])
                    if g == 0:
                        g_matrix(0)
                    take_x(4 * g)
                    pre_a(4 * g + 1)
                    if g == 0:
                        dve.wait_ge(*ecs_ready.at(b, 1))
                    for c in range(NT):
                        s = 4 * g + c
                        heads = slice(HG * g, HG * g + HG)
                        dve.wait_ge(*yoff_filled.at(b, s + 1))
                        if c == 0:
                            dve.wait_ge(*fin_filled.at(b, 4 * g))
                        dve.tensor_tensor(heads3(ybuf[:, c, :]), heads3(bank_o[:, :]), over_heads(ecs[:, c, heads]),
                                          ALU.mult).then_inc(*y1_ready.done())
                        dve.wait_ge(*ydiag_filled.at(b, s + 1))
                        dve.wait_ge(*y1_ready.at(b, s + 1))
                        dve.tensor_tensor(ybuf[:, c, :], ybuf[:, c, :], bank_y[:, :], ALU.add).then_inc(*y_ready.done())
                        if c:
                            read_fillers(g, c - 1, True)
                        if c < NT - 1:
                            take_x(s + 1)
                            take_bc(s + 1)
                        dve.wait_ge(*new_filled.at(b, s + 1))
                        dve.wait_ge(*sdec_ready.at(b, s + 1))
                        dve.tensor_tensor(state[:, g, :], state[:, g, :], bank_o[:, :], ALU.add
                                          ).then_inc(*state_ready.done())
                        if c < NT - 1:
                            g_matrix(s + 1)
                            if s + 2 < 16:
                                pre_a(s + 2)
                        read_fillers(g, c, False)
                    if first and g == 0:
                        dve.wait_ge(late_landed, 48)
                finish(3)

                def rotate_low(r):
                    dve.wait_ge(*rfhi_ready.at(b, r + 1))
                    dve.wait_ge(*perm_filled.at(b, r))
                    dve.tensor_tensor(rf_lo[:, :], rf[:, r % 2, :], rf_hi[:, :].bitcast(F32), ALU.subtract
                                      ).then_inc(*rflo_ready.done())

                def rotate_b(r):
                    dve.wait_ge(*perm_filled.at(b, r + 1))
                    dve.wait_ge(*rot_ready.at(b, r))
                    dve.tensor_tensor(rb[:, :], (bank_y, bank_s)[r % 2][:, :], trg[:, 1, :], ALU.mult).then_inc(*done_link())
                    dve.wait_ge(*ra_ready.at(b, r + 1))
                    after_link()

                dve.tensor_copy(kz[:, :, 0:CH], kz[:, :, T:T + CH]).then_inc(*done_link())
                after_link()
                finish_lo(3)
                dve.wait_ge(*trig_landed.at(b, 2))
                rotate_low(0)
                rotate_b(0)
                for kv in range(KV):
                    for half in range(2):
                        src = slice(HD * kv, HD * kv + HD)
                        dst = slice(HD * half, HD * half + HD)
                        ins = dve.tensor_tensor(kz[dst, 2 * kv + half, CH:], ra[src, 0, :], rb[src, :], ALU.add)
                ins.then_inc(*rot_ready.done())
                rotate_low(1)
                dve.wait_ge(*vz_ready.at(b, 2))
                for n, bk in enumerate((bank_x, bank_o)):
                    dve.wait_ge(*vT_filled.at(b, n + 1))
                    hi, lo = (w[:, 4 * n:4 * n + 4, HD:5 * HD].rearrange("p c (v d) -> p c v d", d=2 * HD)[:, :, :, 0:HD]
                              for w in (vw_hi, vw_lo))
                    src = bk[:, :].rearrange("p (c v d) -> p c v d", v=2, d=HD)
                    dve.tensor_copy(hi, src).then_inc(*vw_ready.done())
                    dve.wait_ge(*vw_ready.at(b, 2 * n + 1))
                    dve.tensor_tensor(lo, src, hi.bitcast(F32), ALU.subtract).then_inc(*vw_ready.done())

                def maxima(a):
                    kv, c = divmod(a, NCH)
                    dve.wait_ge(*score_filled.at(b, a + 1))
                    dve.wait_ge(*p_ready.at(b, a - 1))
                    view = (bank_x, bank_s)[a % 2][:, :].rearrange("p (s k) -> p s k", k=P)
                    if c == 0:
                        m = maskb[:, bass.ds(b, 1), :].to_broadcast([P, 4, CH])
                        dve.tensor_tensor(view[:, :, 0:CH], view[:, :, 0:CH], m, ALU.add).then_inc(*done_link())
                        after_link()
                    dve.tensor_reduce(top[:, a % 2, :], view, AX.X, ALU.max).then_inc(*done_link())
                    after_link()
                    dve.scalar_tensor_tensor(nbias[:, a % 2, :], top[:, a % 2, :], -SCALE, negsink[:, kv, :],
                                             ALU.mult, ALU.min).then_inc(*done_link())
                    after_link()
                    dve.tensor_tensor(nsink[:, a % 2, :], nbias[:, a % 2, :], negsink[:, kv, :], ALU.subtract
                                      ).then_inc(*nb_ready.done())

                def denominators(a):
                    dve.wait_ge(*p_ready.at(b, a + 1))
                    dve.wait_ge(*pn_ready.at(b, a - 1))
                    dve.tensor_tensor(rden[:, a % 2, :], rsum[:, a % 2, :], esink[:, a % 2, :], ALU.add).then_inc(*done_link())
                    after_link()
                    dve.reciprocal(rden[:, a % 2, :], rden[:, a % 2, :]).then_inc(*rec_ready.done())

                def attn_lo(kv):
                    for j in range(4):
                        n = 4 * (4 + kv) + j
                        dve.wait_ge(*yhi_ready.at(b, n + 1))
                        dve.tensor_tensor(ys_lo[:, j, :], zbuf[:, j, :], ys_hi[:, j, :].bitcast(F32), ALU.subtract
                                          ).then_inc(*ylo_ready.done())

                def normalise(a):
                    dve.wait_ge(*rec_ready.at(b, a + 1))
                    dve.tensor_tensor(pbuf[:, a % 2, :, :], pbuf[:, a % 2, :, :],
                                      rden[:, a % 2, :].unsqueeze(2).to_broadcast([P, 4, P]), ALU.mult
                                      ).then_inc(*pn_ready.done())

                for kv in range(KV):
                    for j in range(4):
                        r = 1 + 4 * kv + j
                        if j == 0 and kv:
                            dve.wait_ge(*score_filled.at(b, 8 * kv))
                            rotate_low(r)
                        rotate_b(r)
                        dve.tensor_tensor(qbuf[:, :, j, :], ra[:, r % 2, :].rearrange("p (c q) -> p c q", q=CH),
                                          rb[:, :].rearrange("p (c q) -> p c q", q=CH), ALU.add).then_inc(*rot_ready.done())
                        if j < 3:
                            rotate_low(r + 1)
                    if kv:
                        attn_lo(kv - 1)
                        dve.wait_ge(*ylo_ready.at(b, 4 * (4 + kv)))
                    for j in range(4):
                        key = ("gate", kv, j)
                        if j > 1:
                            maxima(8 * kv + j - 2)
                            denominators(8 * kv + j - 2)
                            normalise(8 * kv + j - 2)
                        gate(key, zbuf[:, j, :], ubank[UNIT[key] % UBANKS][:, :])
                    for c in range(NCH):
                        a = 8 * kv + c
                        if 0 < c < NCH - 1:
                            maxima(a + 1)
                        dve.wait_ge(*pt_ready.at(b, a + 1))
                        dve.wait_ge(*pv_filled.at(b, a))
                        dve.tensor_tensor(ptb_lo[:, :, :].rearrange("p s k -> p (s k)"), bank_y[:, :],
                                          ptb_hi[:, a % 2, :, :].rearrange("p s k -> p (s k)").bitcast(F32),
                                          ALU.subtract).then_inc(*ptlo_ready.done())
                        if 0 < c < NCH - 1:
                            denominators(a + 1)
                            normalise(a + 1)
                        add_branch(3 + kv, c)
                        dve.wait_ge(*pv_filled.at(b, a + 1))
                        part = zbuf[:, :, CH * c:CH * c + CH]
                        dve.tensor_tensor(part, bank_o[:, 0:256].rearrange("p (j q) -> p j q", q=CH), part, ALU.mult
                                          ).then_inc(*yatt_ready.done())
                attn_lo(1)
                for m in range(KT):
                    dve.wait_ge(*acc_ready.at(b, BRANCH[("br", 3, m)] + 1))
                    gate(("ms", m), acc_s[:, m, :], acc_s[:, m, :])
                for m in range(KT):
                    add_branch(5, m)
                if not last:
                    x_norm(b, 1)

                def mix_lo_part(m):
                    dve.wait_ge(*mixhi_ready.at(b, m + 1))
                    dve.tensor_tensor(mix_lo[:, m, :], acc_s[:, m, :], mix_hi[:, m, :].bitcast(F32), ALU.subtract
                                      ).then_inc(*mixlo_ready.done())

                for m in range(KT):
                    dve.wait_ge(*acc_ready.at(b, BRANCH[("br", 5, m)] + 1))
                    gate(("ma", m), acc_a[:, m, :], acc_a[:, m, :])
                    if m:
                        mix_lo_part(m - 1)
                mix_lo_part(KT - 1)
                if not last:
                    for k in range(4):
                        h_high(b, 1, k)
                dve.wait_ge(*res_landed.at(b, 1))
                for m in range(KT):
                    if m < 4 and not last:
                        h_high(b, 1, 4 + m)
                    dve.wait_ge(*outT_filled.at(b, m + 1))
                    part = res[:, :, P * m:P * m + P]
                    dve.scalar_tensor_tensor(part, part, ALPHA, (bank_x, bank_y)[m % 2][:, :].rearrange(
                        "p (t n) -> p t n", n=P), ALU.mult, ALU.add).then_inc(*res_ready.done())
                    if m % 4 == 3:
                        dve.wait_ge(*res_ready.at(b, m + 1))
                        for tt in range(NT):
                            dve.bn_stats(stats[:, 1, tt, m // 4, :], res[:, tt, 512 * (m // 4):512 * (m // 4) + 512]
                                         ).then_inc(*done_link())
                after_link()
                dve.sem_inc(waited, 1)
                for tt in range(NT):
                    ins = dve.bn_aggr(mv[:, 1, tt, :], stats[:, 1, tt, :, :])
                ins.then_inc(*lvar_ready.done())
                dve.wait_ge(*lvar_ready.at(b, 1))
                for tt in range(NT):
                    dve.scalar_tensor_tensor(res[:, tt, :], res[:, tt, :], mv[:, 1, tt, 0:1], lng[:, :],
                                             ALU.subtract, ALU.mult).then_inc(*done_link())
                dve.wait_ge(*lstd_ready.at(b, 1))
                dve.reciprocal(rstd[:, 1, :], std[:, 1, :]).then_inc(*done_link())
                after_link()
                for tt in range(NT):
                    dve.scalar_tensor_tensor(res[:, tt, :], res[:, tt, :], rstd[:, 1, tt:tt + 1], lnb[:, :],
                                             ALU.mult, ALU.add).then_inc(*out_ready.done())
                assert link[0] == chain.per_block, link[0]

            body(0, False)
            with dve.Fori(1, NB - 1) as b:
                body(b, False)
            body(NB - 1, True)

        @block.gpsimd
        def _(pool):
            for s in pool_signals:
                pool.sem_inc(s.sem, s.credit)
            pool.sem_inc(out_stored.sem, 16)
            pool.memset(hist[:, :, :], 0.0).then_inc(setup_pool, 1)
            pool.memset(state[:, :, :], 0.0).then_inc(setup_pool, 1)
            pool.memset(vT[:, :], 0.0).then_inc(setup_pool, 1)
            pool.wait_ge(setup_pool, 3)

            def split(b, l):
                ahead, l = divmod(l, NL)
                n = width(l)
                pool.wait_ge(*hi_ready.at(b, l + 1, ahead))
                pool.tensor_tensor(w_lo[:, l % SPLIT, 0:n], w_raw[:, l % RAW, 0:n],
                                   w_hi[:, l % SPLIT, 0:n].bitcast(F32), ALU.subtract).then_inc(*lo_ready.done())

            def h_low(b, ahead, k):
                pool.wait_ge(*hhi_ready.at(b, k + 1, ahead))
                pool.tensor_tensor(h_lo[:, k, :], hf[:, k % 2, :], h_hi[:, k, :].bitcast(F32), ALU.subtract
                                   ).then_inc(*hlo_ready.done())

            split(0, 0)
            split(0, 1)
            for k in range(KT):
                h_low(0, 0, k)

            def body(b, last):
                def next_split(key):
                    if LOAD[key] + SPLIT < NL or not last:
                        split(b, LOAD[key] + SPLIT)

                def heads3(ap):
                    return ap.rearrange("p (h d) -> p h d", d=HD)

                def over_heads(ap):
                    return ap.unsqueeze(2).to_broadcast([P, HG, HD])

                def weigh(s):
                    pool.wait_ge(*xdt_ready.at(b, s + 1))
                    pool.wait_ge(*decays_ready.at(b, s + 1))
                    pool.wait_ge(*new_filled.at(b, s))
                    pool.tensor_tensor(heads3(xw[:, :]), heads3(xdt[:, s % 2, :]), over_heads(ends[:, s % 4, 0:HG]),
                                       ALU.mult).then_inc(*xw_ready.done())

                def gate(s):
                    g, c = divmod(s, NT)
                    pool.wait_ge(*y2_ready.at(b, s + 1))
                    pool.wait_ge(*gated.at(b, GATED[("z", g, c)] + 1))
                    pool.tensor_tensor(ybuf[:, c, :], ybuf[:, c, :], zbuf[:, c, :], ALU.mult).then_inc(*gate_done.done())

                for g in range(GROUPS):
                    for t in range(6):
                        next_split(("x", g, t))
                        if g == 0 and t == 0:
                            next_split(("dt", 0))
                            next_split(("dt", 1))
                    for i in range(z_before(g)):
                        if i == z_before(g) - 1:
                            weigh(4 * g)
                        next_split(("z", g, i))
                    for c in range(NT):
                        s = 4 * g + c
                        pool.wait_ge(*yoff_filled.at(b, s + 1))
                        pool.wait_ge(*state_ready.at(b, s))
                        pool.tensor_tensor(heads3(state[:, g, :]), heads3(state[:, g, :]), over_heads(ends[:, s % 4, HG:]),
                                           ALU.mult).then_inc(*sdec_ready.done())
                        pool.wait_ge(*y_ready.at(b, s + 1))
                        pool.wait_ge(*xd_ready.at(b, s + 1))
                        pool.tensor_tensor(ybuf[:, c, :], ybuf[:, c, :], xd[:, s % 2, :], ALU.add).then_inc(*y2_ready.done())
                        if c < NT - 1:
                            weigh(s + 1)
                        for kind, n in fillers(g, c):
                            if kind == "z":
                                next_split(("z", g, n))
                            elif n % 2:
                                next_split(("br", g - 1, n // 2))
                        if c == z_step(g):
                            for n in range(c):
                                gate(4 * g + n)
                        if c >= z_step(g):
                            gate(s)

                def rotate_a(r):
                    pool.wait_ge(*rf_ready.at(b, r + 1))
                    pool.wait_ge(*rot_ready.at(b, r - 1))
                    if r == 0:
                        pool.wait_ge(*trig_landed.at(b, 2))
                    pool.tensor_tensor(ra[:, r % 2, :], rf[:, r % 2, :], trg[:, 0, :], ALU.mult).then_inc(*ra_ready.done())

                next_split(("k",))
                rotate_a(0)
                for w in (vw_hi, vw_lo):
                    pool.memset(w[:, :, :].bitcast(F32), 0.0).then_inc(*vz_ready.done())
                next_split(("v",))

                for kv in range(KV):
                    for j in range(4):
                        next_split(("q", kv, j))
                        rotate_a(1 + 4 * kv + j)
                    for j in range(4):
                        next_split(("gate", kv, j))
                    for i in range(4):
                        next_split(("br", 3 + kv, i))
                for m in range(KT):
                    next_split(("ms", m))
                for i in range(4):
                    next_split(("br", 5, i))
                for m in range(KT):
                    if m < KT - 1:
                        next_split(("ma", m))
                    pool.wait_ge(*gated.at(b, GATED[("ma", m)] + 1))
                    pool.tensor_tensor(acc_s[:, m, :], acc_s[:, m, :], acc_a[:, m, :], ALU.add).then_inc(*mixf_ready.done())
                next_split(("ma", KT - 1))
                if not last:
                    for k in range(4):
                        h_low(b, 1, k)
                for m in range(KT):
                    next_split(("out", m))
                    if m < 4 and not last:
                        h_low(b, 1, 4 + m)

            body(0, False)
            with pool.Fori(1, NB - 1) as b:
                body(b, False)
            body(NB - 1, True)

        for s in pe_signals + act_signals + dve_signals + pool_signals:
            assert s.seen == 3 * s.per_block, (s.sem, s.seen, s.per_block)


def kernel(x, c, w_ada, b_ada, w_in, b_qkv, b_merge, attn_sinks, conv_w, conv_b, dt_bias, a_log,
           d_skip, ssd_norm_w, w_branch_attn, w_branch_ssd, w_out, ln_g, ln_b):
    import numpy as np
    import concourse.bacc as bacc
    from concourse.bass_utils import run_bass_kernel_spmd

    f = np.float32

    def tiles(v):
        return np.ascontiguousarray(v).reshape(-1, P).T

    prm = np.zeros((P, NPARAM), f)

    def put(name, v):
        at, n = PARAMS[name]
        prm[:v.shape[0], at:at + n] = v

    c, b_ada, b_qkv, b_merge, attn_sinks, conv_w, conv_b, dt_bias, a_log, d_skip, ssd_norm_w = (
        np.asarray(v) for v in (c, b_ada, b_qkv, b_merge, attn_sinks, conv_w, conv_b, dt_bias, a_log, d_skip, ssd_norm_w))
    put("c", tiles(c[0]))
    put("b_ada", tiles(b_ada[0]))
    put("b_q", tiles(b_qkv[0, :1024]))
    put("b_k", tiles(b_qkv[0, 1024:1152]))
    put("b_v", tiles(b_qkv[0, 1152:]))
    put("b_merge", tiles(b_merge[0]))
    put("conv_w", conv_w[0].reshape(4, CONVT, P).transpose(2, 1, 0).reshape(P, CONVT * 4))
    put("conv_b", tiles(conv_b[0]))
    put("norm_w", tiles(ssd_norm_w[0]))
    put("dt_bias", dt_bias[0][:, None])
    put("a_log", a_log[0][:, None])
    sink = attn_sinks[0].reshape(KV, 2, 2, 2)
    put("sink", np.repeat(sink.transpose(2, 0, 3, 1).reshape(2, 8), 64, axis=0))
    put("d_skip", np.broadcast_to(d_skip[0], (P, 32)))

    consts = np.zeros((3, P, P), f)
    consts[0] = np.eye(P)
    consts[1] = np.triu(np.ones((P, P)))
    for p in range(P):
        if p % HD < 16:
            consts[2, p + 8 if p % HD < 8 else p - 8, p] = 1.0
    half = 8
    inv = np.power(f(500000.0), -np.arange(half, dtype=f) / f(half)).astype(f)
    ang = (np.arange(SEQ, dtype=f)[:, None] * inv[None, :]).astype(f)
    trig = np.zeros((2, P, SEQ), f)
    trig[0] = 1.0
    for p in range(P):
        d = p % HD
        if d < 16:
            trig[0, p] = np.cos(ang[:, d % 8])
            trig[1, p] = np.sin(ang[:, d % 8]) * (-1.0 if d < 8 else 1.0)
    kmask = np.zeros((P, NB, CH), f)
    kmask[:, 0, :] = -1e30

    arrays = {"x": x, "params": prm, "w_ada": w_ada, "w_in": w_in, "w_br_attn": w_branch_attn,
              "w_br_ssd": w_branch_ssd, "w_out": w_out, "ln_g": np.asarray(ln_g)[0], "ln_b": np.asarray(ln_b)[0],
              "consts": consts, "trig": trig, "kmask": kmask}
    arrays = {n: np.ascontiguousarray(a) for n, a in arrays.items()}
    nc = bacc.Bacc("TRN2", target_bir_lowering=False, num_devices=1)
    args = [nc.dram_tensor(n, a.shape, mybir.dt.from_np(a.dtype), kind="ExternalInput").ap() for n, a in arrays.items()]
    args.append(nc.dram_tensor("out", (1, SEQ, D), F32, kind="ExternalOutput").ap())
    program(nc, *args)
    r = run_bass_kernel_spmd(nc, [arrays], core_ids=[0])
    return r.results[0]["out"]
```
